# Optimizing a Trainium2 kernel written in Bass

```python
import math, functools
import jax, jax.numpy as jnp
from jax import lax
import numpy as np

D_MODEL = 1024
BATCH = 1
SEQ = 2048
DEPTH = 1
DEC_BATCH = 8
DEC_SEQ = 4
PAST_LEN = 8192
PAGE_SIZE = 128

PLE_DIM = 256
EPS = 1e-6
A_HEADS = 4
A_DQK = 128
A_DV = 256
A_QK = A_HEADS * A_DQK
A_WIDTH = A_HEADS * A_DV
CONV_W = 4
CHUNK = 64
FORGET_BIAS = 3.0
B_HEADS = 8
B_KV = 2
B_HD = 128
B_WIDTH = B_HEADS * B_HD
IDX_HEADS = 8
IDX_DIM = 64
TOPK_MAX = 256
Q_BLOCK = 128

IN_SPLITS = (
    ('a_q', A_QK), ('a_k', A_QK), ('a_v', A_WIDTH), ('a_i', A_HEADS), ('a_f', A_HEADS),
    ('a_o', A_WIDTH), ('a_z', A_WIDTH),
    ('b_q', B_WIDTH), ('b_k', B_KV * B_HD), ('b_v', B_KV * B_HD), ('b_iq', IDX_HEADS * IDX_DIM),
    ('b_ik', IDX_DIM), ('b_iw', IDX_HEADS), ('b_z', B_WIDTH),
    ('g_a', D_MODEL), ('g_b', D_MODEL),
)
IN_COLS = sum(n for _, n in IN_SPLITS)

kernel_name = 'hybrid_mlstm_dsa_parallel_decode_step'

def rmsnorm(x, g):
    xf = x.astype(jnp.float32)
    y = xf * lax.rsqrt(jnp.mean(xf * xf, axis=-1, keepdims=True) + EPS)
    return (y * g.astype(jnp.float32)).astype(x.dtype)

def split_cols(h):
    names = [nm for nm, _ in IN_SPLITS]
    cuts = np.cumsum([n for _, n in IN_SPLITS])[:-1].tolist()
    return dict(zip(names, jnp.split(h, cuts, axis=-1)))

def causal_conv(u, buf, w, b):
    T = u.shape[1]
    up = jnp.concatenate([buf.astype(u.dtype), u], axis=1)
    y = b + w[0] * up[:, 0:T]
    for j in range(1, CONV_W):
        y = y + w[j] * up[:, j:j + T]
    return jax.nn.silu(y), up[:, up.shape[1] - (CONV_W - 1):]

def mlstm_chunkwise(q, k, v, i_pre, f_pre, C0, n0, m0, chunk):
    f32 = jnp.float32
    B, T, H, _ = q.shape
    nc = T // chunk

    def to_chunks(a):
        a = a.astype(f32).reshape((B, nc, chunk) + a.shape[2:])
        return jnp.moveaxis(jnp.moveaxis(a, 3, 2), 1, 0)

    xs = (to_chunks(q), to_chunks(k), to_chunks(v), to_chunks(i_pre),
          to_chunks(jax.nn.log_sigmoid(f_pre.astype(f32))))
    causal = jnp.tril(jnp.ones((chunk, chunk), dtype=bool))

    def step(carry, blk):
        C, n, m = carry
        qb, kb, vb, ib, lfb = blk
        b = jnp.cumsum(lfb, axis=-1)
        inter = b + m[..., None]
        logd = jnp.where(causal, b[..., :, None] - b[..., None, :] + ib[..., None, :], -jnp.inf)
        m_t = jnp.maximum(inter, jnp.max(logd, axis=-1))
        dmat = jnp.exp(logd - m_t[..., None])
        w_inter = jnp.exp(inter - m_t)
        s = jnp.einsum('bhtd,bhsd->bhts', qb, kb) * dmat
        num = jnp.einsum('bhts,bhsv->bhtv', s, vb) + w_inter[..., None] * jnp.einsum('bhvd,bhtd->bhtv', C, qb)
        den = jnp.sum(s, axis=-1) + w_inter * jnp.einsum('bhd,bhtd->bht', n, qb)
        h = num / jnp.maximum(jnp.abs(den), jnp.exp(-m_t))[..., None]
        m_new = m_t[..., -1]
        w_prev = jnp.exp(b[..., -1] + m - m_new)
        w_s = jnp.exp(b[..., -1:] - b + ib - m_new[..., None])
        C_new = w_prev[..., None, None] * C + jnp.einsum('bhs,bhsv,bhsd->bhvd', w_s, vb, kb)
        n_new = w_prev[..., None] * n + jnp.einsum('bhs,bhsd->bhd', w_s, kb)
        return (C_new, n_new, m_new), h

    (C, n, m), h = lax.scan(step, (C0.astype(f32), n0.astype(f32), m0.astype(f32)), xs)
    h = jnp.moveaxis(jnp.moveaxis(h, 0, 1), 2, 3).reshape(B, T, H, v.shape[-1])
    return h, C, n, m

def mlstm_branch(parts, conv_buf, C0, n0, m0, chunk, conv_w, conv_b, if_bias, norm_a):
    B, T, _ = parts['a_q'].shape
    qk, conv_new = causal_conv(jnp.concatenate([parts['a_q'], parts['a_k']], axis=-1), conv_buf, conv_w, conv_b)
    q = qk[..., :A_QK].reshape(B, T, A_HEADS, A_DQK) * (A_DQK ** -0.5)
    k = qk[..., A_QK:].reshape(B, T, A_HEADS, A_DQK)
    v = parts['a_v'].reshape(B, T, A_HEADS, A_DV)
    i_pre = parts['a_i'] + if_bias[:A_HEADS]
    f_pre = parts['a_f'] + if_bias[A_HEADS:]
    h, C, n, m = mlstm_chunkwise(q, k, v, i_pre, f_pre, C0, n0, m0, chunk)
    h = h * lax.rsqrt(jnp.mean(h * h, axis=-1, keepdims=True) + EPS)
    h = (h.reshape(B, T, A_WIDTH) * norm_a.astype(jnp.float32)).astype(parts['a_v'].dtype)
    y = jax.nn.sigmoid(parts['a_o']) * h * jax.nn.silu(parts['a_z'])
    return y, (C, n, m, conv_new)

def indexer_scores(iq, iw, ik, visible):
    r = jax.nn.relu(jnp.einsum('bthd,bsd->bths', iq.astype(jnp.float32), ik.astype(jnp.float32)) * (IDX_DIM ** -0.5))
    sc = jnp.einsum('bths,bth->bts', r, iw.astype(jnp.float32) * (IDX_HEADS ** -0.5))
    return jnp.where(visible[None], sc, -jnp.inf)

def sparse_attend(q, k_sel, v_sel, valid):
    s = jnp.einsum('btngd,btknd->btngk', q.astype(jnp.float32), k_sel.astype(jnp.float32)) * (B_HD ** -0.5)
    s = jnp.where(valid[:, :, None, None, :], s, -jnp.inf)
    p = jax.nn.softmax(s, axis=-1)
    return jnp.einsum('btngk,btknd->btngd', p, v_sel.astype(jnp.float32))

def dsa_prompt(q, k, v, iq, iw, ik):
    B, S = q.shape[:2]
    topk = min(TOPK_MAX, S // 4)
    nb = S // Q_BLOCK
    key_pos = jnp.arange(S)
    bidx = jnp.arange(B)[:, None, None]

    def blk(a):
        return jnp.moveaxis(a.reshape((B, nb, Q_BLOCK) + a.shape[2:]), 1, 0)

    def one(xs):
        qb, iqb, iwb, t0 = xs
        qpos = t0 + jnp.arange(Q_BLOCK)
        visible = key_pos[None, :] <= qpos[:, None]
        _, sel = lax.top_k(indexer_scores(iqb, iwb, ik, visible), topk)
        valid = sel <= qpos[None, :, None]
        return sparse_attend(qb, k[bidx, sel], v[bidx, sel], valid)

    o = lax.map(one, (blk(q), blk(iq), blk(iw), jnp.arange(nb) * Q_BLOCK))
    return jnp.moveaxis(o, 0, 1).reshape(B, S, B_WIDTH)

def dsa_sample(q, k, v, iq, iw, ik, cache_k, cache_v, cache_ik, page_table):
    B, T = q.shape[:2]
    L = PAST_LEN + T
    topk = min(TOPK_MAX, L // 4)
    ik_past = cache_ik[page_table].reshape(B, PAST_LEN, IDX_DIM).astype(ik.dtype)
    ik_all = jnp.concatenate([ik_past, ik], axis=1)
    qpos = PAST_LEN + jnp.arange(T)
    visible = jnp.arange(L)[None, :] <= qpos[:, None]
    _, sel = lax.top_k(indexer_scores(iq, iw, ik_all, visible), topk)
    valid = sel <= qpos[None, :, None]
    in_past = (sel < PAST_LEN)[..., None, None]
    bidx = jnp.arange(B)[:, None, None]
    ps = jnp.minimum(sel, PAST_LEN - 1)
    phys = page_table[bidx, ps // PAGE_SIZE]
    off = ps % PAGE_SIZE
    ns = jnp.clip(sel - PAST_LEN, 0, T - 1)
    ks = jnp.where(in_past, cache_k[phys, off].astype(k.dtype), k[bidx, ns])
    vs = jnp.where(in_past, cache_v[phys, off].astype(v.dtype), v[bidx, ns])
    return sparse_attend(q, ks, vs, valid).reshape(B, T, B_WIDTH)

def trunk_layer(x, pe, conv_buf, C0, n0, m0, chunk, attend_fn, w_in, conv_w, conv_b, if_bias, norm_a,
                w_a_proj, w_b_proj, w_out, norm_pre, norm_post, w_ple, w_ple_gate):
    B, T, _ = x.shape
    xn = rmsnorm(x, norm_pre)
    parts = split_cols(xn @ w_in)
    ya, (C, n, m, conv_new) = mlstm_branch(parts, conv_buf, C0, n0, m0, chunk, conv_w, conv_b, if_bias, norm_a)
    q = parts['b_q'].reshape(B, T, B_KV, B_HEADS // B_KV, B_HD)
    k = parts['b_k'].reshape(B, T, B_KV, B_HD)
    v = parts['b_v'].reshape(B, T, B_KV, B_HD)
    iq = parts['b_iq'].reshape(B, T, IDX_HEADS, IDX_DIM)
    ik = parts['b_ik']
    yb = attend_fn(q, k, v, iq, parts['b_iw'], ik).astype(x.dtype) * jax.nn.silu(parts['b_z'])
    merged = jax.nn.sigmoid(parts['g_a']) * (ya @ w_a_proj) + jax.nn.sigmoid(parts['g_b']) * (yb @ w_b_proj)
    x = x + rmsnorm(merged @ w_out, norm_post)
    x = x + (pe @ w_ple) * jax.nn.sigmoid(x @ w_ple_gate)
    return x, (k, v, ik, C, n, m, conv_new)

def setup_inputs(seed: int = 0) -> dict:
    key = jax.random.key(seed)
    ks = jax.random.split(key, 24)
    n_pages = PAST_LEN // PAGE_SIZE
    n_pool = (DEC_BATCH * n_pages * 5) // 4
    nrm = jax.random.normal
    f32 = jnp.float32
    page_table = jax.random.permutation(ks[0], n_pool)[:DEC_BATCH * n_pages].reshape(DEC_BATCH, n_pages).astype(jnp.int32)
    if_bias = jnp.concatenate([0.1 * nrm(ks[1], (DEPTH, A_HEADS), f32),
                               FORGET_BIAS + 0.1 * nrm(ks[2], (DEPTH, A_HEADS), f32)], axis=-1)
    return {
        'x_prompt': nrm(ks[3], (BATCH, SEQ, D_MODEL), f32),
        'x_sample': nrm(ks[4], (DEC_BATCH, DEC_SEQ, D_MODEL), f32),
        'cache_k': nrm(ks[5], (DEPTH, n_pool, PAGE_SIZE, B_KV, B_HD), f32),
        'cache_v': nrm(ks[6], (DEPTH, n_pool, PAGE_SIZE, B_KV, B_HD), f32),
        'cache_idx_k': nrm(ks[7], (DEPTH, n_pool, PAGE_SIZE, IDX_DIM), f32),
        'page_table': page_table,
        'state_C': 0.5 * nrm(ks[8], (DEPTH, DEC_BATCH, A_HEADS, A_DV, A_DQK), f32),
        'state_n': nrm(ks[9], (DEPTH, DEC_BATCH, A_HEADS, A_DQK), f32),
        'state_m': nrm(ks[10], (DEPTH, DEC_BATCH, A_HEADS), f32),
        'state_conv': nrm(ks[11], (DEPTH, DEC_BATCH, CONV_W - 1, 2 * A_QK), f32),
        'p_prompt': nrm(ks[12], (DEPTH, BATCH, SEQ, PLE_DIM), f32),
        'p_sample': nrm(ks[13], (DEPTH, DEC_BATCH, DEC_SEQ, PLE_DIM), f32),
        'w_in': nrm(ks[14], (DEPTH, D_MODEL, IN_COLS), f32) * D_MODEL ** -0.5,
        'conv_w': nrm(ks[15], (DEPTH, CONV_W, 2 * A_QK), f32) * CONV_W ** -0.5,
        'conv_b': 0.01 * nrm(ks[16], (DEPTH, 2 * A_QK), f32),
        'if_bias': if_bias,
        'norm_a': 1.0 + 0.01 * nrm(ks[17], (DEPTH, A_WIDTH), f32),
        'w_a_proj': nrm(ks[18], (DEPTH, A_WIDTH, D_MODEL), f32) * A_WIDTH ** -0.5,
        'w_b_proj': nrm(ks[19], (DEPTH, B_WIDTH, D_MODEL), f32) * B_WIDTH ** -0.5,
        'w_out': nrm(ks[20], (DEPTH, D_MODEL, D_MODEL), f32) * D_MODEL ** -0.5,
        'norm_pre': 1.0 + 0.01 * nrm(ks[21], (DEPTH, D_MODEL), f32),
        'norm_post': 1.0 + 0.01 * nrm(ks[22], (DEPTH, D_MODEL), f32),
        'w_ple': nrm(ks[23], (DEPTH, PLE_DIM, D_MODEL), f32) * PLE_DIM ** -0.5,
        'w_ple_gate': nrm(jax.random.fold_in(key, 99), (DEPTH, D_MODEL, D_MODEL), f32) * D_MODEL ** -0.5,
    }

def reference(x_prompt, x_sample, cache_k, cache_v, cache_idx_k, page_table, state_C, state_n, state_m, state_conv,
              p_prompt, p_sample, w_in, conv_w, conv_b, if_bias, norm_a, w_a_proj, w_b_proj, w_out,
              norm_pre, norm_post, w_ple, w_ple_gate):
    f32 = jnp.float32
    B, T = x_prompt.shape[:2]
    Ts = x_sample.shape[1]
    yp, ys = x_prompt, x_sample
    sp_list, ss_list = [], []
    for i in range(DEPTH):
        w = (w_in[i], conv_w[i], conv_b[i], if_bias[i], norm_a[i], w_a_proj[i], w_b_proj[i], w_out[i],
             norm_pre[i], norm_post[i], w_ple[i], w_ple_gate[i])
        zero_conv = jnp.zeros((B, CONV_W - 1, 2 * A_QK), x_prompt.dtype)
        zC = jnp.zeros((B, A_HEADS, A_DV, A_DQK), f32)
        zn = jnp.zeros((B, A_HEADS, A_DQK), f32)
        zm = jnp.zeros((B, A_HEADS), f32)
        yp, sp = trunk_layer(yp, p_prompt[i], zero_conv, zC, zn, zm, math.gcd(T, CHUNK), dsa_prompt, *w)
        attend_s = functools.partial(dsa_sample, cache_k=cache_k[i], cache_v=cache_v[i],
                                     cache_ik=cache_idx_k[i], page_table=page_table)
        ys, ss = trunk_layer(ys, p_sample[i], state_conv[i], state_C[i], state_n[i], state_m[i],
                             math.gcd(Ts, CHUNK), attend_s, *w)
        sp_list.append(sp)
        ss_list.append(ss)

    def stk(lst, j):
        return jnp.stack([s[j] for s in lst])

    return (yp, ys,
            stk(sp_list, 0), stk(sp_list, 1), stk(sp_list, 2), stk(sp_list, 3), stk(sp_list, 4), stk(sp_list, 5), stk(sp_list, 6),
            stk(ss_list, 0), stk(ss_list, 1), stk(ss_list, 2), stk(ss_list, 3), stk(ss_list, 4), stk(ss_list, 5), stk(ss_list, 6))


_drawn_inputs = setup_inputs


def setup_inputs(seed=0):
    import zlib

    import numpy as np

    out = dict(_drawn_inputs(seed))
    spreads = {}
    factors = {'conv_b': 12.979,
     'norm_a': 200.0,
     'norm_pre': 2.72,
     'norm_post': 200.0,
     'cache_k': 3.892,
     'cache_v': 3.922,
     'cache_idx_k': 3.805,
     'p_prompt': 3.676,
     'p_sample': 3.66,
     'w_ple': 3.605,
     'w_ple_gate': 5.246}
    for name, (base, spread) in spreads.items():
        noise = np.random.default_rng([zlib.crc32(name.encode()), seed]).standard_normal(out[name].shape)
        drawn = base * np.exp(spread * noise) if base else spread * noise
        out[name] = __import__('jax').numpy.asarray(drawn.astype(out[name].dtype))
    for name, factor in factors.items():
        out[name] = (out[name] * factor).astype(out[name].dtype)
    return out
```

```python
from contextlib import ExitStack

import concourse.bass as bass
from concourse import mybir

F32 = mybir.dt.float32
BF16 = mybir.dt.bfloat16
I32 = mybir.dt.int32
U32 = mybir.dt.uint32
ALU = mybir.AluOpType
ACT = mybir.ActivationFunctionType
AX_X = mybir.AxisListType.X

P = 128
D = 1024
KT = D // P
SEQ = 2048
NB = SEQ // P
DB, DT = 8, 4
SR = DB * DT
ROWS = SEQ + SR
NT = NB + 1
G = 5
GW = ROWS // G
EPS = 1e-6
AH, DQK, DV = 4, 128, 256
BH, KV, HD = 8, 2, 128
IH, ID = 8, 64
TOPK = 256
PAST = 8192
PAGE = 128
PAGES = PAST // PAGE
POOL = 640
PLE = 256
NEG = -1e30
TAKEN = -3.0e38
HIDDEN = -3.2e38

C_AV, C_AI, C_AO, C_AZ = 1024, 2048, 2056, 3080
C_BQ, C_BK, C_IQ, C_IK = 4104, 5128, 5640, 6152
C_BZ, C_GA = 6224, 7248
COLS = 9296
CH = 512
ROW_CHUNKS = [C_AV, C_AV + CH, C_AO, C_AO + CH, C_AZ, C_AZ + CH, C_BK,
              C_BZ, C_BZ + CH, C_GA, C_GA + CH, C_GA + 2 * CH, C_GA + 3 * CH]
R_AV, R_AO, R_AZ, R_BKV, R_BZ, R_GA = 0, 1024, 2048, 3072, 3584, 4608
RCOLS = CH * len(ROW_CHUNKS)
T_CONV, T_BQ, T_BK, T_IQ, T_ALL = 0, 8, 16, 18, 22


def tile_rows(n):
    return SR if isinstance(n, int) and n == NB else P


def phase_semaphores(nc, ctx, phase):
    taken = []

    def free():
        nc.clear_and_free_semaphores(taken)
        nc.all_engine_barrier()
    ctx.callback(free)

    def sem(name):
        taken.append(nc.alloc_semaphore(f"{phase}_{name}"))
        return taken[-1]
    return sem


def norm_phase(nc, c, d, s):
    with ExitStack() as ctx:
        sb = lambda name, shape, dt=F32: ctx.enter_context(nc.sbuf_tensor(name, shape, dt))
        sem = phase_semaphores(nc, ctx, "norm")
        xt = [sb(f"xt{p}", [P, D]) for p in range(2)]
        xs = [sb(f"xs{p}", [P, D]) for p in range(2)]
        junk = sb("junk", [P, D])
        ss = sb("ss", [P, 2])
        rt = sb("rt", [P, 2])
        rstd = sb("rstd", [P, 2])
        gcol = sb("gcol", [P, KT])
        sconv = sb("sconv", [24, D])
        xps = [ctx.enter_context(nc.psum_tensor(f"xps{p}", [P, 2, 4, P], F32)) for p in range(2)]
        cps = ctx.enter_context(nc.psum_tensor("cps", [P, KT, 24], F32))
        x_loaded = [sem(f"x_loaded{p}") for p in range(2)]
        small_loaded = sem("small_loaded")
        squared, rooted, rstd_ready, scaled = sem("squared"), sem("rooted"), sem("rstd_ready"), sem("scaled")
        transposed, evac_a, evac_v = sem("transposed"), sem("evac_a"), sem("evac_v")
        eps_ready, ident0, ident_ready, conv_t = sem("eps_ready"), sem("ident0"), sem("ident_ready"), sem("conv_t")
        halo = sem("halo")

        def pairs(eng, body):
            for p in range(2):
                body(0, p, P, False)
            with eng.Fori(1, NB // 2) as j:
                for p in range(2):
                    body(j, p, P, True)
            body(NB // 2, 0, SR, True)

        block = ctx.enter_context(nc.Block())

        @block.sync
        def _(sp):
            sp.dma_start(gcol[:, :], d["norm_pre"].rearrange("a (t p) -> (a p) t", p=P)).then_inc(small_loaded, 16)
            sp.dma_start(sconv[:, :], d["state_conv"].rearrange("a b j c -> (a b j) c")).then_inc(small_loaded, 16)

            def load(j, p, rows, warm):
                if warm:
                    sp.wait_ge(scaled, 2 * j + p - 1)
                src = d["x_sample"].rearrange("b t c -> (b t) c") if rows == SR else \
                    d["x_prompt"].rearrange("a (n q) c -> (a n) q c", q=P)[2 * j + p]
                sp.dma_start(xt[p][0:rows, :], src).then_inc(x_loaded[p], 16)
            pairs(sp, load)

        @block.gpsimd
        def _(pool):
            nc.gpsimd.memset(c["ident"][:, :], 0.0).then_inc(ident0, 1)
            pool.wait_ge(ident0, 1)
            nc.gpsimd.affine_select(out=c["ident"][:, :], in_=c["ident"][:, :], compare_op=ALU.not_equal,
                                    fill=1.0, base=0, pattern=[[-1, P]], channel_multiplier=1).then_inc(ident_ready, 1)

        @block.scalar
        def _(act):
            act.wait_ge(eps_ready, 1)

            def tile(j, p, rows, warm):
                n = 2 * j + p
                act.wait_ge(x_loaded[p], 16 * (j + 1))
                if warm:
                    act.wait_ge(rstd_ready, n - 1)
                nc.scalar.activation(junk[0:rows, :], xt[p][0:rows, :], ACT.Square,
                                     accum_out=ss[0:rows, p:p + 1]).then_inc(squared, 1)
                act.wait_ge(squared, n + 1)
                nc.scalar.activation(rt[0:rows, p:p + 1], ss[0:rows, p:p + 1], ACT.Sqrt, scale=1.0 / D,
                                     bias=c["eps"][0:rows, 0:1]).then_inc(rooted, 1)
                act.wait_ge(transposed, n + 1)
                for k in range(KT // 2):
                    nc.scalar.activation(c["xnT"][:, k, bass.ds(n * P, rows)], xps[p][:, k // 4, k % 4, 0:rows],
                                         ACT.Copy, scale=gcol[:, k:k + 1]).then_inc(evac_a, 1)
            act.wait_ge(small_loaded, 32)
            pairs(act, tile)

        @block.vector
        def _(dve):
            nc.vector.memset(c["eps"][:, :], EPS).then_inc(eps_ready, 1)
            dve.wait_ge(small_loaded, 32)
            dve.wait_ge(conv_t, 1)
            nc.vector.tensor_copy(c["us"][:, :, :, 0:3],
                                  cps[:, :, :].rearrange("p t (b j) -> p t b j", j=3)).then_inc(halo, 1)

            def tile(j, p, rows, warm):
                n = 2 * j + p
                dve.wait_ge(rooted, n + 1)
                if warm:
                    dve.wait_ge(scaled, n - 1)
                nc.vector.reciprocal(rstd[0:rows, p:p + 1], rt[0:rows, p:p + 1]).then_inc(rstd_ready, 1)
                dve.wait_ge(rstd_ready, n + 1)
                if warm:
                    dve.wait_ge(transposed, n - 1)
                nc.vector.tensor_scalar(xs[p][0:rows, :], xt[p][0:rows, :], rstd[0:rows, p:p + 1], None,
                                        ALU.mult).then_inc(scaled, 1)
                dve.wait_ge(transposed, n + 1)
                for k in range(KT // 2, KT):
                    nc.vector.tensor_scalar(c["xnT"][:, k, bass.ds(n * P, rows)], xps[p][:, k // 4, k % 4, 0:rows],
                                            gcol[:, k:k + 1], None, ALU.mult).then_inc(evac_v, 1)
            pairs(dve, tile)

        @block.tensor
        def _(pe):
            pe.wait_ge(ident_ready, 1)
            pe.wait_ge(small_loaded, 32)
            for t in range(KT):
                ins = nc.tensor.transpose(cps[:, t, :], sconv[:, t * P:(t + 1) * P], c["ident"][0:24, 0:24])
            ins.then_inc(conv_t, 1)

            def tile(j, p, rows, warm):
                n = 2 * j + p
                pe.wait_ge(scaled, n + 1)
                if warm:
                    pe.wait_ge(evac_a, 4 * (n - 1))
                    pe.wait_ge(evac_v, 4 * (n - 1))
                for k in range(KT):
                    ins = nc.tensor.transpose(xps[p][:, k // 4, k % 4, 0:rows], xs[p][0:rows, k * P:(k + 1) * P],
                                              c["ident"][0:rows, 0:rows])
                ins.then_inc(transposed, 1)
            pairs(pe, tile)


def transposed_projection_phase(nc, c, d, s):
    with ExitStack() as ctx:
        sb = lambda name, shape, dt=F32: ctx.enter_context(nc.sbuf_tensor(name, shape, dt))
        sem = phase_semaphores(nc, ctx, "transposed_projection")
        wt = [sb(f"wt{p}", [P, KT, P]) for p in range(2)]
        u = [sb(f"u{p}", [P, 3 + ROWS]) for p in range(2)]
        acc = [sb(f"acc{p}", [P, ROWS]) for p in range(2)]
        sig = sb("sig", [P, ROWS])
        cw = sb("cw", [P, 5, KT])
        qs = sb("qs", [P, KT])
        last3 = sb("last3", [P, KT, 3])
        raw35 = sb("raw35", [P, KT, 35])
        rows35 = sb("rows35", [35, D])
        gbias = sb("gbias", [8, 1])
        gates = sb("gates", [8, ROWS])
        ki = sb("ki", [P, ROWS])
        pg = ctx.enter_context(nc.psum_tensor("pg", [P, G, 512], F32))
        pt = ctx.enter_context(nc.psum_tensor("pt", [P, 3, 512], F32))
        w_loaded = [sem(f"w_loaded{p}") for p in range(2)]
        consts, qs_set, halo0 = sem("consts"), sem("qs_set"), sem("halo0")
        group_mm, group_out = sem("group_mm"), sem("group_out")
        conv_step, sig_ready, conv_out = sem("conv_step"), sem("sig_ready"), sem("conv_out")
        stored = [sem(f"stored{p}") for p in range(2)]
        raw_ready, raw_t, raw_rows, raw_stored = sem("raw_ready"), sem("raw_t"), sem("raw_rows"), sem("raw_stored")
        w0, ik_moved, gates_stored = sem("w0"), sem("ik_moved"), sem("gates_stored")
        sm_t, sm_out, sm_stored = sem("sm_t"), sem("sm_out"), sem("sm_stored")
        STEPS = 10
        NP_CONV, NP_PLAIN = 4, 7

        w_in = d["w_in"].rearrange("a (k p) n -> (a p) k n", p=P)
        block = ctx.enter_context(nc.Block())

        def tiles(eng, body):
            for p in range(2):
                body(0, p, True, False)
            with eng.Fori(1, NP_CONV) as j:
                for p in range(2):
                    body(j, p, True, True)
            with eng.Fori(NP_CONV, NP_CONV + NP_PLAIN) as j:
                for p in range(2):
                    body(j, p, False, True)

        NTILE = 2 * (NP_CONV + NP_PLAIN)

        @block.sync
        def _(sp):
            for j in range(4):
                sp.dma_start(cw[:, j, :], d["conv_w"][0, j].rearrange("(t p) -> p t", p=P)).then_inc(consts, 16)
            sp.dma_start(cw[:, 4, :], d["conv_b"][0].rearrange("(t p) -> p t", p=P)).then_inc(consts, 16)
            sp.dma_start(gbias[:, :], d["if_bias"].rearrange("a n -> n a")).then_inc(consts, 16)

            def load(j, p, col, warm):
                if warm:
                    sp.wait_ge(group_mm, G * (2 * j + p - 1))
                sp.dma_start(wt[p][:, :, :], w_in[:, :, bass.ds(col, P)]).then_inc(w_loaded[p], 16)
            for p in range(2):
                load(0, p, p * P, False)
            for lo, hi, first in ((1, 4, 2 * P), (4, 9, C_BQ), (9, 11, C_IQ)):
                with sp.Fori(lo, hi) as j:
                    for p in range(2):
                        load(j, p, (2 * (j - lo) + p) * P + first, True)
            sp.wait_ge(w0, 1)
            sp.dma_start(wt[0][:, :, 0:72], w_in[:, :, C_IK:C_IK + 72]).then_inc(w_loaded[0], 16)
            sp.dma_start(wt[0][:, :, 96:104], w_in[:, :, C_AI:C_AI + 8]).then_inc(w_loaded[0], 16)
            sp.wait_ge(group_out, G * NTILE + 2 * G)
            sp.dma_start(c["ikT"][0:64, :], ki[0:64, :]).then_inc(ik_moved, 16)
            sp.dma_start(c["ikT"][64:128, :], ki[0:64, :]).then_inc(ik_moved, 16)
            sp.dma_start(d["ik_scr"], ki[0:64, SEQ:ROWS]).then_inc(ik_moved, 16)
            sp.dma_start(d["gates"], gates[:, :]).then_inc(gates_stored, 16)
            sp.wait_ge(sm_out, NT)
            sp.dma_start(d["o_ik_prompt"].rearrange("a b (n q) e -> (a b q) n e", q=P),
                         c["sm"][:, 0:NB, 0:ID]).then_inc(sm_stored, 16)
            sp.dma_start(d["o_ik_sample"].rearrange("a b t e -> (a b t) e"), c["sm"][0:SR, NB, 0:ID]).then_inc(sm_stored, 16)
            sp.dma_start(d["iw_scr"], c["sm"][0:SR, NB, ID:72]).then_inc(sm_stored, 16)
            sp.wait_ge(raw_rows, 2)
            for b in range(DB):
                sp.dma_start(d["o_conv_sample"][0, b], rows35[DT * b + 1:DT * b + 4, :]).then_inc(raw_stored, 16)
            sp.dma_start(d["o_conv_prompt"][0, 0], rows35[32:35, :]).then_inc(raw_stored, 16)
            sp.wait_ge(raw_stored, 16 * (DB + 1))
            sp.wait_ge(sm_stored, 48)
            sp.wait_ge(ik_moved, 48)
            sp.wait_ge(gates_stored, 16)

        @block.gpsimd
        def _(pool):
            nc.gpsimd.memset(qs[:, 0:4], float(DQK) ** -0.5).then_inc(qs_set, 1)
            nc.gpsimd.memset(qs[:, 4:8], 1.0).then_inc(qs_set, 1)
            for p in range(2):
                nc.gpsimd.memset(u[p][:, 0:3], 0.0).then_inc(halo0, 1)

            def store(j, p, conv, warm):
                n = 2 * j + p
                if conv:
                    pool.wait_ge(conv_out, n + 1)
                    src = acc[p][:, :]
                else:
                    pool.wait_ge(group_out, G * (n + 1))
                    src = u[p][:, 0:ROWS]
                pool.dma_start(d["qt"][n], src).then_inc(stored[p], 16)
            tiles(pool, store)
            pool.wait_ge(group_mm, G * (NTILE - 1))
            nc.gpsimd.memset(wt[0][:, :, 72:96], 0.0).then_inc(w0, 1)
            for p in range(2):
                pool.wait_ge(stored[p], 16 * (NP_CONV + NP_PLAIN))

        @block.tensor
        def _(pe):
            def groups(w, warm_wait, m=P):
                for g in range(G):
                    warm_wait(g)
                    for k in range(KT):
                        ins = nc.tensor.matmul(pg[0:m, g, 0:GW], w[:, k, 0:m], c["xnT"][:, k, g * GW:(g + 1) * GW],
                                               start=k == 0, stop=k == KT - 1)
                    ins.then_inc(group_mm, 1)

            def tile(j, p, conv, warm):
                n = 2 * j + p
                pe.wait_ge(w_loaded[p], 16 * (j + 1))
                first = not warm and p == 0

                def bank_free(g):
                    if not first:
                        pe.wait_ge(group_out, G * (n - 1) + g + 1)
                groups(wt[p], bank_free)
            tiles(pe, tile)
            pe.wait_ge(w_loaded[0], 16 * (NP_CONV + NP_PLAIN) + 32)
            groups(wt[0], lambda g: pe.wait_ge(group_out, G * (NTILE - 1) + g + 1), m=104)
            pe.wait_ge(raw_ready, 2)
            for t in range(KT):
                ins = nc.tensor.transpose(pt[0:35, t // 4, (t % 4) * P:(t % 4 + 1) * P], raw35[:, t, :], c["ident"][:, :])
            ins.then_inc(raw_t, 1)
            pe.wait_ge(group_out, G * NTILE + 2 * G)
            for n in range(NT):
                rows = tile_rows(n)
                if n >= G:
                    pe.wait_ge(sm_out, n - G + 1)
                nc.tensor.transpose(pg[0:rows, n % G, 0:72], ki[0:72, n * P:n * P + rows],
                                    c["ident"][0:72, 0:72]).then_inc(sm_t, 1)

        @block.scalar
        def _(act):
            act.wait_ge(consts, 16 * 6)
            act.wait_ge(halo0, 2)

            def tile(j, p, conv, warm):
                n = 2 * j + p
                for g in range(G):
                    act.wait_ge(group_mm, G * n + g + 1)
                    if conv:
                        if g == 0 and warm:
                            act.wait_ge(conv_step, STEPS * (n - 1))
                        nc.scalar.copy(u[p][:, 3 + g * GW:3 + (g + 1) * GW], pg[:, g, 0:GW]).then_inc(group_out, 1)
                    else:
                        if g == 0:
                            act.wait_ge(stored[p], 16 * j)
                        nc.scalar.copy(u[p][:, g * GW:(g + 1) * GW], pg[:, g, 0:GW]).then_inc(group_out, 1)
                if conv:
                    act.wait_ge(conv_step, STEPS * (n + 1))
                    if warm or p == 1:
                        act.wait_ge(conv_out, n)
                    nc.scalar.activation(sig[:, :], acc[p][:, :], ACT.Sigmoid).then_inc(sig_ready, 1)
            tiles(act, tile)
            for g in range(G):
                act.wait_ge(group_mm, G * NTILE + g + 1)
                nc.scalar.copy(ki[0:72, g * GW:(g + 1) * GW], pg[0:72, g, 0:GW]).then_inc(group_out, 1)
                nc.scalar.activation(gates[:, g * GW:(g + 1) * GW], pg[96:104, g, 0:GW], ACT.Identity,
                                     bias=gbias[:, 0:1]).then_inc(group_out, 1)
            act.wait_ge(raw_t, 1)
            for h in range(2):
                nc.scalar.copy(rows35[:, h * 512:(h + 1) * 512], pt[0:35, h, :]).then_inc(raw_rows, 1)

        @block.vector
        def _(dve):
            dve.wait_ge(qs_set, 2)
            dve.wait_ge(consts, 16 * 6)

            def tile(j, p, conv, warm):
                n = 2 * j + p
                a, raw, us = acc[p], u[p], c["us"]
                dve.wait_ge(group_out, G * (n + 1))
                if warm:
                    dve.wait_ge(stored[p], 16 * j)
                av = a[:, SEQ:ROWS].rearrange("p (b t) -> p b t", t=DT)
                nc.vector.tensor_copy(us[:, n, :, 3:7],
                                      raw[:, 3 + SEQ:3 + ROWS].rearrange("p (b t) -> p b t", t=DT)).then_inc(conv_step, 1)
                nc.vector.tensor_copy(last3[:, n, :], raw[:, SEQ:SEQ + 3]).then_inc(conv_step, 1)
                for k in range(4):
                    wk = cw[:, k, bass.ds(n, 1)]
                    dve.wait_ge(conv_step, STEPS * n + 2 * k + 2)
                    for o, i in ((a[:, 0:SEQ], raw[:, k:k + SEQ]), (av, us[:, n, :, k:k + DT])):
                        if k == 0:
                            ins = nc.vector.tensor_scalar(o, i, wk, cw[:, 4, bass.ds(n, 1)], ALU.mult, ALU.add)
                        else:
                            ins = nc.vector.scalar_tensor_tensor(o, i, wk, o, ALU.mult, ALU.add)
                        ins.then_inc(conv_step, 1)
                dve.wait_ge(sig_ready, n + 1)
                nc.vector.scalar_tensor_tensor(a[:, :], a[:, :], qs[:, bass.ds(n, 1)], sig[:, :],
                                               ALU.mult, ALU.mult).then_inc(conv_out, 1)
            for p in range(2):
                tile(0, p, True, False)
            with dve.Fori(1, NP_CONV) as j:
                for p in range(2):
                    tile(j, p, True, True)
            dve.wait_ge(conv_step, STEPS * 8)
            nc.vector.tensor_copy(raw35[:, :, 0:SR].rearrange("p k (b t) -> p k b t", t=DT),
                                  c["us"][:, :, :, 3:7]).then_inc(raw_ready, 1)
            nc.vector.tensor_copy(raw35[:, :, SR:35], last3[:, :, :]).then_inc(raw_ready, 1)
            for n in range(NT):
                rows = tile_rows(n)
                dve.wait_ge(sm_t, n + 1)
                nc.vector.tensor_copy(c["sm"][0:rows, n, :], pg[0:rows, n % G, 0:72]).then_inc(sm_out, 1)


def index_blocks():
    return list(range(NB - 1, TOPK // P - 1, -1))


def pieces(width, size=1024):
    return [(a, min(size, width - a)) for a in range(0, width, size)]


def row_projection_and_topk_phase(nc, c, d):
    with ExitStack() as ctx:
        sb = lambda name, shape, dt=F32: ctx.enter_context(nc.sbuf_tensor(name, shape, dt))
        sem = phase_semaphores(nc, ctx, "row_projection_and_topk")
        w = [sb(f"w{p}", [P, KT, CH]) for p in range(2)]
        st = sb("st", [P, NT, CH])
        iq = [sb(f"iq{p}", [P, 4, P]) for p in range(2)]
        relu = [sb(f"relu{p}", [P, 1024]) for p in range(2)]
        score = [sb(f"score{p}", [P, SEQ]) for p in range(2)]
        mask = [sb(f"mask{p}", [P, SEQ], BF16) for p in range(2)]
        iws = sb("iws", [P, NB, IH])
        best = sb("best", [P, 8])
        pr = ctx.enter_context(nc.psum_tensor("pr", [P, 4, 512], F32))
        pi = ctx.enter_context(nc.psum_tensor("pi", [P, 2, 1024], F32))
        w_loaded = [sem(f"w_loaded{p}") for p in range(2)]
        iq_loaded = [sem(f"iq_loaded{p}") for p in range(2)]
        row_mm, row_out = sem("row_mm"), sem("row_out")
        half_stored = [sem("first_half_stored"), sem("second_half_stored")]
        idx_mm, relu_ready, relu_used = sem("idx_mm"), sem("relu_ready"), sem("relu_used")
        head_step, scores_ready, top_step, mask_ready = sem("head_step"), sem("scores_ready"), sem("top_step"), sem("mask_ready")
        iws_ready, mask_stored = sem("iws_ready"), [sem(f"mask_stored{p}") for p in range(2)]
        early_step = sem("early_step")

        blocks = index_blocks()
        schedule = [("index", 0), ("index", 1)]
        for n in range(len(ROW_CHUNKS)):
            schedule.append(("rows", n))
            if n + 2 < len(blocks):
                schedule.append(("index", n + 2))
        w_in = d["w_in"].rearrange("a (k p) n -> (a p) k n", p=P)
        r_rows = d["r"][0:SEQ, :].rearrange("(n q) m -> q n m", q=P)
        HALF = NB // 2
        kv_chunk = ROW_CHUNKS.index(C_BK)

        def pieces_before(t):
            return sum(IH * len(pieces((b + 1) * P)) for b in blocks[:t])

        def stored_by(half, n):
            return 16 * ((n + 2 * (n > kv_chunk)) if half == 0 else (2 * n + 4 * (n > kv_chunk)))

        block = ctx.enter_context(nc.Block())

        @block.sync
        def _(sp):
            def load(n):
                sp.dma_start(w[n % 2][:, :, :], w_in[:, :, ROW_CHUNKS[n]:ROW_CHUNKS[n] + CH]).then_inc(w_loaded[n % 2], 16)
            load(0)
            load(1)
            extra = [0, 0]
            for n in range(len(ROW_CHUNKS)):
                cols = slice(n * CH, (n + 1) * CH)
                sp.wait_ge(row_out, NT * n + HALF)
                sp.dma_start(r_rows[:, 0:HALF, cols], st[:, 0:HALF, :]).then_inc(half_stored[0], 16)
                if n == kv_chunk:
                    for name, lo in (("o_k_prompt", 0), ("o_v_prompt", 256)):
                        dst = d[name].rearrange("a b (n q) k e -> (a b q) n (k e)", q=P)
                        sp.dma_start(dst[:, 0:HALF, :], st[:, 0:HALF, lo:lo + 256]).then_inc(half_stored[0], 16)
                sp.wait_ge(row_out, NT * (n + 1))
                sp.dma_start(r_rows[:, HALF:NB, cols], st[:, HALF:NB, :]).then_inc(half_stored[1], 16)
                sp.dma_start(d["r"][SEQ:ROWS, cols], st[0:SR, NB, :]).then_inc(half_stored[1], 16)
                if n == kv_chunk:
                    for name, sname, lo in (("o_k_prompt", "o_k_sample", 0), ("o_v_prompt", "o_v_sample", 256)):
                        dst = d[name].rearrange("a b (n q) k e -> (a b q) n (k e)", q=P)
                        sp.dma_start(dst[:, HALF:NB, :], st[:, HALF:NB, lo:lo + 256]).then_inc(half_stored[1], 16)
                        sp.dma_start(d[sname].rearrange("a b t k e -> (a b t) (k e)"),
                                     st[0:SR, NB, lo:lo + 256]).then_inc(half_stored[1], 16)
                if n + 2 < len(ROW_CHUNKS):
                    sp.wait_ge(row_mm, NT * (n + 1))
                    load(n + 2)
            sp.wait_ge(half_stored[0], stored_by(0, len(ROW_CHUNKS)))
            sp.wait_ge(half_stored[1], stored_by(1, len(ROW_CHUNKS)))

        @block.tensor
        def _(pe):
            piece = 0
            for kind, t in schedule:
                if kind == "rows":
                    pe.wait_ge(w_loaded[t % 2], 16 * (t // 2 + 1))
                    for n in range(NT):
                        m = NT * t + n
                        if m >= 4:
                            pe.wait_ge(row_out, m - 3)
                        rows = tile_rows(n)
                        for k in range(KT):
                            ins = nc.tensor.matmul(pr[0:rows, m % 4, :], c["xnT"][:, k, n * P:n * P + rows],
                                                   w[t % 2][:, k, :], start=k == 0, stop=k == KT - 1)
                        ins.then_inc(row_mm, 1)
                else:
                    b = blocks[t]
                    pe.wait_ge(iq_loaded[t % 2], 16 * (t // 2 + 1))
                    for h in range(IH):
                        half = slice(64 * (h % 2), 64 * (h % 2) + 64)
                        for lo, width in pieces((b + 1) * P):
                            if piece >= 2:
                                pe.wait_ge(relu_ready, piece - 1)
                            for a, n in pieces(width, 512):
                                ins = nc.tensor.matmul(pi[:, piece % 2, a:a + n], iq[t % 2][half, h // 2, :],
                                                       c["ikT"][half, lo + a:lo + a + n], start=True, stop=True)
                            ins.then_inc(idx_mm, 1)
                            piece += 1

        @block.scalar
        def _(act):
            def load_iq(t):
                b = blocks[t]
                if t >= 2:
                    act.wait_ge(idx_mm, pieces_before(t - 1))
                act.dma_start(iq[t % 2][:, :, :], d["qt"][T_IQ:T_ALL, :, b * P:(b + 1) * P].rearrange("t p q -> p t q")
                              ).then_inc(iq_loaded[t % 2], 16)
            load_iq(0)
            piece = 0
            for kind, t in schedule:
                if kind == "rows":
                    for n in range(NT):
                        rows = tile_rows(n)
                        act.wait_ge(row_mm, NT * t + n + 1)
                        if n in (0, HALF) and t:
                            act.wait_ge(half_stored[n // HALF], stored_by(n // HALF, t))
                        nc.scalar.copy(st[0:rows, n, :], pr[0:rows, (NT * t + n) % 4, :]).then_inc(row_out, 1)
                else:
                    if t + 1 < len(blocks):
                        load_iq(t + 1)
                    for _ in range(IH):
                        for lo, width in pieces((blocks[t] + 1) * P):
                            act.wait_ge(idx_mm, piece + 1)
                            if piece >= 2:
                                act.wait_ge(relu_used, piece - 1)
                            nc.scalar.activation(relu[piece % 2][:, 0:width], pi[:, piece % 2, 0:width], ACT.Relu,
                                                 scale=float(ID) ** -0.5).then_inc(relu_ready, 1)
                            piece += 1

        @block.gpsimd
        def _(pool):
            for b in range(TOPK // P):
                nc.gpsimd.memset(mask[b][:, 0:(b + 1) * P], 0.0).then_inc(early_step, 1)
                pool.wait_ge(early_step, 2 * b + 1)
                nc.gpsimd.affine_select(out=mask[b][:, 0:(b + 1) * P], in_=mask[b][:, 0:(b + 1) * P],
                                        compare_op=ALU.is_ge, fill=NEG, base=b * P,
                                        pattern=[[-1, (b + 1) * P]], channel_multiplier=1).then_inc(early_step, 1)
                pool.wait_ge(early_step, 2 * b + 2)
                pool.dma_start(d["mask"][b, :, 0:(b + 1) * P], mask[b][:, 0:(b + 1) * P]).then_inc(mask_stored[b], 16)
            pool.wait_ge(iws_ready, 1)
            piece, steps = 0, 0
            for t, b in enumerate(blocks):
                sc = score[t % 2]
                if t >= 2:
                    pool.wait_ge(mask_ready, t - 1)
                    pool.dma_start(d["mask"][blocks[t - 2], :, 0:(blocks[t - 2] + 1) * P],
                                   mask[t % 2][:, 0:(blocks[t - 2] + 1) * P]).then_inc(mask_stored[t % 2], 16)
                for h in range(IH):
                    wh = iws[:, b, h:h + 1]
                    for lo, width in pieces((b + 1) * P):
                        rl = relu[piece % 2][:, 0:width]
                        pool.wait_ge(relu_ready, piece + 1)
                        if h == 0:
                            nc.gpsimd.tensor_scalar(sc[:, lo:lo + width], rl, wh, None, ALU.mult).then_inc(relu_used, 1)
                        else:
                            nc.gpsimd.tensor_scalar(rl, rl, wh, None, ALU.mult).then_inc(head_step, 1)
                            steps += 1
                            pool.wait_ge(head_step, steps)
                            pool.wait_ge(relu_used, piece)
                            nc.gpsimd.tensor_tensor(sc[:, lo:lo + width], sc[:, lo:lo + width], rl, ALU.add
                                                    ).then_inc(relu_used, 1)
                        piece += 1
                pool.wait_ge(relu_used, piece)
                nc.gpsimd.affine_select(out=sc[:, b * P:(b + 1) * P], in_=sc[:, b * P:(b + 1) * P], compare_op=ALU.is_ge,
                                        fill=HIDDEN, base=0, pattern=[[-1, P]], channel_multiplier=1).then_inc(scores_ready, 1)
            for t in range(len(blocks) - 2, len(blocks)):
                pool.wait_ge(mask_ready, t + 1)
                pool.dma_start(d["mask"][blocks[t], :, 0:(blocks[t] + 1) * P],
                               mask[t % 2][:, 0:(blocks[t] + 1) * P]).then_inc(mask_stored[t % 2], 16)
            for p in range(2):
                pool.wait_ge(mask_stored[p], 16 * (1 + len(blocks) // 2))

        @block.vector
        def _(dve):
            nc.vector.tensor_scalar(iws[:, :, :], c["sm"][:, 0:NB, ID:72], float(IH) ** -0.5, None, ALU.mult
                                    ).then_inc(iws_ready, 1)
            nc.vector.memset(best[:, :], 0.0).then_inc(top_step, 1)
            step = 1
            for t, b in enumerate(blocks):
                sc = score[t % 2][:, 0:(b + 1) * P]
                dve.wait_ge(scores_ready, t + 1)
                for _ in range(TOPK // 8):
                    dve.wait_ge(top_step, step)
                    nc.vector.max(best[:, :], sc).then_inc(top_step, 1)
                    dve.wait_ge(top_step, step + 1)
                    nc.vector.match_replace(sc, best[:, :], sc, TAKEN).then_inc(top_step, 1)
                    step += 2
                dve.wait_ge(top_step, 2 * (TOPK // 8) * (t + 1) + 1)
                dve.wait_ge(mask_stored[t % 2], 16 * (t // 2 + 1))
                nc.vector.tensor_scalar(mask[t % 2][:, 0:(b + 1) * P], sc, TAKEN, NEG, ALU.not_equal, ALU.mult
                                        ).then_inc(mask_ready, 1)


def gate_phase(nc, c, d):
    with ExitStack() as ctx:
        sb = lambda name, shape, dt=F32: ctx.enter_context(nc.sbuf_tensor(name, shape, dt))
        sem = phase_semaphores(nc, ctx, "gate")
        gi, gf = sb("gi", [4, ROWS]), sb("gf", [4, ROWS])
        ab = sb("ab", [4, ROWS])
        lf = sb("lf", [4, ROWS])
        mt = sb("mt", [4, SEQ])
        bt = sb("bt", [4, SEQ])
        reset = sb("reset", [4, SEQ])
        row = sb("row", [P, 4, NB, 4])
        mprev = sb("mprev", [P, NB, 4])
        pz = ctx.enter_context(nc.psum_tensor("pz", [P, 4, NB, 4], F32))
        pb = ctx.enter_context(nc.psum_tensor("pb", [P, 2, 256], F32))
        v, a, g, t = sem("vector_step"), sem("scalar_step"), sem("pool_step"), sem("tensor_step")
        out, loaded = sem("m_stored"), sem("loaded")
        block = ctx.enter_context(nc.Block())

        @block.gpsimd
        def _(pool):
            nc.gpsimd.memset(reset[:, :], 1.0).then_inc(g, 1)
            pool.wait_ge(g, 1)
            nc.gpsimd.memset(reset[:, 0:SEQ:P], 0.0).then_inc(g, 1)
            nc.gpsimd.memset(c["sel"][:, :, :], 0.0).then_inc(g, 1)
            pool.wait_ge(g, 3)
            nc.gpsimd.affine_select(out=c["sel"][:, :, :], in_=c["sel"][:, :, :], compare_op=ALU.not_equal, fill=1.0,
                                    base=0, pattern=[[-1, 4], [0, P]], channel_multiplier=1).then_inc(g, 1)
            nc.gpsimd.memset(c["future"][:, :], 0.0).then_inc(g, 1)
            pool.wait_ge(g, 5)
            nc.gpsimd.affine_select(out=c["future"][:, :], in_=c["future"][:, :], compare_op=ALU.is_ge, fill=NEG,
                                    base=0, pattern=[[1, P]], channel_multiplier=-1).then_inc(g, 1)

        @block.scalar
        def _(act):
            act.wait_ge(v, 1)
            nc.scalar.activation(ab[:, :], ab[:, :], ACT.Exp, scale=-1.0).then_inc(a, 1)
            act.wait_ge(v, 2)
            nc.scalar.activation(ab[:, :], ab[:, :], ACT.Ln).then_inc(a, 1)
            act.wait_ge(v, 12)
            for j, name in enumerate(("ws", "wp", "wi", "em")):
                nc.scalar.activation(c[name][:, :, :], c[name][:, :, :], ACT.Exp).then_inc(a, 1)

        @block.vector
        def _(dve):
            dve.wait_ge(loaded, 32)
            nc.vector.scalar_tensor_tensor(ab[:, :], gf[:, :], -1.0, gf[:, :], ALU.mult, ALU.max).then_inc(v, 1)
            dve.wait_ge(a, 1)
            nc.vector.tensor_scalar(ab[:, :], ab[:, :], 1.0, None, ALU.add).then_inc(v, 1)
            dve.wait_ge(a, 2)
            nc.vector.scalar_tensor_tensor(lf[:, :], gf[:, :], 0.0, ab[:, :], ALU.min, ALU.subtract).then_inc(v, 1)
            dve.wait_ge(v, 3)
            nc.vector.tensor_copy(c["gis"][:, :], gi[:, SEQ:ROWS])
            nc.vector.tensor_copy(c["lfs"][:, :], lf[:, SEQ:ROWS]).then_inc(v, 1)
            nc.vector.tensor_tensor_scan(mt[:, :], lf[:, 0:SEQ], gi[:, 0:SEQ], 0.0, ALU.add, ALU.max).then_inc(v, 1)
            dve.wait_ge(g, 2)
            nc.vector.tensor_tensor_scan(bt[:, :], reset[:, :], lf[:, 0:SEQ], 0.0, ALU.mult, ALU.add).then_inc(v, 1)
            dve.wait_ge(v, 6)
            nc.vector.tensor_tensor(c["g"][:, :], bt[:, :], mt[:, :], ALU.subtract).then_inc(v, 1)
            dve.wait_ge(t, 1)
            nc.vector.tensor_copy(row[:, :, :, :], pz[:, :, :, :]).then_inc(v, 1)
            nc.vector.memset(mprev[:, 0, :], 0.0).then_inc(v, 1)
            dve.wait_ge(t, 2)
            pbm = pb[:, 0, 0:64].rearrange("p (h n) -> p n h", h=4)
            pbg = pb[:, 1, 0:64].rearrange("p (h n) -> p n h", h=4)
            nc.vector.tensor_copy(mprev[:, 1:NB, :], pbm[:, 0:NB - 1, :]).then_inc(v, 1)
            dve.wait_ge(v, 10)
            i, b, m, gg = (row[:, x, :, :] for x in range(4))
            nc.vector.tensor_tensor(c["a"][:, :, :], i, b, ALU.subtract).then_inc(v, 1)
            nc.vector.tensor_tensor(c["wp"][:, :, :], mprev[:, :, :], pbg, ALU.add)
            nc.vector.tensor_tensor(c["wi"][:, :, :], mprev[:, :, :], gg, ALU.add)
            nc.vector.tensor_scalar(c["em"][:, :, :], m, -1.0, None, ALU.mult)
            dve.wait_ge(v, 11)
            nc.vector.tensor_tensor(c["ws"][:, :, :], c["a"][:, :, :], pbg, ALU.add).then_inc(v, 1)

        @block.tensor
        def _(pe):
            pe.wait_ge(v, 7)
            for x, src in enumerate((gi, bt, mt, c["g"])):
                for n in range(NB):
                    ins = nc.tensor.transpose(pz[:, x, n, :], src[0:4, n * P:(n + 1) * P], c["ident"][0:4, 0:4])
            ins.then_inc(t, 1)
            pe.wait_ge(g, 4)
            for x, src in enumerate((mt, c["g"])):
                for h in range(4):
                    ins = nc.tensor.matmul(pb[:, x, h * NB:(h + 1) * NB], c["sel"][:, h, :], src[0:4, P - 1:SEQ:P],
                                           start=True, stop=True)
            ins.then_inc(t, 1)

        @block.sync
        def _(sp):
            sp.dma_start(gi[:, :], d["gates"][0:4, :]).then_inc(loaded, 16)
            sp.dma_start(gf[:, :], d["gates"][4:8, :]).then_inc(loaded, 16)
            sp.wait_ge(v, 5)
            sp.dma_start(d["o_m_prompt"][0, 0].rearrange("(h a) -> h a", a=1), mt[:, SEQ - 1:SEQ]).then_inc(out, 16)
            sp.wait_ge(out, 16)


def key_pieces(i):
    return len(pieces((i + 1) * P))


def key_groups(i):
    return -(-(i + 1) // 4)


def prompt_mixing_phase(nc, c, d):
    with ExitStack() as ctx:
        sb = lambda name, shape, dt=F32: ctx.enter_context(nc.sbuf_tensor("mix_" + name, shape, dt))
        sem = phase_semaphores(nc, ctx, "prompt_mixing")
        ps = lambda name, shape: ctx.enter_context(nc.psum_tensor("mix_" + name, shape, F32))
        kT = sb("kT", [P, KV, SEQ])
        v = sb("v", [P, NB, KV * HD])
        aqk = [sb(f"aqk{p}", [P, 2, AH, P]) for p in range(2)]
        bq = [sb(f"bq{p}", [P, BH, P]) for p in range(2)]
        av = [sb(f"av{p}", [P, AH, DV]) for p in range(2)]
        ozb = [sb(f"ozb{p}", [P, 3, D]) for p in range(2)]
        mk = [sb(f"mk{p}", [P, SEQ], BF16) for p in range(2)]
        prob = [sb(f"prob{p}", [P, SEQ]) for p in range(2)]
        probT = sb("probT", [P, NB, 4, P])
        sg = sb("sg", [P, 3, D])
        h = sb("h", [P, AH, DV])
        inter = sb("inter", [P, AH, DV])
        cT = sb("cT", [P, AH, DV])
        nT = sb("nT", [P, AH])
        nw = sb("nw", [P, AH])
        kw = sb("kw", [P, AH, P])
        dmat = sb("dmat", [P, AH, P])
        sd = sb("sd", [P, AH, P])
        na = sb("na", [P, D])
        ya = sb("ya", [P, AH, DV])
        yb = sb("yb", [P, BH, P])
        oT = sb("oT", [P, 4, P])
        den = sb("den", [P, 4, AH])
        ones = sb("ones", [P, 1])
        mx = sb("mx", [P, 2, 2])
        sums = sb("sums", [P, 2, BH])
        rsum = sb("rsum", [P, BH])
        cout = sb("cout", [P, AH, 2, P])
        slot = ps("slot", [P, 2, 1024])
        pg, ptr, psm = ps("pg", [P, 2, 512]), ps("ptr", [P, 512]), ps("psm", [P, 512])
        resident, loaded = sem("resident"), [sem(f"loaded{p}") for p in range(2)]
        state_init, na_loaded = sem("state_init"), sem("na_loaded")
        gates_scores_mm, inter_mm, intra_mm, state_mm = sem("gates_scores_mm"), sem("inter_mm"), sem("intra_mm"), sem("state_mm")
        dmat_ready, kw_ready, inter_ready = sem("dmat_ready"), sem("kw_ready"), sem("inter_ready")
        sig_ready, sq_ready, rms_ready, pool_step, gates_ready = sem("sig_ready"), sem("sq_ready"), sem("rms_ready"), sem("pool_step"), sem("gates_ready")
        sd_ready, h_ready, state_ready, chain = sem("sd_ready"), sem("h_ready"), sem("state_ready"), sem("chain")
        rden_ready, ya_ready, ya_stored, yb_stored = sem("rden_ready"), sem("ya_ready"), sem("ya_stored"), sem("yb_stored")
        score_mm, masked, nbias_ready, p_ready = sem("score_mm"), sem("masked"), sem("nbias_ready"), sem("p_ready")
        pt_mm, pt_out = sem("pt_mm"), [sem("pt_out_scalar"), sem("pt_out_vector")]
        o_mm, oT_ready, oback_mm, yb_ready = sem("o_mm"), sem("oT_ready"), sem("oback_mm"), sem("yb_ready")
        last_t, last_out, last_stored = sem("last_t"), sem("last_out"), sem("last_stored")
        SCALE = float(HD) ** -0.5

        before_pieces = [sum(BH * key_pieces(j) for j in range(i)) for i in range(NB + 1)]
        before_groups = [sum(BH * key_groups(j) for j in range(i)) for i in range(NB + 1)]
        LOADS = 6

        def groups_out(eng, n):
            for e in range(2):
                if (n + 1 - e) // 2:
                    eng.wait_ge(pt_out[e], (n + 1 - e) // 2)

        def copy_groups(eng, copy, i, hd, e):
            for q in range(key_groups(i)):
                n = before_groups[i] + hd * key_groups(i) + q
                if n % 2 != e:
                    continue
                eng.wait_ge(pt_mm, n + 1)
                if hd % 4 == 0 and 2 * i + hd // 4:
                    eng.wait_ge(o_mm, 2 * i + hd // 4)
                t0, t1 = 4 * q, min(4 * q + 4, i + 1)
                copy(probT[:, t0:t1, hd % 4, :],
                     pg[:, n % 2, 0:(t1 - t0) * P].rearrange("p (t q) -> p t q", q=P)).then_inc(pt_out[e], 1)

        block = ctx.enter_context(nc.Block())

        @block.sync
        def _(sp):
            sp.dma_start(kT[:, :, :], d["qt"][T_BK:T_IQ, :, 0:SEQ].rearrange("k p s -> p k s")).then_inc(resident, 16)
            sp.dma_start(v[:, :, :], d["r"][0:SEQ, R_BKV + 256:R_BKV + 512].rearrange("(n p) e -> p n e", p=P)
                         ).then_inc(resident, 16)
            sp.dma_start(na[:, :], d["norm_a"][0:1, :].to_broadcast([P, D])).then_inc(na_loaded, 16)
            for i in range(NB):
                p, rows = i % 2, slice(i * P, (i + 1) * P)
                if i >= 2:
                    sp.wait_ge(state_mm, i - 1)
                    sp.wait_ge(yb_ready, 8 * (i - 1))
                    sp.wait_ge(gates_ready, i - 1)
                for dst, src in ((aqk[p][:, :, :, :], d["qt"][0:8, :, rows].rearrange("(a t) p q -> p a t q", a=2)),
                                 (bq[p][:, :, :], d["qt"][T_BQ:T_BK, :, rows].rearrange("t p q -> p t q")),
                                 (av[p][:, :, :], d["r"][rows, 0:D].rearrange("q (h e) -> q h e", h=AH)),
                                 (ozb[p][:, 0:2, :], d["r"][rows, R_AO:R_AO + 2 * D].rearrange("q (a e) -> q a e", a=2)),
                                 (ozb[p][:, 2, :], d["r"][rows, R_BZ:R_BZ + D]),
                                 (mk[p][:, 0:(i + 1) * P], d["mask"][i, :, 0:(i + 1) * P])):
                    sp.dma_start(dst, src).then_inc(loaded[p], 16)

        @block.gpsimd
        def _(pool):
            nc.gpsimd.memset(cT[:, :, :], 0.0).then_inc(state_init, 1)
            nc.gpsimd.memset(nT[:, :], 0.0).then_inc(state_init, 1)
            nc.gpsimd.memset(ones[:, :], 1.0).then_inc(state_init, 1)
            pool.wait_ge(na_loaded, 16)
            for i in range(NB):
                p, rows = i % 2, slice(i * P, (i + 1) * P)
                pool.wait_ge(sig_ready, i + 1)
                nc.gpsimd.tensor_tensor(sg[:, 0, :], sg[:, 0, :], sg[:, 1, :], ALU.mult).then_inc(pool_step, 1)
                nc.gpsimd.tensor_tensor(ozb[p][:, 1, :], ozb[p][:, 1, :], na[:, :], ALU.mult).then_inc(pool_step, 1)
                pool.wait_ge(pool_step, 3 * i + 2)
                nc.gpsimd.tensor_tensor(sg[:, 1, :], sg[:, 0, :], ozb[p][:, 1, :], ALU.mult).then_inc(pool_step, 1)
                nc.gpsimd.tensor_tensor(sg[:, 2, :], sg[:, 2, :], ozb[p][:, 2, :], ALU.mult).then_inc(gates_ready, 1)
                pool.wait_ge(ya_ready, 4 * (i + 1))
                pool.dma_start(d["y"][rows, 0:D].rearrange("q (h e) -> q h e", h=AH), ya[:, :, :]).then_inc(ya_stored, 16)
                pool.wait_ge(yb_ready, 8 * (i + 1))
                pool.dma_start(d["y"][rows, D:2 * D].rearrange("q (h e) -> q h e", h=BH), yb[:, :, :]).then_inc(yb_stored, 16)
            pool.wait_ge(last_out, 3)
            pool.dma_start(d["o_C_prompt"].rearrange("a b h (x q) e -> (a b q) h x e", q=P), cout[:, :, :, :]).then_inc(last_stored, 16)
            pool.dma_start(d["o_n_prompt"][0, 0], h[0:4, 0, 0:P]).then_inc(last_stored, 16)
            pool.wait_ge(last_stored, 32)
            pool.wait_ge(ya_stored, 16 * NB)
            pool.wait_ge(yb_stored, 16 * NB)

        @block.tensor
        def _(pe):
            def scores(i, hd):
                for q, (lo, width) in enumerate(pieces((i + 1) * P)):
                    n = before_pieces[i] + hd * key_pieces(i) + q
                    if hd * key_pieces(i) + q >= 2:
                        pe.wait_ge(masked, n - 1)
                    elif n % 2 == 0:
                        pe.wait_ge(state_ready, i + 1)
                        pe.wait_ge(masked, n - 1) if n >= 2 else None
                    else:
                        pe.wait_ge(h_ready, i + 1)
                        pe.wait_ge(masked, n - 1) if n >= 2 else None
                    for a, m in pieces(width, 512):
                        ins = nc.tensor.matmul(slot[:, n % 2, a:a + m], bq[i % 2][:, hd, :],
                                               kT[:, hd // 4, lo + a:lo + a + m], start=True, stop=True)
                    ins.then_inc(score_mm, 1)

            pe.wait_ge(state_init, 3)
            for i in range(NB):
                p, cols = i % 2, slice(i * P, (i + 1) * P)
                pe.wait_ge(loaded[p], 16 * LOADS * (i // 2 + 1))
                if i:
                    groups_out(pe, before_groups[i])
                    pe.wait_ge(oT_ready, 2 * i)
                    pe.wait_ge(state_ready, i)
                for hh in range(AH):
                    nc.tensor.matmul(pg[:, 0, hh * P:(hh + 1) * P], c["sel"][:, hh, :], c["g"][:, cols], start=True, stop=False)
                    nc.tensor.matmul(pg[:, 0, hh * P:(hh + 1) * P], c["ident"][:, :], c["future"][:, :], start=False, stop=True)
                for hh in range(AH):
                    nc.tensor.matmul(pg[:, 1, hh * P:(hh + 1) * P], aqk[p][:, 1, hh, :], aqk[p][:, 0, hh, :], start=True, stop=True)
                for hh in range(AH):
                    ins = nc.tensor.transpose(ptr[:, hh * P:(hh + 1) * P], aqk[p][:, 1, hh, :], c["ident"][:, :])
                ins.then_inc(gates_scores_mm, 1)
                if i:
                    pe.wait_ge(masked, before_pieces[i])
                    pe.wait_ge(yb_ready, 8 * i)
                for hh in range(AH):
                    nc.tensor.matmul(slot[:, 0, hh * DV:(hh + 1) * DV], aqk[p][:, 0, hh, :], cT[:, hh, :], start=True, stop=True)
                    ins = nc.tensor.matmul(psm[:, hh:hh + 1], aqk[p][:, 0, hh, :], nT[:, hh:hh + 1], start=True, stop=True)
                ins.then_inc(inter_mm, 1)
                pe.wait_ge(sd_ready, i + 1)
                for hh in range(AH):
                    nc.tensor.matmul(slot[:, 1, hh * DV:(hh + 1) * DV], sd[:, hh, :], av[p][:, hh, :], start=True, stop=True)
                    ins = nc.tensor.matmul(psm[:, 8 + hh:9 + hh], sd[:, hh, :], ones[:, :], start=True, stop=True)
                ins.then_inc(intra_mm, 1)
                pe.wait_ge(kw_ready, i + 1)
                pe.wait_ge(inter_ready, i + 1)
                for hh in range(AH):
                    nc.tensor.matmul(slot[:, 0, hh * DV:(hh + 1) * DV], kw[:, hh, :], av[p][:, hh, :], start=True, stop=True)
                    ins = nc.tensor.matmul(ptr[:, hh:hh + 1], kw[:, hh, :], ones[:, :], start=True, stop=True)
                ins.then_inc(state_mm, 1)
                scores(i, 0)
                for hd in range(BH):
                    if hd + 1 < BH:
                        scores(i, hd + 1)
                    pe.wait_ge(p_ready, BH * i + hd + 1)
                    for q in range(key_groups(i)):
                        n = before_groups[i] + hd * key_groups(i) + q
                        if n >= 2:
                            pe.wait_ge(pt_out[n % 2], n // 2)
                        if hd == 0 and q < 2:
                            pe.wait_ge(sd_ready, i + 1)
                            pe.wait_ge(dmat_ready, i + 1)
                        for t in range(4 * q, min(4 * q + 4, i + 1)):
                            ins = nc.tensor.transpose(pg[:, n % 2, (t % 4) * P:(t % 4 + 1) * P],
                                                      prob[hd % 2][:, t * P:(t + 1) * P], c["ident"][:, :])
                        ins.then_inc(pt_mm, 1)
                    if hd % 4 == 3:
                        kv = hd // 4
                        groups_out(pe, before_groups[i] + (hd + 1) * key_groups(i))
                        pe.wait_ge(state_ready, i + 1)
                        if 2 * i + kv:
                            pe.wait_ge(oT_ready, 2 * i + kv)
                        for t in range(i + 1):
                            ins = nc.tensor.matmul(ptr[:, :], v[:, t, kv * HD:(kv + 1) * HD], probT[:, t, :, :],
                                                   start=t == 0, stop=t == i)
                        ins.then_inc(o_mm, 1)
                        pe.wait_ge(oT_ready, 2 * i + kv + 1)
                        pe.wait_ge(rden_ready, i + 1)
                        if 2 * i + kv:
                            pe.wait_ge(yb_ready, 8 * i + 4 * kv)
                        for g in range(4):
                            ins = nc.tensor.transpose(psm[:, g * P:(g + 1) * P], oT[:, g, :], c["ident"][:, :])
                        ins.then_inc(oback_mm, 1)
            pe.wait_ge(state_ready, NB)
            pe.wait_ge(masked, before_pieces[NB])
            pe.wait_ge(yb_ready, 8 * NB)
            for hh in range(AH):
                for x in range(2):
                    nc.tensor.transpose(slot[:, hh // 2, (hh % 2 * 2 + x) * P:(hh % 2 * 2 + x + 1) * P],
                                        cT[:, hh, x * P:(x + 1) * P], c["ident"][:, :])
            nc.tensor.transpose(psm[0:4, 0:P], nT[:, :], c["ident"][:, :]).then_inc(last_t, 1)

        @block.scalar
        def _(act):
            def exp(i, hd):
                n = BH * i + hd
                act.wait_ge(nbias_ready, n + 1)
                if i and hd < 2:
                    act.wait_ge(yb_ready, 8 * i)
                nc.scalar.activation(prob[hd % 2][:, 0:(i + 1) * P], prob[hd % 2][:, 0:(i + 1) * P], ACT.Exp,
                                     scale=SCALE, bias=mx[:, hd % 2, 1:2], accum_out=sums[:, 0, hd:hd + 1]).then_inc(p_ready, 1)

            for i in range(NB):
                p = i % 2
                act.wait_ge(gates_scores_mm, i + 1)
                for hh in range(AH):
                    ins = nc.scalar.activation(dmat[:, hh, :], pg[:, 0, hh * P:(hh + 1) * P], ACT.Exp, bias=c["a"][:, i, hh:hh + 1])
                ins.then_inc(dmat_ready, 1)
                for hh in range(AH):
                    ins = nc.scalar.activation(kw[:, hh, :], ptr[:, hh * P:(hh + 1) * P], ACT.Copy, scale=c["ws"][:, i, hh:hh + 1])
                ins.then_inc(kw_ready, 1)
                act.wait_ge(inter_mm, i + 1)
                for hh in range(AH):
                    ins = nc.scalar.activation(inter[:, hh, :], slot[:, 0, hh * DV:(hh + 1) * DV], ACT.Copy,
                                               scale=c["wi"][:, i, hh:hh + 1])
                ins.then_inc(inter_ready, 1)
                act.wait_ge(rden_ready, i + 1)
                for hh in range(AH):
                    ins = nc.scalar.activation(inter[:, hh, :], h[:, hh, :], ACT.Square, scale=den[:, 2, hh:hh + 1],
                                               accum_out=den[:, 3, hh:hh + 1])
                ins.then_inc(sq_ready, 1)
                act.wait_ge(sq_ready, i + 1)
                nc.scalar.activation(den[:, 1, :], den[:, 3, :], ACT.Sqrt, scale=1.0 / DV, bias=c["eps"][:, 0:1]).then_inc(rms_ready, 1)
                act.wait_ge(loaded[p], 16 * LOADS * (i // 2 + 1))
                if i:
                    act.wait_ge(ya_ready, 4 * i)
                    act.wait_ge(yb_ready, 8 * i)
                nc.scalar.activation(sg[:, :, :], ozb[p][:, :, :], ACT.Sigmoid).then_inc(sig_ready, 1)
                exp(i, 0)
                for hd in range(BH):
                    if hd + 1 < BH:
                        exp(i, hd + 1)
                    copy_groups(act, nc.scalar.copy, i, hd, 0)
                    if hd % 4 == 3:
                        kv = hd // 4
                        act.wait_ge(o_mm, 2 * i + kv + 1)
                        if 2 * i + kv:
                            act.wait_ge(oback_mm, 2 * i + kv)
                        nc.scalar.copy(oT[:, :, :], ptr[:, :].rearrange("p (g q) -> p g q", g=4)).then_inc(oT_ready, 1)
            act.wait_ge(last_t, 1)
            for x in range(2):
                nc.scalar.copy(cout[:, 2 * x:2 * x + 2, :, :],
                               slot[:, x, 0:512].rearrange("p (h x e) -> p h x e", h=2, x=2)).then_inc(last_out, 1)
            nc.scalar.copy(h[0:4, 0, 0:P], psm[0:4, 0:P]).then_inc(last_out, 1)

        @block.vector
        def _(dve):
            links = [0]

            def link(ins):
                links[0] += 1
                ins.then_inc(chain, 1)
                dve.wait_ge(chain, links[0])

            def mask_scores(i, hd):
                b = hd % 2
                for q, (lo, width) in enumerate(pieces((i + 1) * P)):
                    n = before_pieces[i] + hd * key_pieces(i) + q
                    dve.wait_ge(score_mm, n + 1)
                    if q == 0 and BH * i + hd >= 2:
                        j, hp = (i, hd - 2) if hd >= 2 else (i - 1, hd + 6)
                        dve.wait_ge(pt_mm, before_groups[j] + (hp + 1) * key_groups(j))
                    if q:
                        dve.wait_ge(masked, n)
                    nc.vector.tensor_tensor_reduce(out=prob[b][:, lo:lo + width], in0=slot[:, n % 2, 0:width],
                                                   in1=mk[i % 2][:, lo:lo + width], scale=1.0,
                                                   scalar=mx[:, b, 0:1] if q else TAKEN, op0=ALU.add, op1=ALU.max,
                                                   accum_out=mx[:, b, 0:1]).then_inc(masked, 1)
                dve.wait_ge(masked, n + 1)
                if BH * i + hd >= 2:
                    dve.wait_ge(p_ready, BH * i + hd - 1)
                nc.vector.tensor_scalar(mx[:, b, 1:2], mx[:, b, 0:1], -SCALE, None, ALU.mult).then_inc(nbias_ready, 1)

            for i in range(NB):
                p = i % 2
                dve.wait_ge(gates_scores_mm, i + 1)
                dve.wait_ge(dmat_ready, i + 1)
                nc.vector.tensor_tensor(sd[:, :, :], pg[:, 1, :].rearrange("p (h q) -> p h q", h=AH), dmat[:, :, :],
                                        ALU.mult).then_inc(sd_ready, 1)
                dve.wait_ge(inter_ready, i + 1)
                dve.wait_ge(intra_mm, i + 1)
                nc.vector.tensor_tensor(h[:, :, :], inter[:, :, :], slot[:, 1, :].rearrange("p (h e) -> p h e", h=AH),
                                        ALU.add).then_inc(h_ready, 1)
                dve.wait_ge(h_ready, i + 1)
                link(nc.vector.tensor_tensor(den[:, 0, :], psm[:, 0:4], c["wi"][:, i, :], ALU.mult))
                link(nc.vector.tensor_tensor(den[:, 0, :], psm[:, 8:12], den[:, 0, :], ALU.add))
                link(nc.vector.scalar_tensor_tensor(den[:, 1, :], den[:, 0, :], -1.0, den[:, 0, :], ALU.mult, ALU.max))
                link(nc.vector.tensor_tensor(den[:, 1, :], den[:, 1, :], c["em"][:, i, :], ALU.max))
                nc.vector.reciprocal(den[:, 2, :], den[:, 1, :]).then_inc(rden_ready, 1)
                dve.wait_ge(state_mm, i + 1)
                for hh in range(AH):
                    nc.vector.scalar_tensor_tensor(cT[:, hh, :], cT[:, hh, :], c["wp"][:, i, hh:hh + 1],
                                                   slot[:, 0, hh * DV:(hh + 1) * DV], ALU.mult, ALU.add)
                link(nc.vector.tensor_tensor(nw[:, :], nT[:, :], c["wp"][:, i, :], ALU.mult))
                nc.vector.tensor_tensor(nT[:, :], nw[:, :], ptr[:, 0:4], ALU.add).then_inc(state_ready, 1)
                dve.wait_ge(rms_ready, i + 1)
                link(nc.vector.reciprocal(den[:, 0, :], den[:, 1, :]))
                link(nc.vector.tensor_tensor(den[:, 0, :], den[:, 0, :], den[:, 2, :], ALU.mult))
                dve.wait_ge(gates_ready, i + 1)
                if i:
                    dve.wait_ge(ya_stored, 16 * i)
                for hh in range(AH):
                    nc.vector.scalar_tensor_tensor(ya[:, hh, :], h[:, hh, :], den[:, 0, hh:hh + 1],
                                                   sg[:, 1, hh * DV:(hh + 1) * DV], ALU.mult, ALU.mult).then_inc(ya_ready, 1)
                mask_scores(i, 0)
                for hd in range(BH):
                    if hd + 1 < BH:
                        mask_scores(i, hd + 1)
                    copy_groups(dve, nc.vector.tensor_copy, i, hd, 1)
                    if hd % 4 == 3:
                        kv = hd // 4
                        dve.wait_ge(oback_mm, 2 * i + kv + 1)
                        link(nc.vector.reciprocal(rsum[:, 4 * kv:4 * kv + 4], sums[:, 0, 4 * kv:4 * kv + 4]))
                        if i and kv == 0:
                            dve.wait_ge(yb_stored, 16 * i)
                        for g in range(4):
                            hq = 4 * kv + g
                            nc.vector.scalar_tensor_tensor(yb[:, hq, :], psm[:, g * P:(g + 1) * P], rsum[:, hq:hq + 1],
                                                           sg[:, 2, hq * P:(hq + 1) * P], ALU.mult, ALU.mult).then_inc(yb_ready, 1)


class Steps:

    def __init__(self, sem, *names):
        self.sem, self.names, self.done = sem, list(names), 0
        assert len(set(names)) == len(names), "a step's name is used twice"

    def __getitem__(self, name):
        return self.names.index(name) + 1

    def step(self, name):
        assert self.names[self.done] == name, (self.names[self.done], name)
        self.done += 1
        return 1


GATHERS = DB // 2
SB_COLS = PAST + DT
SEG = SB_COLS // 4


def sample_index_phase(nc, c, d):
    with ExitStack() as ctx:
        sb = lambda name, shape, dt=F32: ctx.enter_context(nc.sbuf_tensor("si_" + name, shape, dt))
        sem = phase_semaphores(nc, ctx, "sample_index")
        ps = lambda name, shape: ctx.enter_context(nc.psum_tensor("si_" + name, shape, F32))
        pages = [sb(f"pages{p}", [P, PAGE * ID]) for p in range(2)]
        ptab = sb("ptab", [P, GATHERS], I32)
        iq = sb("iq", [P, IH, SR])
        iqd = sb("iqd", [P, DB, 2, IH, DT])
        iwc = sb("iwc", [P, GATHERS])
        msel = sb("msel", [P, 2, 36])
        w2 = sb("w2", [P, GATHERS, 2, 36])
        ik = sb("ik", [ID, SR])
        keys = [sb(f"keys{p}", [P, 8, P]) for p in range(2)]
        relu = [sb(f"relu{p}", [P, 512]) for p in range(2)]
        rnew = [sb(f"rnew{p}", [P, DT]) for p in range(2)]
        score = [sb(f"score{p}", [36, SB_COLS]) for p in range(2)]
        later = sb("later", [36, DT])
        pt = ps("pt", [P, 2, 512])
        p1 = ps("p1", [P, 2, 512])
        p2 = ps("p2", [P, 2, 512])
        pn = ps("pn", [P, 512])
        pn2 = ps("pn2", [P, 512])
        loaded, paged, stored = sem("loaded"), [sem(f"paged{p}") for p in range(2)], [sem(f"score_stored{p}") for p in range(2)]
        setup = Steps(sem("setup"), "msel0", "sel0", "sel1", "sel2", "sel3", "iqd0", "iqd1", "w2")
        iwr, zeroed = sem("iw_reordered"), sem("zeroed")
        pages_t, keys_out = sem("pages_t"), [sem("keys_out_scalar"), sem("keys_out_vector")]
        heads_mm, relu_ready = sem("heads_mm"), [sem("relu_ready_scalar"), sem("relu_ready_vector")]
        sum_mm, score_out = sem("sum_mm"), [sem("score_out_even"), sem("score_out_odd")]
        new_mm, new_relu, new_sum, new_out = sem("new_mm"), sem("new_relu"), sem("new_sum"), sem("new_out")
        NG = PAGE // 2 // 8
        def copy_keys(eng, copy, half, n):
            eng.wait_ge(pages_t, n + 1)
            if n >= 2:
                eng.wait_ge(heads_mm, 2 * (n - 1))
            copy(keys[n % 2][:, 4 * half:4 * half + 4, :],
                 pt[:, half, :].rearrange("p (k s) -> p k s", k=4)).then_inc(keys_out[half], 1)

        def copy_scores(eng, copy, e, n):
            q, g = n // NG, n % NG
            eng.wait_ge(sum_mm, 2 * n + 1 + e)
            if g == 0 and q >= 2:
                eng.wait_ge(stored[q % 2], 16 * 8 * (q // 2))
            dst = score[q % 2][:, 0:PAST].rearrange("r (p k) -> r k p", k=PAGE)[:, 16 * g + e:16 * g + 16:2, :]
            copy(dst, p2[0:36, e, :].rearrange("r (k p) -> r k p", k=8)).then_inc(score_out[e], 1)

        block = ctx.enter_context(nc.Block())

        @block.sync
        def _(sp):
            for q in range(GATHERS):
                sp.dma_start(ptab[:, q:q + 1], d["page_table"][2 * q:2 * q + 2, :].rearrange("b (p a) -> (b p) a", a=1)
                             ).then_inc(loaded, 16)
            qsrc = d["qt"][T_IQ:T_ALL, :, SEQ:ROWS].rearrange("t (e d) s -> d (t e) s", e=2)
            for e in range(2):
                sp.dma_start(iq[64 * e:64 * e + 64, :, :], qsrc).then_inc(loaded, 16)
            sp.dma_start(ik[:, :], d["ik_scr"]).then_inc(loaded, 16)
            for b in range(2):
                for h in range(IH):
                    sp.dma_start(d["iwc_scr"][b, h], d["iw_scr"].rearrange("(q b t) h -> b h t q", b=2, t=DT)[b, h]).then_inc(iwr, 16)
            sp.wait_ge(iwr, 16 * 2 * IH)
            for b in range(2):
                for e in range(2):
                    sp.dma_start(iwc[64 * b + 32 * e:64 * b + 32 * e + 32, :],
                                 d["iwc_scr"][b].rearrange("h t q -> (h t) q")).then_inc(loaded, 16)
            for q in range(GATHERS):
                for e in range(2):
                    sp.wait_ge(score_out[e], NG * (q + 1))
                sp.wait_ge(new_out, q + 1)
                for b in range(2):
                    row = (2 * q + b) * DT
                    for s in range(4):
                        sp.dma_start(d["ss_scr"][s, row:row + DT, :],
                                     score[q % 2][32 * b:32 * b + DT, s * SEG:(s + 1) * SEG]).then_inc(stored[q % 2], 16)
            for p in range(2):
                sp.wait_ge(stored[p], 16 * 8 * GATHERS // 2)

        @block.gpsimd
        def _(pool):
            nc.gpsimd.memset(iqd[:, :, :, :, :], 0.0).then_inc(zeroed, 1)
            nc.gpsimd.memset(msel[:, :, :], 0.0).then_inc(zeroed, 1)
            for p in range(2):
                nc.gpsimd.memset(rnew[p][:, :], 0.0).then_inc(zeroed, 1)
            nc.gpsimd.memset(later[:, :], 0.0).then_inc(zeroed, 1)
            pool.wait_ge(zeroed, 5)
            for b in range(2):
                nc.gpsimd.affine_select(out=later[32 * b:32 * b + DT, :], in_=later[32 * b:32 * b + DT, :],
                                        compare_op=ALU.is_ge, fill=HIDDEN, base=0, pattern=[[-1, DT]],
                                        channel_multiplier=1).then_inc(zeroed, 1)
            pool.wait_ge(zeroed, 7)
            pool.wait_ge(loaded, 16 * (GATHERS + 7))
            for q in range(GATHERS):
                if q >= 2:
                    pool.wait_ge(pages_t, NG * (q - 1))
                pool.indirect_dma_start(out=pages[q % 2][:, :], out_offset=None,
                                        in_=d["cache_idx_k"].rearrange("a n s e -> (a n) (s e)"),
                                        in_offset=bass.IndirectOffsetOnAxis(ap=ptab[:, q:q + 1].bitcast(U32), axis=0)
                                        ).then_inc(paged[q % 2], 16)

        @block.tensor
        def _(pe):
            pe.wait_ge(setup.sem, setup["w2"])
            for q in range(GATHERS):
                pe.wait_ge(paged[q % 2], 16 * (q // 2 + 1))
                for b in range(2):
                    n = 2 * q + b
                    if n:
                        pe.wait_ge(new_relu, n)
                    nc.tensor.matmul(pn[0:32, 0:DT], iqd[0:64, n, 0, :, :].rearrange("p h t -> p (h t)"),
                                     ik[:, n * DT:(n + 1) * DT], start=True, stop=True).then_inc(new_mm, 1)
                pe.wait_ge(new_relu, 2 * q + 2)
                if q:
                    pe.wait_ge(new_out, q)
                nc.tensor.matmul(pn2[0:36, 0:DT], w2[:, q, 0, :], rnew[q % 2][:, :], start=True, stop=True).then_inc(new_sum, 1)

                def turn(g):
                    n = NG * q + g
                    for half in range(2):
                        if n:
                            pe.wait_ge(keys_out[half], n)
                        for k in range(4):
                            kp = 8 * g + 4 * half + k
                            ins = nc.tensor.transpose(pt[:, half, k * P:(k + 1) * P], pages[q % 2][:, kp * P:(kp + 1) * P],
                                                      c["ident"][:, :])
                    ins.then_inc(pages_t, 1)

                def total(g):
                    n = NG * q + g
                    for e in range(2):
                        pe.wait_ge(relu_ready[e], n + 1)
                    for e in range(2):
                        if n:
                            pe.wait_ge(score_out[e], n)
                        nc.tensor.matmul(p2[0:36, e, :], w2[:, q, e, :], relu[n % 2][:, :], start=True, stop=True).then_inc(sum_mm, 1)

                turn(0)
                for g in range(NG):
                    n = NG * q + g
                    for e in range(2):
                        pe.wait_ge(keys_out[e], n + 1)
                    for b in range(2):
                        if n:
                            pe.wait_ge(relu_ready[b], n)
                        nc.tensor.matmul(p1[0:64, b, :], iqd[:, 2 * q + b, :, :, :].rearrange("p e h t -> p (e h t)"),
                                         keys[n % 2][:, :, 64 * b:64 * b + 64], start=True, stop=True).then_inc(heads_mm, 1)
                    if g + 1 < NG:
                        turn(g + 1)
                    total(g)

        @block.scalar
        def _(act):
            act.wait_ge(zeroed, 7)
            for q in range(GATHERS):
                for b in range(2):
                    act.wait_ge(new_mm, 2 * q + b + 1)
                    if q >= 2:
                        act.wait_ge(new_sum, q - 1)
                    nc.scalar.activation(rnew[q % 2][64 * b:64 * b + 32, :], pn[0:32, 0:DT], ACT.Relu,
                                         scale=float(ID) ** -0.5).then_inc(new_relu, 1)
                copy_keys(act, nc.scalar.copy, 0, NG * q)
                for g in range(NG):
                    n = NG * q + g
                    act.wait_ge(heads_mm, 2 * n + 1)
                    if n >= 2:
                        act.wait_ge(sum_mm, 2 * (n - 1))
                    nc.scalar.activation(relu[n % 2][0:64, :], p1[0:64, 0, :], ACT.Relu, scale=float(ID) ** -0.5
                                         ).then_inc(relu_ready[0], 1)
                    if g + 1 < NG:
                        copy_keys(act, nc.scalar.copy, 0, n + 1)
                    copy_scores(act, nc.scalar.copy, 0, n)

        @block.vector
        def _(dve):
            dve.wait_ge(zeroed, 7)
            dve.wait_ge(loaded, 16 * (GATHERS + 7))
            nc.vector.tensor_copy(msel[0:1, 0, 0:1], msel[0:1, 0, 0:1]).then_inc(setup.sem, setup.step("msel0"))
            dve.wait_ge(setup.sem, setup["msel0"])
            for b in range(2):
                for e in range(2):
                    lo = 64 * b + 32 * e
                    nc.vector.reduce_sum(msel[lo:lo + 32, e, 32 * b:32 * b + DT],
                                         c["ident"][lo:lo + 32, lo:lo + 32].rearrange("p (h t) -> p t h", t=DT),
                                         AX_X).then_inc(setup.sem, setup.step(f"sel{2 * b + e}"))
            for e in range(2):
                nc.vector.tensor_copy(iqd[64 * e:64 * e + 64, :, e, :, :],
                                      iq[64 * e:64 * e + 64, :, :].rearrange("p h (b t) -> p b h t", t=DT)
                                      ).then_inc(setup.sem, setup.step(f"iqd{e}"))
            dve.wait_ge(setup.sem, setup["sel3"])
            for q in range(GATHERS):
                ins = nc.vector.tensor_scalar(w2[:, q, :, :], msel[:, :, :], iwc[:, q:q + 1], float(IH) ** -0.5,
                                              ALU.mult, ALU.mult)
            ins.then_inc(setup.sem, setup.step("w2"))
            for q in range(GATHERS):
                dve.wait_ge(new_sum, q + 1)
                if q >= 2:
                    dve.wait_ge(stored[q % 2], 16 * 8 * (q // 2))
                nc.vector.tensor_tensor(score[q % 2][:, PAST:SB_COLS], pn2[0:36, 0:DT], later[:, :], ALU.add).then_inc(new_out, 1)
                copy_keys(dve, nc.vector.tensor_copy, 1, NG * q)
                for g in range(NG):
                    n = NG * q + g
                    dve.wait_ge(heads_mm, 2 * n + 2)
                    if n >= 2:
                        dve.wait_ge(sum_mm, 2 * (n - 1))
                    nc.vector.tensor_scalar(relu[n % 2][64:128, :], p1[0:64, 1, :], float(ID) ** -0.5, 0.0,
                                            ALU.mult, ALU.max).then_inc(relu_ready[1], 1)
                    if g + 1 < NG:
                        copy_keys(dve, nc.vector.tensor_copy, 1, n + 1)
                    copy_scores(dve, nc.vector.tensor_copy, 1, n)


def sample_select_phase(nc, c, d):
    with ExitStack() as ctx:
        sb = lambda name, shape, dt=F32: ctx.enter_context(nc.sbuf_tensor("ss_" + name, shape, dt))
        sem = phase_semaphores(nc, ctx, "sample_select")
        score = sb("score", [P, SEG])
        val = sb("val", [P, TOPK])
        idx = sb("idx", [P, TOPK], U32)
        idf = sb("idf", [P, TOPK])
        segb = sb("segb", [P, 1])
        val4 = sb("val4", [SR, 4, TOPK])
        idf4 = sb("idf4", [SR, 4, TOPK])
        pos = sb("pos", [SR, TOPK])
        best = sb("best", [SR, 8])
        pint = sb("pint", [SR, 2, TOPK], I32)
        pfl = sb("pfl", [SR, 2, TOPK])
        ptab = sb("ptab", [SR, PAGES], I32)
        ptf = sb("ptf", [SR, PAGES])
        iota = sb("iota", [SR, PAGES])
        one = sb("one", [SR, 64, PAGES])
        phys = sb("phys", [SR, TOPK])
        seln = sb("seln", [SR, DT])
        junk = sb("junk", [SR, TOPK])
        bm = sb("bm", [SR, DB])
        bias = sb("bias", [SR, TOPK + SR])
        expand = sb("expand", [SR, SR, 4])
        pp = ctx.enter_context(nc.psum_tensor("ss_pp", [P, 2, 512], F32))
        pb = ctx.enter_context(nc.psum_tensor("ss_pb", [P, 512], F32))
        loaded, moved, chain = sem("loaded"), sem("moved"), sem("chain")
        merged_ready, turned, copied, iota_ready, select_done = sem("merged_ready"), sem("turned"), sem("copied"), sem("iota_ready"), sem("select_done")
        block = ctx.enter_context(nc.Block())

        @block.sync
        def _(sp):
            sp.dma_start(score[:, :], d["ss_scr"].rearrange("s r k -> (s r) k")).then_inc(loaded, 16)
            for b in range(DB):
                sp.dma_start(ptab[DT * b:DT * b + DT, :], d["page_table"][b:b + 1, :].to_broadcast([DT, PAGES])).then_inc(loaded, 16)
            sp.wait_ge(merged_ready, 1)
            for s in range(4):
                sp.dma_start(val4[:, s, :], val[32 * s:32 * s + 32, :]).then_inc(moved, 16)
                sp.dma_start(idf4[:, s, :], idf[32 * s:32 * s + 32, :]).then_inc(moved, 16)

        @block.gpsimd
        def _(pool):
            nc.gpsimd.iota(pint[:, 0, 0:PAGES], pattern=[[1, PAGES]], base=0, channel_multiplier=0).then_inc(iota_ready, 1)

        @block.vector
        def _(dve):
            links = [0]

            def link(ins):
                links[0] += 1
                ins.then_inc(chain, 1)
                dve.wait_ge(chain, links[0])

            for s in range(4):
                nc.vector.memset(segb[32 * s:32 * s + 32, :], float(s * SEG + 1))
            dve.wait_ge(iota_ready, 1)
            link(nc.vector.tensor_copy(iota[:, :], pint[:, 0, 0:PAGES]))
            dve.wait_ge(loaded, 16 * (1 + DB))
            link(nc.vector.tensor_copy(ptf[:, :], ptab[:, :]))
            for j in range(TOPK // 8):
                v8 = val[:, 8 * j:8 * j + 8]
                link(nc.vector.max(v8, score[:, :]))
                nc.vector.max_index(idx[:, 8 * j:8 * j + 8], v8, score[:, :])
                link(nc.vector.match_replace(score[:, :], v8, score[:, :], TAKEN))
            link(nc.vector.tensor_copy(idf[:, :], idx[:, :]))
            nc.vector.tensor_scalar(idf[:, :], idf[:, :], segb[:, 0:1], None, ALU.add).then_inc(merged_ready, 1)
            dve.wait_ge(moved, 16 * 8)
            flat = val4[:, :, :].rearrange("p s k -> p (s k)")
            for j in range(TOPK // 8):
                link(nc.vector.max(best[:, :], flat))
                link(nc.vector.match_replace(flat, best[:, :], flat, TAKEN))
            link(nc.vector.scalar_tensor_tensor(flat, flat, TAKEN, idf4[:, :, :].rearrange("p s k -> p (s k)"),
                                                ALU.is_equal, ALU.mult))
            for j in range(TOPK // 8):
                link(nc.vector.max(pos[:, 8 * j:8 * j + 8], flat))
                link(nc.vector.match_replace(flat, pos[:, 8 * j:8 * j + 8], flat, -1.0))
            link(nc.vector.tensor_scalar(pos[:, :], pos[:, :], -1.0, None, ALU.add))
            link(nc.vector.tensor_copy(pint[:, 1, :], pos[:, :]))
            nc.vector.tensor_scalar(pint[:, 0, :], pint[:, 1, :], 7, None, ALU.arith_shift_right)
            link(nc.vector.tensor_scalar(pint[:, 1, :], pint[:, 1, :], PAGE - 1, None, ALU.bitwise_and))
            link(nc.vector.tensor_copy(pfl[:, :, :], pint[:, :, :]))
            for q in range(TOPK // 64):
                cols = slice(64 * q, 64 * q + 64)
                link(nc.vector.tensor_tensor(one[:, :, :], pfl[:, 0, cols].unsqueeze(2).to_broadcast([SR, 64, PAGES]),
                                             iota[:, :].unsqueeze(1).to_broadcast([SR, 64, PAGES]), ALU.is_equal))
                link(nc.vector.tensor_tensor(one[:, :, :], one[:, :, :],
                                             ptf[:, :].unsqueeze(1).to_broadcast([SR, 64, PAGES]), ALU.mult))
                link(nc.vector.reduce_sum(phys[:, cols], one[:, :, :], AX_X))
            link(nc.vector.scalar_tensor_tensor(phys[:, :], phys[:, :], float(PAGE), pfl[:, 1, :], ALU.mult, ALU.add))
            nc.vector.tensor_scalar(bias[:, 0:TOPK], pos[:, :], float(PAST), NEG, ALU.is_ge, ALU.mult)
            for t in range(DT):
                link(nc.vector.tensor_scalar(junk[:, :], pos[:, :], float(PAST + t), None, ALU.is_equal, ALU.max,
                                             accum_out=seln[:, t:t + 1]))
            link(nc.vector.reduce_sum(bm[:, :], c["ident"][0:SR, 0:SR].rearrange("p (b t) -> p b t", t=DT), AX_X))
            bnew = bias[:, TOPK:TOPK + SR].rearrange("p (b t) -> p b t", t=DT)
            link(nc.vector.tensor_tensor(bnew, bm[:, :].unsqueeze(2).to_broadcast([SR, DB, DT]),
                                         seln[:, :].unsqueeze(1).to_broadcast([SR, DB, DT]), ALU.mult))
            link(nc.vector.tensor_scalar(bnew, bnew, -1.0, -NEG, ALU.add, ALU.mult))
            nc.vector.tensor_copy(expand[:, :, :], c["ident"][0:SR, 0:SR].unsqueeze(2).to_broadcast([SR, SR, 4])
                                  ).then_inc(select_done, 1)
            dve.wait_ge(turned, 2)
            nc.vector.tensor_copy(c["rowid"][:, :, :], pp[:, 0, 0:2 * SR].rearrange("p (a r) -> p a r", a=2)).then_inc(copied, 1)
            nc.vector.tensor_copy(c["sbias"][:, :], pb[:, 0:TOPK + SR]).then_inc(copied, 1)

        @block.tensor
        def _(pe):
            pe.wait_ge(select_done, 1)
            for a in range(2):
                ins = nc.tensor.transpose(pp[:, 0, a * SR:(a + 1) * SR], phys[:, a * P:(a + 1) * P], c["ident"][0:SR, 0:SR])
            ins.then_inc(turned, 1)
            nc.tensor.matmul(pb[:, 0:TOPK + SR], expand[:, :, :].rearrange("p r g -> p (r g)"), bias[:, :],
                             start=True, stop=True).then_inc(turned, 1)


def sample_attention_phase(nc, c, d):
    with ExitStack() as ctx:
        sb = lambda name, shape, dt=F32: ctx.enter_context(nc.sbuf_tensor("sa_" + name, shape, dt))
        sem = phase_semaphores(nc, ctx, "sample_attention")
        ps = lambda name, shape: ctx.enter_context(nc.psum_tensor("sa_" + name, shape, F32))
        KS = 6
        WIN = 2 * P - 4
        kg = [sb(f"kg{s}", [P, 2, KV * HD]) for s in range(KS)]
        vg = sb("vg", [P, SR, 2, KV * HD])
        q = sb("q", [P, BH, SR])
        qw = [sb(f"qw{p}", [P, KV, WIN]) for p in range(2)]
        qa = sb("qa", [P, KV, SR, 4])
        kTn = sb("kTn", [P, KV, SR])
        vn = sb("vn", [SR, KV * HD])
        kT = [sb(f"kT{p}", [P, KV, 2, P]) for p in range(2)]
        x = sb("x", [P, KV, TOPK + SR])
        xT = sb("xT", [P, KV, 3, P])
        stat = sb("stat", [P, 3, KV])
        oT = sb("oT", [P, KV, SR, 4])
        bz = sb("bz", [SR, D])
        sz = sb("sz", [SR, D])
        yb = sb("yb", [SR, D])
        pk = [ps(f"pk{p}", [P, 512]) for p in range(2)]
        psc = ps("psc", [P, KV, 512])
        pn = ps("pn", [P, 512])
        po = ps("po", [P, 512])
        py = ps("py", [P, 2, 512])
        loaded = sem("loaded")
        k_in = [sem(f"k_in{s}") for s in range(KS)]
        v_in, zero = sem("v_in"), sem("zero")
        window, turned, k_out, score_mm = sem("window"), sem("turned"), sem("k_out"), sem("score_mm")
        v = Steps(sem("vector_steps"), "x", "new", "max", "nmax", "rsum", "norm0", "norm1", "xT0", "yb")
        a = Steps(sem("scalar_steps"), "exp0", "exp1", "xT1", "xTn", "oT", "sig")
        t = Steps(sem("tensor_steps"), "new", "xT", "o", "y")
        sz_ready, y_stored = sem("sz_ready"), sem("y_stored")
        SCALE = float(HD) ** -0.5
        block = ctx.enter_context(nc.Block())

        @block.sync
        def _(sp):
            sp.dma_start(q[:, :, :], d["qt"][T_BQ:T_BK, :, SEQ:ROWS].rearrange("t p s -> p t s")).then_inc(loaded, 16)
            sp.dma_start(kTn[:, :, :], d["qt"][T_BK:T_IQ, :, SEQ:ROWS].rearrange("t p s -> p t s")).then_inc(loaded, 16)
            sp.dma_start(vn[:, :], d["r"][SEQ:ROWS, R_BKV + 256:R_BKV + 512]).then_inc(loaded, 16)
            sp.dma_start(bz[:, :], d["r"][SEQ:ROWS, R_BZ:R_BZ + D]).then_inc(loaded, 16)
            sp.wait_ge(v.sem, v["yb"])
            sp.dma_start(d["y"][SEQ:ROWS, D:2 * D], yb[:, :]).then_inc(y_stored, 16)
            sp.wait_ge(y_stored, 16)

        @block.gpsimd
        def _(pool):
            for p in range(2):
                nc.gpsimd.memset(qw[p][:, :, :], 0.0).then_inc(zero, 1)

            def gather(dst, cache, r, half):
                return pool.indirect_dma_start(out=dst, out_offset=None,
                                               in_=d[cache].rearrange("a n s k e -> (a n s) (k e)"),
                                               in_offset=bass.IndirectOffsetOnAxis(ap=c["rowid"][:, half, r:r + 1], axis=0))
            for r in range(SR):
                if r >= KS:
                    pool.wait_ge(turned, r - KS + 1)
                for half in range(2):
                    gather(kg[r % KS][:, half, :], "cache_k", r, half).then_inc(k_in[r % KS], 16)
                for half in range(2):
                    gather(vg[:, r, half, :], "cache_v", r, half).then_inc(v_in, 16)
            pool.wait_ge(a.sem, a["sig"])
            nc.gpsimd.tensor_tensor(sz[:, :], sz[:, :], bz[:, :], ALU.mult).then_inc(sz_ready, 1)

        @block.tensor
        def _(pe):
            def turn(r):
                pe.wait_ge(k_in[r % KS], 32 * (r // KS + 1))
                if r >= 2:
                    pe.wait_ge(k_out, r - 1)
                for kv in range(KV):
                    for half in range(2):
                        ins = nc.tensor.transpose(pk[r % 2][:, (2 * kv + half) * P:(2 * kv + half + 1) * P],
                                                  kg[r % KS][:, half, kv * HD:(kv + 1) * HD], c["ident"][:, :])
                ins.then_inc(turned, 1)

            turn(0)
            for r in range(SR):
                if r + 1 < SR:
                    turn(r + 1)
                pe.wait_ge(k_out, r + 1)
                pe.wait_ge(window, r + 1)
                lo = P - 4 - 4 * r
                for kv in range(KV):
                    ins = nc.tensor.matmul(psc[:, kv, 0:TOPK], qw[r % 2][:, kv, lo:lo + P],
                                           kT[r % 2][:, kv, :, :].rearrange("p a k -> p (a k)"),
                                           start=r == 0, stop=r == SR - 1)
                ins.then_inc(score_mm, 1)
            for kv in range(KV):
                ins = nc.tensor.matmul(pn[:, kv * SR:(kv + 1) * SR], qa[:, kv, :, :].rearrange("p r g -> p (r g)"),
                                       kTn[:, kv, :], start=True, stop=True)
            ins.then_inc(t.sem, t.step("new"))
            pe.wait_ge(v.sem, v["norm1"])
            for kv in range(KV):
                for half in range(2):
                    nc.tensor.transpose(pk[0][:, (2 * kv + half) * P:(2 * kv + half + 1) * P],
                                        x[:, kv, half * P:(half + 1) * P], c["ident"][:, :])
                ins = nc.tensor.transpose(pk[1][0:SR, kv * P:(kv + 1) * P], x[:, kv, TOPK:TOPK + SR], c["ident"][:, :])
            ins.then_inc(t.sem, t.step("xT"))
            pe.wait_ge(a.sem, a["xTn"])
            pe.wait_ge(v_in, 32 * SR)
            for kv in range(KV):
                for r in range(SR):
                    o = po[:, kv * P + 4 * r:kv * P + 4 * r + 4]
                    for half in range(2):
                        nc.tensor.matmul(o, vg[:, r, half, kv * HD:(kv + 1) * HD], xT[:, kv, half, 4 * r:4 * r + 4],
                                         start=half == 0, stop=False)
                    ins = nc.tensor.matmul(o, vn[:, kv * HD:(kv + 1) * HD], xT[0:SR, kv, 2, 4 * r:4 * r + 4],
                                           start=False, stop=True)
            ins.then_inc(t.sem, t.step("o"))
            pe.wait_ge(a.sem, a["oT"])
            for kv in range(KV):
                for g in range(4):
                    ins = nc.tensor.transpose(py[0:SR, kv, g * P:(g + 1) * P], oT[:, kv, :, g], c["ident"][:, :])
            ins.then_inc(t.sem, t.step("y"))

        @block.vector
        def _(dve):
            dve.wait_ge(zero, 2)
            dve.wait_ge(loaded, 16 * 4)
            nc.vector.tensor_copy(qa[:, :, :, :], q[:, :, :].rearrange("p (k g) r -> p k r g", k=KV))
            for r in range(SR):
                if r >= 2:
                    dve.wait_ge(score_mm, r - 1)
                nc.vector.tensor_copy(qw[r % 2][:, :, P - 4:P],
                                      q[:, :, r].rearrange("p (k g) -> p k g", k=KV)).then_inc(window, 1)
            dve.wait_ge(score_mm, SR)
            nc.vector.tensor_tensor(x[:, :, 0:TOPK], psc[:, :, 0:TOPK],
                                    c["sbias"][:, 0:TOPK].unsqueeze(1).to_broadcast([P, KV, TOPK]), ALU.add
                                    ).then_inc(v.sem, v.step("x"))
            dve.wait_ge(t.sem, t["new"])
            nc.vector.tensor_tensor(x[:, :, TOPK:TOPK + SR], pn[:, 0:KV * SR].rearrange("p (k s) -> p k s", k=KV),
                                    c["sbias"][:, TOPK:TOPK + SR].unsqueeze(1).to_broadcast([P, KV, SR]), ALU.add
                                    ).then_inc(v.sem, v.step("new"))
            dve.wait_ge(v.sem, v["new"])
            nc.vector.reduce_max(stat[:, 0, :], x[:, :, :], AX_X).then_inc(v.sem, v.step("max"))
            dve.wait_ge(v.sem, v["max"])
            nc.vector.tensor_scalar(stat[:, 0, :], stat[:, 0, :], -SCALE, None, ALU.mult).then_inc(v.sem, v.step("nmax"))
            dve.wait_ge(a.sem, a["exp1"])
            nc.vector.reciprocal(stat[:, 2, :], stat[:, 1, :]).then_inc(v.sem, v.step("rsum"))
            dve.wait_ge(v.sem, v["rsum"])
            for kv in range(KV):
                nc.vector.tensor_scalar(x[:, kv, :], x[:, kv, :], stat[:, 2, kv:kv + 1], None, ALU.mult
                                        ).then_inc(v.sem, v.step(f"norm{kv}"))
            dve.wait_ge(t.sem, t["xT"])
            nc.vector.tensor_copy(xT[:, :, 0:2, :], pk[0][:, :].rearrange("p (k h s) -> p k h s", k=KV, h=2)
                                  ).then_inc(v.sem, v.step("xT0"))
            dve.wait_ge(t.sem, t["y"])
            dve.wait_ge(sz_ready, 1)
            nc.vector.tensor_tensor(yb[:, :], py[0:SR, :, :].rearrange("p a b -> p (a b)"), sz[:, :], ALU.mult
                                    ).then_inc(v.sem, v.step("yb"))

        @block.scalar
        def _(act):
            for r in range(SR):
                act.wait_ge(turned, r + 1)
                if r >= 2:
                    act.wait_ge(score_mm, r - 1)
                nc.scalar.copy(kT[r % 2][:, :, :, :], pk[r % 2][:, :].rearrange("p (k h s) -> p k h s", k=KV, h=2)
                               ).then_inc(k_out, 1)
            act.wait_ge(v.sem, v["nmax"])
            for kv in range(KV):
                nc.scalar.activation(x[:, kv, :], x[:, kv, :], ACT.Exp, scale=SCALE, bias=stat[:, 0, kv:kv + 1],
                                     accum_out=stat[:, 1, kv:kv + 1]).then_inc(a.sem, a.step(f"exp{kv}"))
            act.wait_ge(t.sem, t["xT"])
            nc.scalar.copy(xT[0:SR, :, 2, :], pk[1][0:SR, 0:2 * P].rearrange("p (k s) -> p k s", k=KV)
                           ).then_inc(a.sem, a.step("xT1"))
            act.wait_ge(v.sem, v["xT0"])
            act.wait_ge(a.sem, a["xT1"])
            nc.scalar.copy(stat[:, 0, :], stat[:, 2, :]).then_inc(a.sem, a.step("xTn"))
            act.wait_ge(t.sem, t["o"])
            nc.scalar.copy(oT[:, :, :, :], po[:, 0:2 * P].rearrange("p (k r g) -> p k r g", k=KV, g=4)
                           ).then_inc(a.sem, a.step("oT"))
            act.wait_ge(loaded, 64)
            nc.scalar.activation(sz[:, :], bz[:, :], ACT.Sigmoid).then_inc(a.sem, a.step("sig"))


def sample_memory_phase(nc, c, d):
    with ExitStack() as ctx:
        sb = lambda name, shape, dt=F32: ctx.enter_context(nc.sbuf_tensor("sm_" + name, shape, dt))
        sem = phase_semaphores(nc, ctx, "sample_memory")
        ps = lambda name, shape: ctx.enter_context(nc.psum_tensor("sm_" + name, shape, F32))
        C = sb("C", [P, DB, AH, 2, P])
        qk = sb("qk", [P, 2, AH, SR])
        vr = sb("vr", [SR, AH, DV])
        oz = sb("oz", [SR, 2, D])
        sg = sb("sg", [SR, 2, D])
        na = sb("na", [SR, D])
        m0 = sb("m0", [AH, DB])
        m0r = sb("m0r", [SR, AH])
        nr = sb("nr", [SR, AH, P])
        n8 = sb("n8", [DB, AH, P])
        mt, bt, gt = (sb(n, [AH, SR]) for n in ("mt", "bt", "gt"))
        row = sb("row", [SR, 4, AH])
        am = sb("am", [SR, AH])
        ws, wi, em, wpr = (sb(n, [SR, AH]) for n in ("ws", "wi", "em", "wpr"))
        fut = sb("fut", [SR, DB, DT])
        last = sb("last", [SR, DB, DT])
        bm = sb("bm", [SR, DB])
        ones = sb("ones", [SR, P])
        one4 = sb("one4", [AH, DT])
        wpx = sb("wpx", [SR, DB, AH])
        wpb = sb("wpb", [P, DB, AH])
        wp8 = sb("wp8", [DB, AH])
        dm = sb("dm", [SR, AH, SR])
        sd = sb("sd", [SR, AH, SR])
        kq = sb("kq", [SR, 2, AH, P])
        kwz = sb("kwz", [SR, DB, AH, P])
        qz = sb("qz", [P, AH, DB, SR])
        cT = [sb(f"cT{p}", [P, 2, P]) for p in range(2)]
        inter = sb("inter", [SR, AH, DV])
        h = sb("h", [SR, AH, DV])
        ya = sb("ya", [SR, AH, DV])
        den = sb("den", [SR, 5, AH])
        prod = sb("prod", [SR, AH, P])
        pa = ps("pa", [P, 512])
        pc = [ps(f"pc{p}", [P, 512]) for p in range(2)]
        pi = ps("pi", [P, 2, 512])
        pn = ps("pn", [P, 2, 512])
        pr = ps("pr", [P, 512])
        loaded, c_loaded, stored = sem("loaded"), sem("c_loaded"), sem("stored")
        g = Steps(sem("pool_steps"), "qz0", "fut0", "fut1", "fut2", "ones", "so", "zn", "gz")
        v = Steps(sem("vector_steps"), "last", "bm", "m", "b", "g", "row", "gl", "wi0", "em0", "ws0", "wpr0",
                  "wpx", "wpb", "kwz", "qz", "sd", "qn", "qnr", "hh", "den0", "den1", "den2", "den3", "den4", "rden",
                  "decay", "n0", "n1", "rms", "rr", "ya")
        a = Steps(sem("scalar_steps"), "wi", "em", "ws", "wpr", "dm", "kw", "q", "inter", "sq", "rt", "sig")
        t = Steps(sem("tensor_steps"), "rows", "last", "dm", "kq", "wpb", "intra", "inter", "n8")
        c_turned, c_out, c_used = sem("memory_turned"), sem("memory_out"), sem("memory_used")
        upd_mm, upd_done = sem("update_mm"), sem("update_done")
        block = ctx.enter_context(nc.Block())

        @block.sync
        def _(sp):
            sp.dma_start(qk[:, :, :, :], d["qt"][0:8, :, SEQ:ROWS].rearrange("(a t) p s -> p a t s", a=2)).then_inc(loaded, 16)
            sp.dma_start(vr[:, :, :].rearrange("p h e -> p (h e)"), d["r"][SEQ:ROWS, 0:D]).then_inc(loaded, 16)
            sp.dma_start(oz[:, :, :].rearrange("p a e -> p (a e)"), d["r"][SEQ:ROWS, R_AO:R_AO + 2 * D]).then_inc(loaded, 16)
            sp.dma_start(na[:, :], d["norm_a"][0:1, :].to_broadcast([SR, D])).then_inc(loaded, 16)
            sp.dma_start(m0[:, :], d["state_m"][0].rearrange("b h -> h b")).then_inc(loaded, 16)
            sp.dma_start(n8[:, :, :].rearrange("p h e -> p (h e)"), d["state_n"][0].rearrange("b h e -> b (h e)")).then_inc(loaded, 16)
            for b in range(DB):
                rows = slice(DT * b, DT * b + DT)
                sp.dma_start(m0r[rows, :], d["state_m"][0, b:b + 1, :].to_broadcast([DT, AH])).then_inc(loaded, 16)
                sp.dma_start(nr[rows, :, :].rearrange("p h e -> p (h e)"),
                             d["state_n"][0, b:b + 1].rearrange("b h e -> b (h e)").to_broadcast([DT, AH * P])).then_inc(loaded, 16)
            for b in range(DB):
                sp.dma_start(C[:, b, :, :, :], d["state_C"][0, b].rearrange("h (x p) e -> p h x e", p=P)).then_inc(c_loaded, 16)
            sp.wait_ge(v.sem, v["b"])
            sp.dma_start(d["o_m_sample"][0].rearrange("b h -> h b"), mt[:, DT - 1:SR:DT]).then_inc(stored, 16)
            sp.wait_ge(v.sem, v["n1"])
            sp.dma_start(d["o_n_sample"][0].rearrange("b h e -> b (h e)"), n8[:, :, :].rearrange("p h e -> p (h e)")).then_inc(stored, 16)
            sp.wait_ge(v.sem, v["ya"])
            sp.dma_start(d["y"][SEQ:ROWS, 0:D], ya[:, :, :].rearrange("p h e -> p (h e)")).then_inc(stored, 16)
            sp.wait_ge(upd_done, 16)
            for b in range(DB):
                sp.dma_start(d["o_C_sample"][0, b].rearrange("h (x p) e -> p h x e", p=P), C[:, b, :, :, :]).then_inc(stored, 16)
            sp.wait_ge(stored, 16 * (3 + DB))

        N_LOADED = 16 * (6 + 2 * DB)

        @block.gpsimd
        def _(pool):
            nc.gpsimd.memset(qz[:, :, :, :], 0.0).then_inc(g.sem, g.step("qz0"))
            nc.gpsimd.memset(fut[:, :, :], 0.0).then_inc(g.sem, g.step("fut0"))
            pool.wait_ge(g.sem, g["fut0"])
            nc.gpsimd.affine_select(out=fut[:, :, :], in_=fut[:, :, :], compare_op=ALU.is_ge, fill=NEG, base=0,
                                    pattern=[[-DT, DB], [0, DT]], channel_multiplier=1).then_inc(g.sem, g.step("fut1"))
            pool.wait_ge(g.sem, g["fut1"])
            nc.gpsimd.affine_select(out=fut[:, :, :], in_=fut[:, :, :], compare_op=ALU.is_ge, fill=NEG, base=0,
                                    pattern=[[DT, DB], [1, DT]], channel_multiplier=-1).then_inc(g.sem, g.step("fut2"))
            nc.gpsimd.memset(ones[:, :], 1.0).then_inc(g.sem, g.step("ones"))
            pool.wait_ge(a.sem, a["sig"])
            nc.gpsimd.tensor_tensor(sg[:, 0, :], sg[:, 0, :], sg[:, 1, :], ALU.mult).then_inc(g.sem, g.step("so"))
            nc.gpsimd.tensor_tensor(oz[:, 1, :], oz[:, 1, :], na[:, :], ALU.mult).then_inc(g.sem, g.step("zn"))
            pool.wait_ge(g.sem, g["zn"])
            nc.gpsimd.tensor_tensor(sg[:, 1, :], sg[:, 0, :], oz[:, 1, :], ALU.mult).then_inc(g.sem, g.step("gz"))

        @block.vector
        def _(dve):
            def step(ins, name):
                ins.then_inc(v.sem, v.step(name))
                dve.wait_ge(v.sem, v[name])
            nc.vector.memset(one4[:, :], 1.0)
            id32 = c["ident"][0:SR, 0:SR].rearrange("p (b t) -> p b t", t=DT)
            step(nc.vector.tensor_copy(last[:, :, :], id32[:, :, DT - 1:DT].to_broadcast([SR, DB, DT])), "last")
            step(nc.vector.reduce_sum(bm[:, :], id32, AX_X), "bm")
            dve.wait_ge(loaded, N_LOADED)
            for b in range(DB):
                cols = slice(DT * b, DT * b + DT)
                ins = nc.vector.tensor_tensor_scan(mt[:, cols], c["lfs"][:, cols], c["gis"][:, cols], m0[:, b:b + 1],
                                                   ALU.add, ALU.max)
            step(ins, "m")
            for b in range(DB):
                cols = slice(DT * b, DT * b + DT)
                ins = nc.vector.tensor_tensor_scan(bt[:, cols], one4[:, :], c["lfs"][:, cols], 0.0, ALU.mult, ALU.add)
            step(ins, "b")
            step(nc.vector.tensor_tensor(gt[:, :], bt[:, :], mt[:, :], ALU.subtract), "g")
            dve.wait_ge(t.sem, t["rows"])
            step(nc.vector.tensor_copy(row[:, :, :], pa[0:SR, 0:16].rearrange("p (x h) -> p x h", x=4)), "row")
            i, b_, m, gg = (row[:, x, :] for x in range(4))
            step(nc.vector.tensor_tensor(am[:, :], i, b_, ALU.subtract), "gl")
            step(nc.vector.tensor_tensor(wi[:, :], gg, m0r[:, :], ALU.add), "wi0")
            step(nc.vector.tensor_scalar(em[:, :], m, -1.0, None, ALU.mult), "em0")
            dve.wait_ge(t.sem, t["last"])
            step(nc.vector.tensor_tensor(ws[:, :], am[:, :], pa[0:SR, 16:20], ALU.add), "ws0")
            step(nc.vector.tensor_tensor(wpr[:, :], m0r[:, :], pa[0:SR, 16:20], ALU.add), "wpr0")
            dve.wait_ge(a.sem, a["wpr"])
            step(nc.vector.tensor_tensor(wpx[:, :, :], wpr[:, :].unsqueeze(1).to_broadcast([SR, DB, AH]),
                                         last[:, :, 0:1].to_broadcast([SR, DB, AH]), ALU.mult), "wpx")
            dve.wait_ge(t.sem, t["wpb"])
            nc.vector.tensor_copy(wp8[:, :], pr[0:DB, 0:AH])
            step(nc.vector.tensor_copy(wpb[:, :, :], pr[:, 32:64].rearrange("p (b h) -> p b h", b=DB)), "wpb")
            dve.wait_ge(a.sem, a["kw"])
            for b in range(DB):
                ins = nc.vector.tensor_scalar(kwz[:, b, :, :], kq[:, 0, :, :], bm[:, b:b + 1], None, ALU.mult)
            step(ins, "kwz")
            dve.wait_ge(g.sem, g["qz0"])
            for b in range(DB):
                cols = slice(DT * b, DT * b + DT)
                ins = nc.vector.tensor_copy(qz[:, :, b, cols], qk[:, 0, :, cols])
            step(ins, "qz")
            dve.wait_ge(a.sem, a["dm"])
            step(nc.vector.tensor_tensor(sd[:, :, :], pa[0:SR, 256:384].rearrange("p (h s) -> p h s", h=AH), dm[:, :, :],
                                         ALU.mult), "sd")
            dve.wait_ge(a.sem, a["q"])
            step(nc.vector.tensor_tensor(prod[:, :, :], kq[:, 1, :, :], nr[:, :, :], ALU.mult), "qn")
            step(nc.vector.reduce_sum(den[:, 0, :], prod[:, :, :], AX_X), "qnr")
            dve.wait_ge(t.sem, t["intra"])
            dve.wait_ge(a.sem, a["inter"])
            step(nc.vector.tensor_tensor(h[:, :, :], inter[:, :, :], pn[0:SR, :, :].rearrange("p a (h e) -> p (a h) e", h=2),
                                         ALU.add), "hh")
            step(nc.vector.tensor_tensor(den[:, 0, :], den[:, 0, :], wi[:, :], ALU.mult), "den0")
            step(nc.vector.tensor_tensor(den[:, 0, :], pa[0:SR, 384:388], den[:, 0, :], ALU.add), "den1")
            step(nc.vector.scalar_tensor_tensor(den[:, 1, :], den[:, 0, :], -1.0, den[:, 0, :], ALU.mult, ALU.max), "den2")
            step(nc.vector.tensor_tensor(den[:, 1, :], den[:, 1, :], em[:, :], ALU.max), "den3")
            step(nc.vector.reciprocal(den[:, 2, :], den[:, 1, :]), "den4")
            step(nc.vector.tensor_copy(den[:, 4, :], den[:, 2, :]), "rden")
            dve.wait_ge(c_used, AH * DB)
            step(nc.vector.tensor_tensor(C[:, :, :, :, :].rearrange("p b h x e -> p (b h) (x e)"),
                                         C[:, :, :, :, :].rearrange("p b h x e -> p (b h) (x e)"),
                                         wpb[:, :, :].rearrange("p b h -> p (b h)").unsqueeze(2).to_broadcast([P, DB * AH, 2 * P]),
                                         ALU.mult), "decay")
            step(nc.vector.tensor_tensor(n8[:, :, :], n8[:, :, :], wp8[:, :].unsqueeze(2).to_broadcast([DB, AH, P]), ALU.mult), "n0")
            dve.wait_ge(t.sem, t["n8"])
            step(nc.vector.tensor_tensor(n8[:, :, :], n8[:, :, :], pr[0:DB, :].rearrange("p (h e) -> p h e", h=AH), ALU.add), "n1")
            dve.wait_ge(a.sem, a["rt"])
            step(nc.vector.reciprocal(den[:, 0, :], den[:, 1, :]), "rms")
            step(nc.vector.tensor_tensor(den[:, 0, :], den[:, 0, :], den[:, 2, :], ALU.mult), "rr")
            dve.wait_ge(g.sem, g["gz"])
            for hh in range(AH):
                ins = nc.vector.scalar_tensor_tensor(ya[:, hh, :], h[:, hh, :], den[:, 0, hh:hh + 1],
                                                     sg[:, 1, hh * DV:(hh + 1) * DV], ALU.mult, ALU.mult)
            step(ins, "ya")
            for n in range(16):
                hh, x, half = n // 4, n // 2 % 2, n % 2
                dve.wait_ge(upd_mm, n + 1)
                nc.vector.tensor_tensor(C[:, 4 * half:4 * half + 4, hh, x, :], C[:, 4 * half:4 * half + 4, hh, x, :],
                                        pc[n % 2][:, :].rearrange("p (b e) -> p b e", b=4), ALU.add).then_inc(upd_done, 1)

        @block.scalar
        def _(act):
            def step(ins, name):
                ins.then_inc(a.sem, a.step(name))
            for name, x, after in (("wi", wi, "wi0"), ("em", em, "em0"), ("ws", ws, "ws0"), ("wpr", wpr, "wpr0")):
                act.wait_ge(v.sem, v[after])
                step(nc.scalar.activation(x[:, :], x[:, :], ACT.Exp), name)
            act.wait_ge(t.sem, t["dm"])
            for hh in range(AH):
                ins = nc.scalar.activation(dm[:, hh, :], pa[0:SR, 128 + hh * SR:128 + (hh + 1) * SR], ACT.Exp, bias=am[:, hh:hh + 1])
            step(ins, "dm")
            act.wait_ge(t.sem, t["kq"])
            act.wait_ge(a.sem, a["ws"])
            for hh in range(AH):
                ins = nc.scalar.activation(kq[:, 0, hh, :], pn[0:SR, 0, hh * P:(hh + 1) * P], ACT.Copy, scale=ws[:, hh:hh + 1])
            step(ins, "kw")
            step(nc.scalar.copy(kq[:, 1, :, :], pn[0:SR, 1, :].rearrange("p (h e) -> p h e", h=AH)), "q")
            for n in range(AH * DB):
                act.wait_ge(c_turned, n + 1)
                if n >= 2:
                    act.wait_ge(c_used, n - 1)
                nc.scalar.copy(cT[n % 2][:, :, :], pc[n % 2][:, 0:2 * P].rearrange("p (x e) -> p x e", x=2)).then_inc(c_out, 1)
            act.wait_ge(t.sem, t["inter"])
            for hh in range(AH):
                ins = nc.scalar.activation(inter[:, hh, :], pi[0:SR, hh // 2, (hh % 2) * DV:(hh % 2 + 1) * DV], ACT.Copy,
                                           scale=wi[:, hh:hh + 1])
            step(ins, "inter")
            act.wait_ge(v.sem, v["rden"])
            for hh in range(AH):
                ins = nc.scalar.activation(inter[:, hh, :], h[:, hh, :], ACT.Square, scale=den[:, 2, hh:hh + 1],
                                           accum_out=den[:, 3, hh:hh + 1])
            step(ins, "sq")
            act.wait_ge(a.sem, a["sq"])
            step(nc.scalar.activation(den[:, 1, :], den[:, 3, :], ACT.Sqrt, scale=1.0 / DV, bias=c["eps"][0:SR, 0:1]), "rt")
            act.wait_ge(loaded, N_LOADED)
            step(nc.scalar.activation(sg[:, :, :], oz[:, :, :], ACT.Sigmoid), "sig")

        @block.tensor
        def _(pe):
            pe.wait_ge(v.sem, v["g"])
            for x, src in enumerate((c["gis"], bt, mt, gt)):
                ins = nc.tensor.transpose(pa[0:SR, 4 * x:4 * x + 4], src[:, :], c["ident"][0:4, 0:4])
            ins.then_inc(t.sem, t.step("rows"))
            pe.wait_ge(v.sem, v["row"])
            nc.tensor.matmul(pa[0:SR, 16:20], last[:, :, :].rearrange("p b t -> p (b t)"), row[:, 3, :],
                             start=True, stop=True).then_inc(t.sem, t.step("last"))
            pe.wait_ge(g.sem, g["ones"])
            pe.wait_ge(v.sem, v["wpr0"])
            for hh in range(AH):
                o = pa[0:SR, 128 + hh * SR:128 + (hh + 1) * SR]
                nc.tensor.matmul(o, c["sel"][:, hh, 0:SR], gt[:, :], start=True, stop=False)
                nc.tensor.matmul(o, c["ident"][0:SR, 0:SR], fut[:, :, :].rearrange("p b t -> p (b t)"), start=False, stop=True)
            for hh in range(AH):
                ins = nc.tensor.matmul(pa[0:SR, 256 + hh * SR:256 + (hh + 1) * SR], qk[:, 1, hh, :], qk[:, 0, hh, :],
                                       start=True, stop=True)
            ins.then_inc(t.sem, t.step("dm"))
            for x in range(2):
                for hh in range(AH):
                    ins = nc.tensor.transpose(pn[0:SR, x, hh * P:(hh + 1) * P], qk[:, 1 - x, hh, :], c["ident"][:, :])
            ins.then_inc(t.sem, t.step("kq"))
            pe.wait_ge(v.sem, v["wpx"])
            nc.tensor.matmul(pr[:, 32:64], ones[:, :], wpx[:, :, :].rearrange("p b h -> p (b h)"), start=True, stop=True)
            nc.tensor.matmul(pr[0:DB, 0:AH], last[:, :, 0], wpr[:, :], start=True, stop=True).then_inc(t.sem, t.step("wpb"))
            pe.wait_ge(v.sem, v["sd"])
            pe.wait_ge(a.sem, a["q"])
            for hh in range(AH):
                nc.tensor.matmul(pn[0:SR, hh // 2, (hh % 2) * DV:(hh % 2 + 1) * DV], sd[:, hh, :], vr[:, hh, :], start=True, stop=True)
                ins = nc.tensor.matmul(pa[0:SR, 384 + hh:385 + hh], sd[:, hh, :], ones[:, 0:1], start=True, stop=True)
            ins.then_inc(t.sem, t.step("intra"))
            for n in range(AH * DB):
                hh, b = n // DB, n % DB
                if hh == 0:
                    pe.wait_ge(c_loaded, 16 * DB)
                if n >= 2:
                    pe.wait_ge(c_out, n - 1)
                for x in range(2):
                    ins = nc.tensor.transpose(pc[n % 2][:, x * P:(x + 1) * P], C[:, b, hh, x, :], c["ident"][:, :])
                ins.then_inc(c_turned, 1)
                pe.wait_ge(c_out, n + 1)
                pe.wait_ge(v.sem, v["qz"])
                nc.tensor.matmul(pi[0:SR, hh // 2, (hh % 2) * DV:(hh % 2 + 1) * DV], qz[:, hh, b, :],
                                 cT[n % 2][:, :, :].rearrange("p x e -> p (x e)"),
                                 start=b == 0, stop=b == DB - 1).then_inc(c_used, 1)
            nc.tensor.matmul(pr[0:DB, 0:8], bm[:, :], ones[:, 0:8], start=True, stop=True).then_inc(t.sem, t.step("inter"))
            pe.wait_ge(v.sem, v["n0"])
            nc.tensor.matmul(pr[0:DB, :], bm[:, :], kq[:, 0, :, :].rearrange("p h e -> p (h e)"), start=True, stop=True
                             ).then_inc(t.sem, t.step("n8"))
            for n in range(16):
                hh, x, half = n // 4, n // 2 % 2, n % 2
                if n >= 2:
                    pe.wait_ge(upd_done, n - 1)
                nc.tensor.matmul(pc[n % 2][:, :], vr[:, hh, x * P:(x + 1) * P], kwz[:, 4 * half:4 * half + 4, hh, :],
                                 start=True, stop=True).then_inc(upd_mm, 1)


def output_phase(nc, c, d):
    with ExitStack() as ctx:
        sb = lambda name, shape, dt=F32: ctx.enter_context(nc.sbuf_tensor("out_" + name, shape, dt))
        sem = phase_semaphores(nc, ctx, "output")
        wa, wb, wo, wg = (sb(n, [P, KT, D]) for n in ("wa", "wb", "wo", "wg"))
        wp = sb("wp", [P, PLE // P, D])
        npost = sb("npost", [P, D])
        y = sb("y", [P, 2, KT, P])
        g = sb("g", [P, 2, D])
        x = [sb(f"x{p}", [P, D]) for p in range(2)]
        pe_in = [sb(f"pe{p}", [P, PLE]) for p in range(2)]
        yT = sb("yT", [P, 2, KT, P])
        mT = sb("mT", [P, KT, P])
        xT = sb("xT", [P, KT, P])
        peT = sb("peT", [P, 2, P])
        merged = sb("merged", [P, D])
        tmp = sb("tmp", [P, D])
        sg2 = sb("sg2", [P, D])
        st = sb("st", [P, 4])
        U = [ctx.enter_context(nc.psum_tensor(f"out_u{j}", [P, 2, 512], F32)) for j in range(4)]
        y_loaded, g_loaded = sem("y_loaded"), sem("g_loaded")
        x_loaded, x_stored = [sem(f"x_loaded{p}") for p in range(2)], [sem(f"x_stored{p}") for p in range(2)]
        w_loaded = {n: sem(f"{n}_loaded") for n in ("wa", "wb", "wo", "wg", "wp", "npost")}
        filled, out_a, out_v = sem("filled"), sem("out_a"), sem("out_v")
        ab_mm, out_mm, gate_mm, ple_mm = sem("ab_mm"), sem("out_mm"), sem("gate_mm"), sem("ple_mm")
        g_ready, sq_ready, rms_ready, sg2_ready = sem("g_ready"), sem("sq_ready"), sem("rms_ready"), sem("sg2_ready")
        merge_step, merged_ready, norm_step, x1_ready, y_ready = (
            sem(n) for n in ("merge_step", "merged_ready", "norm_step", "x1_ready", "y_ready"))
        FILLS = 5

        def before(n):
            return FILLS * n + 2

        def steps(eng, body):
            for p in range(2):
                body(0, p, P, P, False)
            with eng.Fori(1, NB // 2 - 1) as j:
                for p in range(2):
                    body(j, p, P, P, True)
            body(NB // 2 - 1, 0, P, P, True)
            body(NB // 2 - 1, 1, P, SR, True)
            body(NB // 2, 0, SR, 0, True)

        block = ctx.enter_context(nc.Block())

        @block.sync
        def _(sp):
            def load_y(n, rows):
                src = d["y"][SEQ:ROWS, :] if rows == SR else d["y"][0:SEQ, :].rearrange("(n q) m -> n q m", q=P)[n]
                sp.dma_start(y[0:rows, :, :, :].rearrange("p a k q -> p (a k q)"), src).then_inc(y_loaded, 16)

            def load_g(n, rows):
                src = d["r"][SEQ:ROWS, R_GA:R_GA + 2 * D] if rows == SR else \
                    d["r"][0:SEQ, R_GA:R_GA + 2 * D].rearrange("(n q) m -> n q m", q=P)[n]
                sp.dma_start(g[0:rows, :, :].rearrange("p a k -> p (a k)"), src).then_inc(g_loaded, 16)

            def load_x(n, p, rows):
                xs = d["x_sample"].rearrange("b t c -> (b t) c") if rows == SR else \
                    d["x_prompt"].rearrange("a (n q) c -> (a n) q c", q=P)[n]
                ps = d["p_sample"].rearrange("a b t c -> (a b t) c") if rows == SR else \
                    d["p_prompt"].rearrange("a e (n q) c -> (a e n) q c", q=P)[n]
                sp.dma_start(x[p][0:rows, :], xs).then_inc(x_loaded[p], 16)
                sp.dma_start(pe_in[p][0:rows, :], ps).then_inc(x_loaded[p], 16)

            load_y(0, P)
            for dst, name, key in ((wa, "w_a_proj", "wa"), (wb, "w_b_proj", "wb")):
                sp.dma_start(dst[:, :, :], d[name].rearrange("a (k p) n -> (a p) k n", p=P)).then_inc(w_loaded[key], 16)
            load_g(0, P)
            sp.dma_start(wo[:, :, :], d["w_out"].rearrange("a (k p) n -> (a p) k n", p=P)).then_inc(w_loaded["wo"], 16)
            load_x(0, 0, P)
            sp.dma_start(npost[:, :], d["norm_post"][0:1, :].to_broadcast([P, D])).then_inc(w_loaded["npost"], 16)
            sp.dma_start(wg[:, :, :], d["w_ple_gate"].rearrange("a (k p) n -> (a p) k n", p=P)).then_inc(w_loaded["wg"], 16)
            sp.dma_start(wp[:, :, :], d["w_ple"].rearrange("a (k p) n -> (a p) k n", p=P)).then_inc(w_loaded["wp"], 16)
            load_x(1, 1, P)

            def step(j, p, rows, nxt, warm):
                n = 2 * j + p
                if nxt:
                    sp.wait_ge(filled, before(n))
                    load_y(n + 1, nxt)
                    sp.wait_ge(merged_ready, n + 1)
                    load_g(n + 1, nxt)
                if warm or p:
                    q = 1 - p
                    if nxt:
                        sp.wait_ge(x_stored[q], 16 * (j + p))
                        load_x(n + 1, q, nxt)
            steps(sp, step)
            for p in range(2):
                sp.wait_ge(x_stored[p], 16 * (NB // 2 + 1 - p))

        @block.gpsimd
        def _(pool):
            def store(j, p, rows, nxt, warm):
                n = 2 * j + p
                pool.wait_ge(y_ready, n + 1)
                dst = d["y_sample"].rearrange("b t c -> (b t) c") if rows == SR else \
                    d["y_prompt"].rearrange("a (n q) c -> (a n) q c", q=P)[n]
                pool.dma_start(dst, x[p][0:rows, :]).then_inc(x_stored[p], 16)
            steps(pool, store)

        @block.tensor
        def _(pe):
            def free(a, v):
                pe.wait_ge(out_a, a)
                pe.wait_ge(out_v, v)

            def transposes(src, rows, n=KT):
                for k in range(n):
                    ins = nc.tensor.transpose(U[3][:, k // 4, (k % 4) * P:(k % 4) * P + rows], src(k),
                                              c["ident"][0:rows, 0:rows])
                ins.then_inc(filled, 1)

            def product(dst, lhs, w, rows, halves=(0, 1), kt=KT):
                for h in halves:
                    for k in range(kt):
                        ins = nc.tensor.matmul(dst[0:rows, h, :], lhs(k), w[:, k, h * 512:(h + 1) * 512],
                                               start=k == 0, stop=k == kt - 1)
                return ins

            def branches(n, rows):
                pe.wait_ge(w_loaded["wa"], 16)
                product(U[0], lambda k: yT[:, 0, k, 0:rows], wa, rows)
                pe.wait_ge(w_loaded["wb"], 16)
                product(U[1], lambda k: yT[:, 1, k, 0:rows], wb, rows).then_inc(ab_mm, 1)

            pe.wait_ge(y_loaded, 16)
            transposes(lambda k: y[:, 0, k, :], P)
            free(1, 1)
            transposes(lambda k: y[:, 1, k, :], P)
            free(2, 2)
            branches(0, P)

            def step(j, p, rows, nxt, warm):
                n = 2 * j + p
                cnt = before(n)
                pe.wait_ge(merged_ready, n + 1)
                free(cnt, cnt)
                transposes(lambda k: merged[0:rows, k * P:(k + 1) * P], rows)
                free(cnt + 1, cnt + 1)
                pe.wait_ge(w_loaded["wo"], 16)
                if warm or p:
                    pe.wait_ge(sg2_ready, n)
                if nxt:
                    pe.wait_ge(y_loaded, 16 * (n + 2))
                    transposes(lambda k: y[0:nxt, 0, k, :], nxt)
                product(U[2], lambda k: mT[:, k, 0:rows], wo, rows, (0,))
                if nxt:
                    free(cnt + 2, cnt + 2)
                    transposes(lambda k: y[0:nxt, 1, k, :], nxt)
                product(U[2], lambda k: mT[:, k, 0:rows], wo, rows, (1,)).then_inc(out_mm, 1)
                cnt = cnt + 3 if nxt else cnt + 1
                if nxt:
                    free(cnt, cnt)
                    branches(n + 1, nxt)
                pe.wait_ge(x1_ready, n + 1)
                transposes(lambda k: x[p][0:rows, k * P:(k + 1) * P], rows)
                free(cnt + 1, cnt + 1)
                pe.wait_ge(x_loaded[p], 32 * (j + 1))
                transposes(lambda k: pe_in[p][0:rows, k * P:(k + 1) * P], rows, 2)
                pe.wait_ge(w_loaded["wg"], 16)
                product(U[2], lambda k: xT[:, k, 0:rows], wg, rows).then_inc(gate_mm, 1)
                free(cnt + 2, cnt + 1)
                pe.wait_ge(w_loaded["wp"], 16)
                product(U[3], lambda k: peT[:, k, 0:rows], wp, rows, kt=2).then_inc(ple_mm, 1)
            steps(pe, step)

        def copy_half(eng, copy, dst, half, rows, cnt, done):
            eng.wait_ge(filled, cnt + 1)
            copy(dst[:, 4 * half:4 * half + 4, 0:rows],
                 U[3][:, half, :].rearrange("p (k q) -> p k q", k=4)[:, :, 0:rows]).then_inc(done, 1)

        @block.scalar
        def _(act):
            copy = nc.scalar.copy
            copy_half(act, copy, yT[:, 0], 0, P, 0, out_a)
            copy_half(act, copy, yT[:, 1], 0, P, 1, out_a)

            def gate(n, rows):
                act.wait_ge(g_loaded, 16 * (n + 1))
                nc.scalar.activation(g[0:rows, :, :], g[0:rows, :, :], ACT.Sigmoid).then_inc(g_ready, 1)
            gate(0, P)

            def step(j, p, rows, nxt, warm):
                n = 2 * j + p
                cnt = before(n)
                if warm or p:
                    act.wait_ge(out_mm, n)
                copy_half(act, copy, mT, 0, rows, cnt, out_a)
                cnt = cnt + 1
                if nxt:
                    act.wait_ge(ab_mm, n + 1)
                    copy_half(act, copy, yT[:, 0], 0, nxt, cnt, out_a)
                    copy_half(act, copy, yT[:, 1], 0, nxt, cnt + 1, out_a)
                    cnt = cnt + 2
                act.wait_ge(out_mm, n + 1)
                if warm or p:
                    act.wait_ge(y_ready, n)
                    act.wait_ge(norm_step, 2 * n)
                nc.scalar.activation(sg2[0:rows, :], U[2][0:rows, :, :].rearrange("p a b -> p (a b)"), ACT.Square,
                                     accum_out=st[0:rows, 0:1]).then_inc(sq_ready, 1)
                act.wait_ge(sq_ready, n + 1)
                nc.scalar.activation(st[0:rows, 1:2], st[0:rows, 0:1], ACT.Sqrt, scale=1.0 / D,
                                     bias=c["eps"][0:rows, 0:1]).then_inc(rms_ready, 1)
                if nxt:
                    gate(n + 1, nxt)
                if warm or p:
                    act.wait_ge(gate_mm, n)
                copy_half(act, copy, xT, 0, rows, cnt, out_a)
                if warm or p:
                    act.wait_ge(ple_mm, n)
                act.wait_ge(filled, cnt + 2)
                copy(peT[:, :, 0:rows], U[3][:, 0, 0:2 * P].rearrange("p (k q) -> p k q", k=2)[:, :, 0:rows]).then_inc(out_a, 1)
                act.wait_ge(gate_mm, n + 1)
                nc.scalar.activation(sg2[0:rows, :], U[2][0:rows, :, :].rearrange("p a b -> p (a b)"), ACT.Sigmoid
                                     ).then_inc(sg2_ready, 1)
            steps(act, step)

        @block.vector
        def _(dve):
            copy = nc.vector.tensor_copy
            flat = lambda u, rows: u[0:rows, :, :].rearrange("p a b -> p (a b)")
            copy_half(dve, copy, yT[:, 0], 1, P, 0, out_v)
            copy_half(dve, copy, yT[:, 1], 1, P, 1, out_v)

            def merge(n, rows, first=False):
                dve.wait_ge(ab_mm, n + 1)
                dve.wait_ge(g_ready, n + 1)
                if not first:
                    dve.wait_ge(filled, before(n - 1) + 1)
                nc.vector.tensor_tensor(merged[0:rows, :], flat(U[0], rows), g[0:rows, 0, :], ALU.mult).then_inc(merge_step, 1)
                nc.vector.tensor_tensor(tmp[0:rows, :], flat(U[1], rows), g[0:rows, 1, :], ALU.mult).then_inc(merge_step, 1)
                dve.wait_ge(merge_step, 2 * (n + 1))
                nc.vector.tensor_tensor(merged[0:rows, :], merged[0:rows, :], tmp[0:rows, :], ALU.add).then_inc(merged_ready, 1)
            merge(0, P, True)
            dve.wait_ge(w_loaded["npost"], 16)

            def step(j, p, rows, nxt, warm):
                n = 2 * j + p
                cnt = before(n)
                if warm or p:
                    dve.wait_ge(out_mm, n)
                copy_half(dve, copy, mT, 1, rows, cnt, out_v)
                cnt = cnt + 1
                if nxt:
                    dve.wait_ge(ab_mm, n + 1)
                    copy_half(dve, copy, yT[:, 0], 1, nxt, cnt, out_v)
                    copy_half(dve, copy, yT[:, 1], 1, nxt, cnt + 1, out_v)
                    cnt = cnt + 2
                dve.wait_ge(rms_ready, n + 1)
                dve.wait_ge(merged_ready, n + 1)
                nc.vector.reciprocal(st[0:rows, 2:3], st[0:rows, 1:2]).then_inc(norm_step, 1)
                dve.wait_ge(norm_step, 2 * n + 1)
                nc.vector.scalar_tensor_tensor(tmp[0:rows, :], flat(U[2], rows), st[0:rows, 2:3], npost[0:rows, :],
                                               ALU.mult, ALU.mult).then_inc(norm_step, 1)
                dve.wait_ge(x_loaded[p], 32 * (j + 1))
                dve.wait_ge(norm_step, 2 * n + 2)
                nc.vector.tensor_tensor(x[p][0:rows, :], x[p][0:rows, :], tmp[0:rows, :], ALU.add).then_inc(x1_ready, 1)
                if warm or p:
                    dve.wait_ge(gate_mm, n)
                copy_half(dve, copy, xT, 1, rows, cnt, out_v)
                if nxt:
                    merge(n + 1, nxt)
                dve.wait_ge(sg2_ready, n + 1)
                dve.wait_ge(ple_mm, n + 1)
                nc.vector.tensor_tensor(sg2[0:rows, :], flat(U[3], rows), sg2[0:rows, :], ALU.mult).then_inc(out_v, 1)
                dve.wait_ge(out_v, cnt + 2)
                dve.wait_ge(filled, cnt + 1)
                nc.vector.tensor_tensor(x[p][0:rows, :], x[p][0:rows, :], sg2[0:rows, :], ALU.add).then_inc(y_ready, 1)
            steps(dve, step)


def allocate(nc, d):
    t = lambda name, shape, dt=F32: nc.dram_tensor(name, shape, dt, kind="Internal").ap()
    d["qt"] = t("qt_scr", (T_ALL, P, ROWS))
    d["r"] = t("r_scr", (ROWS, RCOLS))
    d["y"] = t("y_scr", (ROWS, 2 * D))
    d["gates"] = t("gates_scr", (8, ROWS))
    d["mask"] = t("mask_scr", (NB, P, SEQ), BF16)
    d["ik_scr"] = t("ik_scr", (ID, SR))
    d["iwc_scr"] = t("iwc_scr", (2, IH, DT, GATHERS))
    d["ss_scr"] = t("ss_scr", (4, SR, SEG))
    d["iw_scr"] = t("iw_scr", (SR, IH))


def program(nc, d):
    allocate(nc, d)
    with ExitStack() as top:
        top.enter_context(nc.allow_non_contiguous_dma(reason="a few small vectors are loaded by column"))
        c = {}
        def sb(name, shape, dt=F32):
            c[name] = top.enter_context(nc.sbuf_tensor(name, shape, dt))
        sb("ident", [P, P])
        sb("eps", [P, 1])
        with ExitStack() as proj:
            def sbp(name, shape, dt=F32):
                c[name] = proj.enter_context(nc.sbuf_tensor(name, shape, dt))
            sbp("ikT", [P, ROWS])
            sbp("sm", [P, NT, 72])
            sbp("us", [P, KT, DB, 7])
            sbp("xnT", [P, KT, ROWS])
            norm_phase(nc, c, d, None)
            transposed_projection_phase(nc, c, d, None)
            row_projection_and_topk_phase(nc, c, d)
        mixing = top.enter_context(ExitStack())

        def sbm(name, shape, dt=F32):
            c[name] = mixing.enter_context(nc.sbuf_tensor(name, shape, dt))
        sbm("sel", [4, 4, P])
        sbm("future", [P, P])
        sbm("lfs", [4, SR])
        sbm("gis", [4, SR])
        sbm("g", [4, SEQ])
        for name in ("a", "ws", "wp", "wi", "em"):
            sbm(name, [P, NB, 4])
        gate_phase(nc, c, d)
        prompt_mixing_phase(nc, c, d)
        sbm("rowid", [P, 2, SR], U32)
        sbm("sbias", [P, TOPK + SR])
        sample_index_phase(nc, c, d)
        sample_select_phase(nc, c, d)
        sample_attention_phase(nc, c, d)
        sample_memory_phase(nc, c, d)
        mixing.close()
        output_phase(nc, c, d)


INS = ["x_prompt", "x_sample", "cache_k", "cache_v", "cache_idx_k", "page_table", "state_C", "state_n", "state_m",
       "state_conv", "p_prompt", "p_sample", "w_in", "conv_w", "conv_b", "if_bias", "norm_a", "w_a_proj",
       "w_b_proj", "w_out", "norm_pre", "norm_post", "w_ple", "w_ple_gate"]
OUTS = [("y_prompt", (1, SEQ, D)), ("y_sample", (DB, DT, D)),
        ("o_k_prompt", (1, 1, SEQ, KV, HD)), ("o_v_prompt", (1, 1, SEQ, KV, HD)), ("o_ik_prompt", (1, 1, SEQ, ID)),
        ("o_C_prompt", (1, 1, AH, DV, DQK)), ("o_n_prompt", (1, 1, AH, DQK)), ("o_m_prompt", (1, 1, AH)),
        ("o_conv_prompt", (1, 1, 3, D)),
        ("o_k_sample", (1, DB, DT, KV, HD)), ("o_v_sample", (1, DB, DT, KV, HD)), ("o_ik_sample", (1, DB, DT, ID)),
        ("o_C_sample", (1, DB, AH, DV, DQK)), ("o_n_sample", (1, DB, AH, DQK)), ("o_m_sample", (1, DB, AH)),
        ("o_conv_sample", (1, DB, 3, D))]


def kernel(**inputs):
    import numpy as _np
    import concourse.bacc as _bacc
    from concourse import mybir as _mybir
    from concourse.bass_utils import run_bass_kernel_spmd as _run

    nc = _bacc.Bacc("TRN2", target_bir_lowering=False, num_devices=1)
    arrays, d = {}, {}
    for name in INS:
        a = _np.ascontiguousarray(inputs[name])
        arrays[f"in_{name}"] = a
        d[name] = nc.dram_tensor(f"in_{name}", a.shape, _mybir.dt.from_np(a.dtype), kind="ExternalInput").ap()
    for name, shape in OUTS:
        d[name] = nc.dram_tensor(f"out_{name}", shape, F32, kind="ExternalOutput").ap()
    program(nc, d)
    r = _run(nc, [arrays], core_ids=[0])
    return tuple(r.results[0][f"out_{name}"] for name, _ in OUTS)
```

```python
from contextlib import ExitStack

import concourse.bass as bass
from concourse import mybir

F32 = mybir.dt.float32
BF16 = mybir.dt.bfloat16
I32 = mybir.dt.int32
U32 = mybir.dt.uint32
ALU = mybir.AluOpType
ACT = mybir.ActivationFunctionType
AX_X = mybir.AxisListType.X

P = 128
D = 1024
KT = D // P
SEQ = 2048
NB = SEQ // P
DB, DT = 8, 4
SR = DB * DT
ROWS = SEQ + SR
NT = NB + 1
G = 5
GW = ROWS // G
EPS = 1e-6
AH, DQK, DV = 4, 128, 256
BH, KV, HD = 8, 2, 128
IH, ID = 8, 64
TOPK = 256
PAST = 8192
PAGE = 128
PAGES = PAST // PAGE
POOL = 640
PLE = 256
NEG = -1e30
TAKEN = -3.0e38
HIDDEN = -3.2e38

C_AV, C_AI, C_AO, C_AZ = 1024, 2048, 2056, 3080
C_BQ, C_BK, C_IQ, C_IK = 4104, 5128, 5640, 6152
C_BZ, C_GA = 6224, 7248
COLS = 9296
CH = 512
ROW_CHUNKS = [C_AV, C_AV + CH, C_AO, C_AO + CH, C_AZ, C_AZ + CH, C_BK,
              C_BZ, C_BZ + CH, C_GA, C_GA + CH, C_GA + 2 * CH, C_GA + 3 * CH]
R_AV, R_AO, R_AZ, R_BKV, R_BZ, R_GA = 0, 1024, 2048, 3072, 3584, 4608
RCOLS = CH * len(ROW_CHUNKS)
T_CONV, T_BQ, T_BK, T_IQ, T_ALL = 0, 8, 16, 18, 22


def tile_rows(n):
    return SR if isinstance(n, int) and n == NB else P


def phase_semaphores(nc, ctx, phase):
    taken = []

    def free():
        nc.clear_and_free_semaphores(taken)
        nc.all_engine_barrier()
    ctx.callback(free)

    def sem(name):
        taken.append(nc.alloc_semaphore(f"{phase}_{name}"))
        return taken[-1]
    return sem


def norm_phase(nc, c, d, s):
    with ExitStack() as ctx:
        sb = lambda name, shape, dt=F32: ctx.enter_context(nc.sbuf_tensor(name, shape, dt))
        sem = phase_semaphores(nc, ctx, "norm")
        xt = [sb(f"xt{p}", [P, D]) for p in range(2)]
        xs = [sb(f"xs{p}", [P, D]) for p in range(2)]
        junk = sb("junk", [P, D])
        ss = sb("ss", [P, 2])
        rt = sb("rt", [P, 2])
        rstd = sb("rstd", [P, 2])
        gcol = sb("gcol", [P, KT])
        sconv = sb("sconv", [24, D])
        xps = [ctx.enter_context(nc.psum_tensor(f"xps{p}", [P, 2, 4, P], F32)) for p in range(2)]
        cps = ctx.enter_context(nc.psum_tensor("cps", [P, KT, 24], F32))
        x_loaded = [sem(f"x_loaded{p}") for p in range(2)]
        small_loaded = sem("small_loaded")
        squared, rooted, rstd_ready, scaled = sem("squared"), sem("rooted"), sem("rstd_ready"), sem("scaled")
        transposed, evac_a, evac_v = sem("transposed"), sem("evac_a"), sem("evac_v")
        conv_t = sem("conv_t")
        halo = sem("halo")

        def pairs(eng, body):
            for p in range(2):
                body(0, p, P, False)
            with eng.Fori(1, NB // 2) as j:
                for p in range(2):
                    body(j, p, P, True)
            body(NB // 2, 0, SR, True)

        block = ctx.enter_context(nc.Block())

        @block.sync
        def _(sp):
            sp.dma_start(gcol[:, :], d["norm_pre"].rearrange("a (t p) -> (a p) t", p=P)).then_inc(small_loaded, 16)
            sp.dma_start(sconv[:, :], d["state_conv"].rearrange("a b j c -> (a b j) c")).then_inc(small_loaded, 16)

            def load(j, p, rows, warm):
                if warm:
                    sp.wait_ge(scaled, 2 * j + p - 1)
                src = d["x_sample"].rearrange("b t c -> (b t) c") if rows == SR else \
                    d["x_prompt"].rearrange("a (n q) c -> (a n) q c", q=P)[2 * j + p]
                sp.dma_start(xt[p][0:rows, :], src).then_inc(x_loaded[p], 16)
            pairs(sp, load)

        @block.scalar
        def _(act):
            def tile(j, p, rows, warm):
                n = 2 * j + p
                act.wait_ge(x_loaded[p], 16 * (j + 1))
                if warm:
                    act.wait_ge(rstd_ready, n - 1)
                nc.scalar.activation(junk[0:rows, :], xt[p][0:rows, :], ACT.Square,
                                     accum_out=ss[0:rows, p:p + 1]).then_inc(squared, 1)
                act.wait_ge(squared, n + 1)
                nc.scalar.activation(rt[0:rows, p:p + 1], ss[0:rows, p:p + 1], ACT.Sqrt, scale=1.0 / D,
                                     bias=c["eps"][0:rows, 0:1]).then_inc(rooted, 1)
                act.wait_ge(transposed, n + 1)
                for k in range(KT // 2):
                    nc.scalar.activation(c["xnT"][:, k, bass.ds(n * P, rows)], xps[p][:, k // 4, k % 4, 0:rows],
                                         ACT.Copy, scale=gcol[:, k:k + 1]).then_inc(evac_a, 1)
            act.wait_ge(small_loaded, 32)
            pairs(act, tile)

        @block.vector
        def _(dve):
            dve.wait_ge(small_loaded, 32)
            dve.wait_ge(conv_t, 1)
            nc.vector.tensor_copy(c["us"][:, :, :, 0:3],
                                  cps[:, :, :].rearrange("p t (b j) -> p t b j", j=3)).then_inc(halo, 1)

            def tile(j, p, rows, warm):
                n = 2 * j + p
                dve.wait_ge(rooted, n + 1)
                if warm:
                    dve.wait_ge(scaled, n - 1)
                nc.vector.reciprocal(rstd[0:rows, p:p + 1], rt[0:rows, p:p + 1]).then_inc(rstd_ready, 1)
                dve.wait_ge(rstd_ready, n + 1)
                if warm:
                    dve.wait_ge(transposed, n - 1)
                nc.vector.tensor_scalar(xs[p][0:rows, :], xt[p][0:rows, :], rstd[0:rows, p:p + 1], None,
                                        ALU.mult).then_inc(scaled, 1)
                dve.wait_ge(transposed, n + 1)
                for k in range(KT // 2, KT):
                    nc.vector.tensor_scalar(c["xnT"][:, k, bass.ds(n * P, rows)], xps[p][:, k // 4, k % 4, 0:rows],
                                            gcol[:, k:k + 1], None, ALU.mult).then_inc(evac_v, 1)
            pairs(dve, tile)

        @block.tensor
        def _(pe):
            pe.wait_ge(small_loaded, 32)
            for t in range(KT):
                ins = nc.tensor.transpose(cps[:, t, :], sconv[:, t * P:(t + 1) * P], c["ident"][0:24, 0:24])
            ins.then_inc(conv_t, 1)

            def tile(j, p, rows, warm):
                n = 2 * j + p
                pe.wait_ge(scaled, n + 1)
                if warm:
                    pe.wait_ge(evac_a, 4 * (n - 1))
                    pe.wait_ge(evac_v, 4 * (n - 1))
                for k in range(KT):
                    ins = nc.tensor.transpose(xps[p][:, k // 4, k % 4, 0:rows], xs[p][0:rows, k * P:(k + 1) * P],
                                              c["ident"][0:rows, 0:rows])
                ins.then_inc(transposed, 1)
            pairs(pe, tile)


def transposed_projection_phase(nc, c, d, s):
    with ExitStack() as ctx:
        sb = lambda name, shape, dt=F32: ctx.enter_context(nc.sbuf_tensor(name, shape, dt))
        sem = phase_semaphores(nc, ctx, "transposed_projection")
        wt = [sb(f"wt{p}", [P, KT, P]) for p in range(2)]
        u = [sb(f"u{p}", [P, 3 + ROWS]) for p in range(2)]
        acc = [sb(f"acc{p}", [P, ROWS]) for p in range(2)]
        sig = sb("sig", [P, ROWS])
        cw = sb("cw", [P, 5, KT])
        qs = sb("qs", [P, KT])
        last3 = sb("last3", [P, KT, 3])
        raw35 = sb("raw35", [P, KT, 35])
        rows35 = sb("rows35", [35, D])
        gbias = sb("gbias", [8, 1])
        gates = sb("gates", [8, ROWS])
        ki = sb("ki", [P, ROWS])
        pg = ctx.enter_context(nc.psum_tensor("pg", [P, G, 512], F32))
        pt = ctx.enter_context(nc.psum_tensor("pt", [P, 3, 512], F32))
        w_loaded = [sem(f"w_loaded{p}") for p in range(2)]
        consts, qs_set, halo0 = sem("consts"), sem("qs_set"), sem("halo0")
        group_mm, group_out = sem("group_mm"), sem("group_out")
        conv_step, sig_ready, conv_out = sem("conv_step"), sem("sig_ready"), sem("conv_out")
        stored = [sem(f"stored{p}") for p in range(2)]
        raw_ready, raw_t, raw_rows, raw_stored = sem("raw_ready"), sem("raw_t"), sem("raw_rows"), sem("raw_stored")
        w0, ik_moved, gates_stored = sem("w0"), sem("ik_moved"), sem("gates_stored")
        sm_t, sm_out, sm_stored = sem("sm_t"), sem("sm_out"), sem("sm_stored")
        STEPS = 10
        NP_CONV, NP_PLAIN = 4, 7
        load_scores, move_candidates, count_pages, begin_take, take, finish_take, keep, turn_rows = sample_selection(
            nc, c, d, lambda name, shape, dt=F32: sb("ss_" + name, shape, dt), sem, pt[:, 2, :])

        w_in = d["w_in"].rearrange("a (k p) n -> (a p) k n", p=P)
        block = ctx.enter_context(nc.Block())

        def tiles(eng, body):
            for p in range(2):
                body(0, p, True, False)
            with eng.Fori(1, NP_CONV) as j:
                for p in range(2):
                    body(j, p, True, True)
            with eng.Fori(NP_CONV, NP_CONV + NP_PLAIN) as j:
                for p in range(2):
                    body(j, p, False, True)

        NTILE = 2 * (NP_CONV + NP_PLAIN)

        @block.sync
        def _(sp):
            for j in range(4):
                sp.dma_start(cw[:, j, :], d["conv_w"][0, j].rearrange("(t p) -> p t", p=P)).then_inc(consts, 16)
            sp.dma_start(cw[:, 4, :], d["conv_b"][0].rearrange("(t p) -> p t", p=P)).then_inc(consts, 16)
            sp.dma_start(gbias[:, :], d["if_bias"].rearrange("a n -> n a")).then_inc(consts, 16)

            def load(j, p, col, warm):
                if warm:
                    sp.wait_ge(group_mm, G * (2 * j + p - 1))
                sp.dma_start(wt[p][:, :, :], w_in[:, :, bass.ds(col, P)]).then_inc(w_loaded[p], 16)
            for p in range(2):
                load(0, p, p * P, False)
            load_scores(sp)
            for lo, hi, first in ((1, 4, 2 * P), (4, 7, C_BQ), (7, 9, C_BQ + 6 * P), (9, 11, C_IQ)):
                if lo == 7:
                    move_candidates(sp)
                with sp.Fori(lo, hi) as j:
                    for p in range(2):
                        load(j, p, (2 * (j - lo) + p) * P + first, True)
            sp.wait_ge(w0, 1)
            sp.dma_start(wt[0][:, :, 0:72], w_in[:, :, C_IK:C_IK + 72]).then_inc(w_loaded[0], 16)
            sp.dma_start(wt[0][:, :, 96:104], w_in[:, :, C_AI:C_AI + 8]).then_inc(w_loaded[0], 16)
            sp.wait_ge(group_out, G * NTILE + 2 * G)
            sp.dma_start(c["ikT"][0:64, :], ki[0:64, :]).then_inc(ik_moved, 16)
            sp.dma_start(c["ikT"][64:128, :], ki[0:64, :]).then_inc(ik_moved, 16)
            sp.dma_start(d["gates"], gates[:, :]).then_inc(gates_stored, 16)
            sp.wait_ge(sm_out, NT)
            sp.dma_start(d["o_ik_prompt"].rearrange("a b (n q) e -> (a b q) n e", q=P),
                         c["sm"][:, 0:NB, 0:ID]).then_inc(sm_stored, 16)
            sp.dma_start(d["o_ik_sample"].rearrange("a b t e -> (a b t) e"), c["sm"][0:SR, NB, 0:ID]).then_inc(sm_stored, 16)
            sp.wait_ge(raw_rows, 2)
            for b in range(DB):
                sp.dma_start(d["o_conv_sample"][0, b], rows35[DT * b + 1:DT * b + 4, :]).then_inc(raw_stored, 16)
            sp.dma_start(d["o_conv_prompt"][0, 0], rows35[32:35, :]).then_inc(raw_stored, 16)
            sp.wait_ge(raw_stored, 16 * (DB + 1))
            sp.wait_ge(sm_stored, 32)
            sp.wait_ge(ik_moved, 32)
            sp.wait_ge(gates_stored, 16)

        @block.gpsimd
        def _(pool):
            nc.gpsimd.memset(qs[:, 0:4], float(DQK) ** -0.5).then_inc(qs_set, 1)
            nc.gpsimd.memset(qs[:, 4:8], 1.0).then_inc(qs_set, 1)
            for p in range(2):
                nc.gpsimd.memset(u[p][:, 0:3], 0.0).then_inc(halo0, 1)
            count_pages(pool)

            def store(j, p, conv, warm):
                n = 2 * j + p
                if conv:
                    pool.wait_ge(conv_out, n + 1)
                    src = acc[p][:, :]
                else:
                    pool.wait_ge(group_out, G * (n + 1))
                    src = u[p][:, 0:ROWS]
                pool.dma_start(d["qt"][n], src).then_inc(stored[p], 16)
            tiles(pool, store)
            pool.wait_ge(group_mm, G * (NTILE - 1))
            nc.gpsimd.memset(wt[0][:, :, 72:96], 0.0).then_inc(w0, 1)
            for p in range(2):
                pool.wait_ge(stored[p], 16 * (NP_CONV + NP_PLAIN))

        @block.tensor
        def _(pe):
            def groups(w, warm_wait, m=P):
                for g in range(G):
                    warm_wait(g)
                    for k in range(KT):
                        ins = nc.tensor.matmul(pg[0:m, g, 0:GW], w[:, k, 0:m], c["xnT"][:, k, g * GW:(g + 1) * GW],
                                               start=k == 0, stop=k == KT - 1)
                    ins.then_inc(group_mm, 1)

            def tile(j, p, conv, warm):
                n = 2 * j + p
                pe.wait_ge(w_loaded[p], 16 * (j + 1))
                first = not warm and p == 0

                def bank_free(g):
                    if not first:
                        pe.wait_ge(group_out, G * (n - 1) + g + 1)
                groups(wt[p], bank_free)
            tiles(pe, tile)
            pe.wait_ge(w_loaded[0], 16 * (NP_CONV + NP_PLAIN) + 32)
            groups(wt[0], lambda g: pe.wait_ge(group_out, G * (NTILE - 1) + g + 1), m=104)
            turn_rows(pe)
            pe.wait_ge(raw_ready, 2)
            for t in range(KT):
                ins = nc.tensor.transpose(pt[0:35, t // 4, (t % 4) * P:(t % 4 + 1) * P], raw35[:, t, :], c["ident"][:, :])
            ins.then_inc(raw_t, 1)
            pe.wait_ge(group_out, G * NTILE + 2 * G)
            for n in range(NT):
                rows = tile_rows(n)
                if n >= G:
                    pe.wait_ge(sm_out, n - G + 1)
                nc.tensor.transpose(pg[0:rows, n % G, 0:72], ki[0:72, n * P:n * P + rows],
                                    c["ident"][0:72, 0:72]).then_inc(sm_t, 1)

        @block.scalar
        def _(act):
            act.wait_ge(consts, 16 * 6)
            act.wait_ge(halo0, 2)

            def tile(j, p, conv, warm):
                n = 2 * j + p
                for g in range(G):
                    act.wait_ge(group_mm, G * n + g + 1)
                    if conv:
                        if g == 0 and warm:
                            act.wait_ge(conv_step, STEPS * (n - 1))
                        nc.scalar.copy(u[p][:, 3 + g * GW:3 + (g + 1) * GW], pg[:, g, 0:GW]).then_inc(group_out, 1)
                    else:
                        if g == 0:
                            act.wait_ge(stored[p], 16 * j)
                        nc.scalar.copy(u[p][:, g * GW:(g + 1) * GW], pg[:, g, 0:GW]).then_inc(group_out, 1)
                if conv:
                    act.wait_ge(conv_step, STEPS * (n + 1))
                    if warm or p == 1:
                        act.wait_ge(conv_out, n)
                    nc.scalar.activation(sig[:, :], acc[p][:, :], ACT.Sigmoid).then_inc(sig_ready, 1)
            tiles(act, tile)
            for g in range(G):
                act.wait_ge(group_mm, G * NTILE + g + 1)
                nc.scalar.copy(ki[0:72, g * GW:(g + 1) * GW], pg[0:72, g, 0:GW]).then_inc(group_out, 1)
                nc.scalar.activation(gates[:, g * GW:(g + 1) * GW], pg[96:104, g, 0:GW], ACT.Identity,
                                     bias=gbias[:, 0:1]).then_inc(group_out, 1)
            act.wait_ge(raw_t, 1)
            for h in range(2):
                nc.scalar.copy(rows35[:, h * 512:(h + 1) * 512], pt[0:35, h, :]).then_inc(raw_rows, 1)

        @block.vector
        def _(dve):
            dve.wait_ge(qs_set, 2)
            dve.wait_ge(consts, 16 * 6)

            def tile(j, p, conv, warm):
                n = 2 * j + p
                a, raw, us = acc[p], u[p], c["us"]
                dve.wait_ge(group_out, G * (n + 1))
                if warm:
                    dve.wait_ge(stored[p], 16 * j)
                av = a[:, SEQ:ROWS].rearrange("p (b t) -> p b t", t=DT)
                nc.vector.tensor_copy(us[:, n, :, 3:7],
                                      raw[:, 3 + SEQ:3 + ROWS].rearrange("p (b t) -> p b t", t=DT)).then_inc(conv_step, 1)
                nc.vector.tensor_copy(last3[:, n, :], raw[:, SEQ:SEQ + 3]).then_inc(conv_step, 1)
                for k in range(4):
                    wk = cw[:, k, bass.ds(n, 1)]
                    dve.wait_ge(conv_step, STEPS * n + 2 * k + 2)
                    for o, i in ((a[:, 0:SEQ], raw[:, k:k + SEQ]), (av, us[:, n, :, k:k + DT])):
                        if k == 0:
                            ins = nc.vector.tensor_scalar(o, i, wk, cw[:, 4, bass.ds(n, 1)], ALU.mult, ALU.add)
                        else:
                            ins = nc.vector.scalar_tensor_tensor(o, i, wk, o, ALU.mult, ALU.add)
                        ins.then_inc(conv_step, 1)
                dve.wait_ge(sig_ready, n + 1)
                nc.vector.scalar_tensor_tensor(a[:, :], a[:, :], qs[:, bass.ds(n, 1)], sig[:, :],
                                               ALU.mult, ALU.mult).then_inc(conv_out, 1)
            for n in range(2 * NP_CONV):
                tile(n // 2, n % 2, True, n >= 2)
                if n == 0:
                    begin_take(dve)
                take(dve, range(2 * n, 2 * n + 2))
            dve.wait_ge(conv_step, STEPS * 8)
            nc.vector.tensor_copy(raw35[:, :, 0:SR].rearrange("p k (b t) -> p k b t", t=DT),
                                  c["us"][:, :, :, 3:7]).then_inc(raw_ready, 1)
            nc.vector.tensor_copy(raw35[:, :, SR:35], last3[:, :, :]).then_inc(raw_ready, 1)
            take(dve, range(4 * NP_CONV, TOPK // 8))
            finish_take(dve)
            keep(dve)
            for n in range(NT):
                rows = tile_rows(n)
                dve.wait_ge(sm_t, n + 1)
                nc.vector.tensor_copy(c["sm"][0:rows, n, :], pg[0:rows, n % G, 0:72]).then_inc(sm_out, 1)


def index_blocks():
    return list(range(NB - 1, TOPK // P - 1, -1))


def pieces(width, size=1024):
    return [(a, min(size, width - a)) for a in range(0, width, size)]


def row_projection_and_topk_phase(nc, c, d):
    with ExitStack() as ctx:
        sb = lambda name, shape, dt=F32: ctx.enter_context(nc.sbuf_tensor(name, shape, dt))
        sem = phase_semaphores(nc, ctx, "row_projection_and_topk")
        w = [sb(f"w{p}", [P, KT, CH]) for p in range(2)]
        st = sb("st", [P, NT, CH])
        iq = [sb(f"iq{p}", [P, 4, P]) for p in range(2)]
        relu = [sb(f"relu{p}", [P, 1024]) for p in range(2)]
        score = [sb(f"score{p}", [P, SEQ]) for p in range(2)]
        mask = [sb(f"mask{p}", [P, SEQ], BF16) for p in range(2)]
        iws = sb("iws", [P, NB, IH])
        best = sb("best", [P, 8])
        pr = ctx.enter_context(nc.psum_tensor("pr", [P, 4, 512], F32))
        pi = ctx.enter_context(nc.psum_tensor("pi", [P, 2, 1024], F32))
        w_loaded = [sem(f"w_loaded{p}") for p in range(2)]
        iq_loaded = [sem(f"iq_loaded{p}") for p in range(2)]
        row_mm, row_out = sem("row_mm"), sem("row_out")
        half_stored = [sem("first_half_stored"), sem("second_half_stored")]
        idx_mm, relu_ready, relu_used = sem("idx_mm"), sem("relu_ready"), sem("relu_used")
        head_step, scores_ready, top_step, mask_ready = sem("head_step"), sem("scores_ready"), sem("top_step"), sem("mask_ready")
        iws_ready, mask_stored = sem("iws_ready"), [sem(f"mask_stored{p}") for p in range(2)]
        early_step = sem("early_step")

        blocks = index_blocks()
        schedule = [("index", 0), ("index", 1)]
        for n in range(len(ROW_CHUNKS)):
            schedule.append(("rows", n))
            if n + 2 < len(blocks):
                schedule.append(("index", n + 2))
        w_in = d["w_in"].rearrange("a (k p) n -> (a p) k n", p=P)
        r_rows = d["r"][0:SEQ, :].rearrange("(n q) m -> q n m", q=P)
        HALF = NB // 2
        kv_chunk = ROW_CHUNKS.index(C_BK)

        def pieces_before(t):
            return sum(IH * len(pieces((b + 1) * P)) for b in blocks[:t])

        def stored_by(half, n):
            return 16 * ((n + 2 * (n > kv_chunk)) if half == 0 else (2 * n + 4 * (n > kv_chunk)))

        block = ctx.enter_context(nc.Block())

        @block.sync
        def _(sp):
            def load(n):
                sp.dma_start(w[n % 2][:, :, :], w_in[:, :, ROW_CHUNKS[n]:ROW_CHUNKS[n] + CH]).then_inc(w_loaded[n % 2], 16)
            load(0)
            load(1)
            extra = [0, 0]
            for n in range(len(ROW_CHUNKS)):
                cols = slice(n * CH, (n + 1) * CH)
                sp.wait_ge(row_out, NT * n + HALF)
                sp.dma_start(r_rows[:, 0:HALF, cols], st[:, 0:HALF, :]).then_inc(half_stored[0], 16)
                if n == kv_chunk:
                    for name, lo in (("o_k_prompt", 0), ("o_v_prompt", 256)):
                        dst = d[name].rearrange("a b (n q) k e -> (a b q) n (k e)", q=P)
                        sp.dma_start(dst[:, 0:HALF, :], st[:, 0:HALF, lo:lo + 256]).then_inc(half_stored[0], 16)
                sp.wait_ge(row_out, NT * (n + 1))
                sp.dma_start(r_rows[:, HALF:NB, cols], st[:, HALF:NB, :]).then_inc(half_stored[1], 16)
                sp.dma_start(d["r"][SEQ:ROWS, cols], st[0:SR, NB, :]).then_inc(half_stored[1], 16)
                if n == kv_chunk:
                    for name, sname, lo in (("o_k_prompt", "o_k_sample", 0), ("o_v_prompt", "o_v_sample", 256)):
                        dst = d[name].rearrange("a b (n q) k e -> (a b q) n (k e)", q=P)
                        sp.dma_start(dst[:, HALF:NB, :], st[:, HALF:NB, lo:lo + 256]).then_inc(half_stored[1], 16)
                        sp.dma_start(d[sname].rearrange("a b t k e -> (a b t) (k e)"),
                                     st[0:SR, NB, lo:lo + 256]).then_inc(half_stored[1], 16)
                if n + 2 < len(ROW_CHUNKS):
                    sp.wait_ge(row_mm, NT * (n + 1))
                    load(n + 2)
            sp.wait_ge(half_stored[0], stored_by(0, len(ROW_CHUNKS)))
            sp.wait_ge(half_stored[1], stored_by(1, len(ROW_CHUNKS)))

        @block.tensor
        def _(pe):
            piece = 0
            for kind, t in schedule:
                if kind == "rows":
                    pe.wait_ge(w_loaded[t % 2], 16 * (t // 2 + 1))
                    for n in range(NT):
                        m = NT * t + n
                        if m >= 4:
                            pe.wait_ge(row_out, m - 3)
                        rows = tile_rows(n)
                        for k in range(KT):
                            ins = nc.tensor.matmul(pr[0:rows, m % 4, :], c["xnT"][:, k, n * P:n * P + rows],
                                                   w[t % 2][:, k, :], start=k == 0, stop=k == KT - 1)
                        ins.then_inc(row_mm, 1)
                else:
                    b = blocks[t]
                    pe.wait_ge(iq_loaded[t % 2], 16 * (t // 2 + 1))
                    for h in range(IH):
                        half = slice(64 * (h % 2), 64 * (h % 2) + 64)
                        for lo, width in pieces((b + 1) * P):
                            if piece >= 2:
                                pe.wait_ge(relu_ready, piece - 1)
                            for a, n in pieces(width, 512):
                                ins = nc.tensor.matmul(pi[:, piece % 2, a:a + n], iq[t % 2][half, h // 2, :],
                                                       c["ikT"][half, lo + a:lo + a + n], start=True, stop=True)
                            ins.then_inc(idx_mm, 1)
                            piece += 1

        @block.scalar
        def _(act):
            def load_iq(t):
                b = blocks[t]
                if t >= 2:
                    act.wait_ge(idx_mm, pieces_before(t - 1))
                act.dma_start(iq[t % 2][:, :, :], d["qt"][T_IQ:T_ALL, :, b * P:(b + 1) * P].rearrange("t p q -> p t q")
                              ).then_inc(iq_loaded[t % 2], 16)
            load_iq(0)
            piece = 0
            for kind, t in schedule:
                if kind == "rows":
                    for n in range(NT):
                        rows = tile_rows(n)
                        act.wait_ge(row_mm, NT * t + n + 1)
                        if n in (0, HALF) and t:
                            act.wait_ge(half_stored[n // HALF], stored_by(n // HALF, t))
                        nc.scalar.copy(st[0:rows, n, :], pr[0:rows, (NT * t + n) % 4, :]).then_inc(row_out, 1)
                else:
                    if t + 1 < len(blocks):
                        load_iq(t + 1)
                    for _ in range(IH):
                        for lo, width in pieces((blocks[t] + 1) * P):
                            act.wait_ge(idx_mm, piece + 1)
                            if piece >= 2:
                                act.wait_ge(relu_used, piece - 1)
                            nc.scalar.activation(relu[piece % 2][:, 0:width], pi[:, piece % 2, 0:width], ACT.Relu,
                                                 scale=float(ID) ** -0.5).then_inc(relu_ready, 1)
                            piece += 1

        @block.gpsimd
        def _(pool):
            for b in range(TOPK // P):
                nc.gpsimd.memset(mask[b][:, 0:(b + 1) * P], 0.0).then_inc(early_step, 1)
                pool.wait_ge(early_step, 2 * b + 1)
                nc.gpsimd.affine_select(out=mask[b][:, 0:(b + 1) * P], in_=mask[b][:, 0:(b + 1) * P],
                                        compare_op=ALU.is_ge, fill=NEG, base=b * P,
                                        pattern=[[-1, (b + 1) * P]], channel_multiplier=1).then_inc(early_step, 1)
                pool.wait_ge(early_step, 2 * b + 2)
                pool.dma_start(d["mask"][b, :, 0:(b + 1) * P], mask[b][:, 0:(b + 1) * P]).then_inc(mask_stored[b], 16)
            pool.wait_ge(iws_ready, 1)
            piece, steps = 0, 0
            for t, b in enumerate(blocks):
                sc = score[t % 2]
                if t >= 2:
                    pool.wait_ge(mask_ready, t - 1)
                    pool.dma_start(d["mask"][blocks[t - 2], :, 0:(blocks[t - 2] + 1) * P],
                                   mask[t % 2][:, 0:(blocks[t - 2] + 1) * P]).then_inc(mask_stored[t % 2], 16)
                for h in range(IH):
                    wh = iws[:, b, h:h + 1]
                    for lo, width in pieces((b + 1) * P):
                        rl = relu[piece % 2][:, 0:width]
                        pool.wait_ge(relu_ready, piece + 1)
                        if h == 0:
                            nc.gpsimd.tensor_scalar(sc[:, lo:lo + width], rl, wh, None, ALU.mult).then_inc(relu_used, 1)
                        else:
                            nc.gpsimd.tensor_scalar(rl, rl, wh, None, ALU.mult).then_inc(head_step, 1)
                            steps += 1
                            pool.wait_ge(head_step, steps)
                            pool.wait_ge(relu_used, piece)
                            nc.gpsimd.tensor_tensor(sc[:, lo:lo + width], sc[:, lo:lo + width], rl, ALU.add
                                                    ).then_inc(relu_used, 1)
                        piece += 1
                pool.wait_ge(relu_used, piece)
                nc.gpsimd.affine_select(out=sc[:, b * P:(b + 1) * P], in_=sc[:, b * P:(b + 1) * P], compare_op=ALU.is_ge,
                                        fill=HIDDEN, base=0, pattern=[[-1, P]], channel_multiplier=1).then_inc(scores_ready, 1)
            for t in range(len(blocks) - 2, len(blocks)):
                pool.wait_ge(mask_ready, t + 1)
                pool.dma_start(d["mask"][blocks[t], :, 0:(blocks[t] + 1) * P],
                               mask[t % 2][:, 0:(blocks[t] + 1) * P]).then_inc(mask_stored[t % 2], 16)
            for p in range(2):
                pool.wait_ge(mask_stored[p], 16 * (1 + len(blocks) // 2))

        @block.vector
        def _(dve):
            nc.vector.tensor_scalar(iws[:, :, :], c["sm"][:, 0:NB, ID:72], float(IH) ** -0.5, None, ALU.mult
                                    ).then_inc(iws_ready, 1)
            nc.vector.memset(best[:, :], 0.0).then_inc(top_step, 1)
            step = 1
            for t, b in enumerate(blocks):
                sc = score[t % 2][:, 0:(b + 1) * P]
                dve.wait_ge(scores_ready, t + 1)
                for _ in range(TOPK // 8):
                    dve.wait_ge(top_step, step)
                    nc.vector.max(best[:, :], sc).then_inc(top_step, 1)
                    dve.wait_ge(top_step, step + 1)
                    nc.vector.match_replace(sc, best[:, :], sc, TAKEN).then_inc(top_step, 1)
                    step += 2
                dve.wait_ge(top_step, 2 * (TOPK // 8) * (t + 1) + 1)
                dve.wait_ge(mask_stored[t % 2], 16 * (t // 2 + 1))
                nc.vector.tensor_scalar(mask[t % 2][:, 0:(b + 1) * P], sc, TAKEN, NEG, ALU.not_equal, ALU.mult
                                        ).then_inc(mask_ready, 1)


def gate_phase(nc, c, d):
    with ExitStack() as ctx:
        sb = lambda name, shape, dt=F32: ctx.enter_context(nc.sbuf_tensor(name, shape, dt))
        sem = phase_semaphores(nc, ctx, "gate")
        gi, gf = sb("gi", [4, ROWS]), sb("gf", [4, ROWS])
        ab = sb("ab", [4, ROWS])
        lf = sb("lf", [4, ROWS])
        mt = sb("mt", [4, SEQ])
        bt = sb("bt", [4, SEQ])
        reset = sb("reset", [4, SEQ])
        row = sb("row", [P, 4, NB, 4])
        mprev = sb("mprev", [P, NB, 4])
        pz = ctx.enter_context(nc.psum_tensor("pz", [P, 4, NB, 4], F32))
        pb = ctx.enter_context(nc.psum_tensor("pb", [P, 2, 256], F32))
        v, a, g, t = sem("vector_step"), sem("scalar_step"), sem("pool_step"), sem("tensor_step")
        out, loaded = sem("m_stored"), sem("loaded")
        block = ctx.enter_context(nc.Block())

        @block.gpsimd
        def _(pool):
            nc.gpsimd.memset(reset[:, :], 1.0).then_inc(g, 1)
            pool.wait_ge(g, 1)
            nc.gpsimd.memset(reset[:, 0:SEQ:P], 0.0).then_inc(g, 1)
            nc.gpsimd.memset(c["sel"][:, :, :], 0.0).then_inc(g, 1)
            pool.wait_ge(g, 3)
            nc.gpsimd.affine_select(out=c["sel"][:, :, :], in_=c["sel"][:, :, :], compare_op=ALU.not_equal, fill=1.0,
                                    base=0, pattern=[[-1, 4], [0, P]], channel_multiplier=1).then_inc(g, 1)
            nc.gpsimd.memset(c["future"][:, :], 0.0).then_inc(g, 1)
            pool.wait_ge(g, 5)
            nc.gpsimd.affine_select(out=c["future"][:, :], in_=c["future"][:, :], compare_op=ALU.is_ge, fill=NEG,
                                    base=0, pattern=[[1, P]], channel_multiplier=-1).then_inc(g, 1)

        @block.scalar
        def _(act):
            act.wait_ge(v, 1)
            nc.scalar.activation(ab[:, :], ab[:, :], ACT.Exp, scale=-1.0).then_inc(a, 1)
            act.wait_ge(v, 2)
            nc.scalar.activation(ab[:, :], ab[:, :], ACT.Ln).then_inc(a, 1)
            act.wait_ge(v, 12)
            for j, name in enumerate(("ws", "wp", "wi", "em")):
                nc.scalar.activation(c[name][:, :, :], c[name][:, :, :], ACT.Exp).then_inc(a, 1)

        @block.vector
        def _(dve):
            dve.wait_ge(loaded, 32)
            nc.vector.scalar_tensor_tensor(ab[:, :], gf[:, :], -1.0, gf[:, :], ALU.mult, ALU.max).then_inc(v, 1)
            dve.wait_ge(a, 1)
            nc.vector.tensor_scalar(ab[:, :], ab[:, :], 1.0, None, ALU.add).then_inc(v, 1)
            dve.wait_ge(a, 2)
            nc.vector.scalar_tensor_tensor(lf[:, :], gf[:, :], 0.0, ab[:, :], ALU.min, ALU.subtract).then_inc(v, 1)
            dve.wait_ge(v, 3)
            nc.vector.tensor_copy(c["gis"][:, :], gi[:, SEQ:ROWS])
            nc.vector.tensor_copy(c["lfs"][:, :], lf[:, SEQ:ROWS]).then_inc(v, 1)
            nc.vector.tensor_tensor_scan(mt[:, :], lf[:, 0:SEQ], gi[:, 0:SEQ], 0.0, ALU.add, ALU.max).then_inc(v, 1)
            dve.wait_ge(g, 2)
            nc.vector.tensor_tensor_scan(bt[:, :], reset[:, :], lf[:, 0:SEQ], 0.0, ALU.mult, ALU.add).then_inc(v, 1)
            dve.wait_ge(v, 6)
            nc.vector.tensor_tensor(c["g"][:, :], bt[:, :], mt[:, :], ALU.subtract).then_inc(v, 1)
            dve.wait_ge(t, 1)
            nc.vector.tensor_copy(row[:, :, :, :], pz[:, :, :, :]).then_inc(v, 1)
            nc.vector.memset(mprev[:, 0, :], 0.0).then_inc(v, 1)
            dve.wait_ge(t, 2)
            pbm = pb[:, 0, 0:64].rearrange("p (h n) -> p n h", h=4)
            pbg = pb[:, 1, 0:64].rearrange("p (h n) -> p n h", h=4)
            nc.vector.tensor_copy(mprev[:, 1:NB, :], pbm[:, 0:NB - 1, :]).then_inc(v, 1)
            dve.wait_ge(v, 10)
            i, b, m, gg = (row[:, x, :, :] for x in range(4))
            nc.vector.tensor_tensor(c["a"][:, :, :], i, b, ALU.subtract).then_inc(v, 1)
            nc.vector.tensor_tensor(c["wp"][:, :, :], mprev[:, :, :], pbg, ALU.add)
            nc.vector.tensor_tensor(c["wi"][:, :, :], mprev[:, :, :], gg, ALU.add)
            nc.vector.tensor_scalar(c["em"][:, :, :], m, -1.0, None, ALU.mult)
            dve.wait_ge(v, 11)
            nc.vector.tensor_tensor(c["ws"][:, :, :], c["a"][:, :, :], pbg, ALU.add).then_inc(v, 1)

        @block.tensor
        def _(pe):
            pe.wait_ge(v, 7)
            for x, src in enumerate((gi, bt, mt, c["g"])):
                for n in range(NB):
                    ins = nc.tensor.transpose(pz[:, x, n, :], src[0:4, n * P:(n + 1) * P], c["ident"][0:4, 0:4])
            ins.then_inc(t, 1)
            pe.wait_ge(g, 4)
            for x, src in enumerate((mt, c["g"])):
                for h in range(4):
                    ins = nc.tensor.matmul(pb[:, x, h * NB:(h + 1) * NB], c["sel"][:, h, :], src[0:4, P - 1:SEQ:P],
                                           start=True, stop=True)
            ins.then_inc(t, 1)

        @block.sync
        def _(sp):
            sp.dma_start(gi[:, :], d["gates"][0:4, :]).then_inc(loaded, 16)
            sp.dma_start(gf[:, :], d["gates"][4:8, :]).then_inc(loaded, 16)
            sp.wait_ge(v, 5)
            sp.dma_start(d["o_m_prompt"][0, 0].rearrange("(h a) -> h a", a=1), mt[:, SEQ - 1:SEQ]).then_inc(out, 16)
            sp.wait_ge(out, 16)


AHEAD = 3


def key_pieces(i):
    return len(pieces((i + 1) * P))


def key_groups(i):
    return -(-(i + 1) // 4)


def mixing_events():
    heads = [(i, hd) for i in range(NB) for hd in range(BH)]
    events = [(m, 0) for m in ("M1", "M2", "M3", "Q", "M4", "Y")] + [("S", 0, hd) for hd in range(AHEAD)]
    events += [("E", 0, hd) for hd in range(AHEAD - 1)]
    for n, (i, hd) in enumerate(heads):
        events.append(("T", i, hd))
        if n + AHEAD < len(heads):
            events.append(("S", *heads[n + AHEAD]))
        if n + AHEAD - 1 < len(heads):
            events.append(("E", *heads[n + AHEAD - 1]))
        if hd % 4 == 3:
            events.append(("O", i, hd // 4))
        if hd == 0 and i:
            events.append(("B", i - 1, 1))
        if hd == 4:
            events.append(("B", i, 0))
        if hd == 3:
            events.append(("Q", i + 1))
        if i + 1 < NB and hd in (0, 1, 2, 4, 5):
            events.append(({0: "M1", 1: "M2", 2: "M3", 4: "M4", 5: "Y"}[hd], i + 1))
    events.append(("B", NB - 1, 1))
    return events


def numbered(events):
    slots, banks = [], []
    for e in events:
        if e[0] == "S":
            slots += [(*e, q) for q in range(key_pieces(e[1]))]
        elif e[0] == "T":
            banks += [(*e, q) for q in range(key_groups(e[1]))]
        elif e[0] in ("M1", "M2"):
            slots.append(e)
        elif e[0] in ("M3", "M4"):
            slots += [e, (*e, "sums")]
        if e[0] == "M1":
            banks.append(e)
    return {k: n for n, k in enumerate(slots)}, {k: n for n, k in enumerate(banks)}


def prompt_mixing_phase(nc, c, d):
    with ExitStack() as ctx:
        sb = lambda name, shape, dt=F32: ctx.enter_context(nc.sbuf_tensor("mix_" + name, shape, dt))
        sem = phase_semaphores(nc, ctx, "prompt_mixing")
        ps = lambda name, shape: ctx.enter_context(nc.psum_tensor("mix_" + name, shape, F32))
        kT = sb("kT", [P, KV, SEQ])
        v = sb("v", [P, NB, KV * HD])
        aqk = [sb(f"aqk{p}", [P, 2, AH, P]) for p in range(2)]
        bq = [sb(f"bq{p}", [P, BH, P]) for p in range(2)]
        av = [sb(f"av{p}", [P, AH, DV]) for p in range(2)]
        ozb = [sb(f"ozb{p}", [P, 3, D]) for p in range(2)]
        mk = [sb(f"mk{p}", [P, SEQ], BF16) for p in range(2)]
        prob = [sb(f"prob{p}", [P, SEQ]) for p in range(AHEAD)]
        probT = sb("probT", [P, NB, 4, P])
        sga = sb("sga", [P, 2, D])
        sgb = sb("sgb", [P, D])
        h = sb("h", [P, AH, DV])
        inter = sb("inter", [P, AH, DV])
        cT = sb("cT", [P, AH, DV])
        nT = sb("nT", [P, AH])
        nw = sb("nw", [P, AH])
        kw = sb("kw", [P, AH, P])
        dmat = sb("dmat", [P, AH, P])
        sd = sb("sd", [P, AH, P])
        na = sb("na", [P, D])
        ya = sb("ya", [P, AH, DV])
        yb = sb("yb", [P, BH, P])
        oT = sb("oT", [P, 4, P])
        den = sb("den", [P, 4, AH])
        ones = sb("ones", [P, 1])
        mx = sb("mx", [P, AHEAD, 2])
        sums = sb("sums", [P, 2, BH])
        rsum = sb("rsum", [P, BH])
        cout = sb("cout", [P, AH, 2, P])
        slot = ps("slot", [P, 2, 1024])
        pg, po, pb = ps("pg", [P, 2, 512]), ps("po", [P, 512]), ps("pb", [P, 512])
        resident, state_init, na_loaded = sem("resident"), sem("state_init"), sem("na_loaded")
        m_loaded, a_loaded = [sem(f"m_loaded{p}") for p in range(2)], [sem(f"a_loaded{p}") for p in range(2)]
        slot_mm, slot_free = sem("slot_mm"), [sem(f"slot_free{x}") for x in range(2)]
        turned, bank_free = sem("turned"), [sem(f"bank_free{x}") for x in range(2)]
        dmat_ready = sem("dmat_ready")
        rden_ready, sq_ready, rms_ready, chain = sem("rden_ready"), sem("sq_ready"), sem("rms_ready"), sem("chain")
        sig_a, sig_b, pool_step, gates_a, gates_b = sem("sig_a"), sem("sig_b"), sem("pool_step"), sem("gates_a"), sem("gates_b")
        ya_ready, ya_stored, yb_stored = sem("ya_ready"), sem("ya_stored"), sem("yb_stored")
        nbias_ready, p_ready = sem("nbias_ready"), sem("p_ready")
        o_mm, oT_ready, oback_mm, yb_ready = sem("o_mm"), sem("oT_ready"), sem("oback_mm"), sem("yb_ready")
        last_t, last_out, last_stored = sem("last_t"), sem("last_out"), sem("last_stored")
        SCALE = float(HD) ** -0.5

        events = mixing_events()
        slot_no, bank_no = numbered(events)

        def slot_filled(eng, key):
            n = slot_no[key]
            eng.wait_ge(slot_mm, n + 1)
            return n % 2

        def after_slot(eng, key):
            n = slot_no[key]
            eng.wait_ge(slot_free[n % 2], n // 2 + 1)

        def after_bank(eng, key):
            n = bank_no[key]
            eng.wait_ge(bank_free[n % 2], n // 2 + 1)

        block = ctx.enter_context(nc.Block())

        @block.sync
        def _(sp):
            def load_m(i):
                p, rows = i % 2, slice(i * P, (i + 1) * P)
                if i >= 2:
                    after_slot(sp, ("M4", i - 2))
                    sp.wait_ge(gates_a, i - 1)
                for dst, src in ((aqk[p][:, :, :, :], d["qt"][0:8, :, rows].rearrange("(a t) p q -> p a t q", a=2)),
                                 (av[p][:, :, :], d["r"][rows, 0:D].rearrange("q (h e) -> q h e", h=AH)),
                                 (ozb[p][:, 0:2, :], d["r"][rows, R_AO:R_AO + 2 * D].rearrange("q (a e) -> q a e", a=2))):
                    sp.dma_start(dst, src).then_inc(m_loaded[p], 16)

            def load_a(i):
                p, rows = i % 2, slice(i * P, (i + 1) * P)
                if i >= 2:
                    after_slot(sp, ("S", i - 2, BH - 1, key_pieces(i - 2) - 1))
                    sp.wait_ge(gates_b, i - 1)
                for dst, src in ((bq[p][:, :, :], d["qt"][T_BQ:T_BK, :, rows].rearrange("t p q -> p t q")),
                                 (mk[p][:, 0:(i + 1) * P], d["mask"][i, :, 0:(i + 1) * P]),
                                 (ozb[p][:, 2, :], d["r"][rows, R_BZ:R_BZ + D])):
                    sp.dma_start(dst, src).then_inc(a_loaded[p], 16)
            load_m(0)
            sp.dma_start(kT[:, :, :], d["qt"][T_BK:T_IQ, :, 0:SEQ].rearrange("k p s -> p k s")).then_inc(resident, 16)
            sp.dma_start(na[:, :], d["norm_a"][0:1, :].to_broadcast([P, D])).then_inc(na_loaded, 16)
            load_a(0)
            sp.dma_start(v[:, :, :], d["r"][0:SEQ, R_BKV + 256:R_BKV + 512].rearrange("(n p) e -> p n e", p=P)
                         ).then_inc(resident, 16)
            load_m(1)
            load_a(1)
            for i in range(2, NB):
                load_m(i)
                load_a(i)

        @block.gpsimd
        def _(pool):
            nc.gpsimd.memset(cT[:, :, :], 0.0).then_inc(state_init, 1)
            nc.gpsimd.memset(nT[:, :], 0.0).then_inc(state_init, 1)
            nc.gpsimd.memset(ones[:, :], 1.0).then_inc(state_init, 1)
            pool.wait_ge(na_loaded, 16)

            for e in events:
                i, p = e[1], e[1] % 2
                if e[0] == "Q":
                    if i < NB:
                        pool.wait_ge(sig_a, i + 1)
                        nc.gpsimd.tensor_tensor(sga[:, 0, :], sga[:, 0, :], sga[:, 1, :], ALU.mult).then_inc(pool_step, 1)
                        nc.gpsimd.tensor_tensor(ozb[p][:, 1, :], ozb[p][:, 1, :], na[:, :], ALU.mult).then_inc(pool_step, 1)
                        pool.wait_ge(pool_step, 2 * i + 2)
                        nc.gpsimd.tensor_tensor(sga[:, 1, :], sga[:, 0, :], ozb[p][:, 1, :], ALU.mult).then_inc(gates_a, 1)
                    if i:
                        pool.wait_ge(sig_b, i)
                        nc.gpsimd.tensor_tensor(sgb[:, :], sgb[:, :], ozb[1 - p][:, 2, :], ALU.mult).then_inc(gates_b, 1)
                elif e[0] == "Y":
                    rows = slice(i * P, (i + 1) * P)
                    pool.wait_ge(ya_ready, 4 * (i + 1))
                    pool.dma_start(d["y"][rows, 0:D].rearrange("q (h e) -> q h e", h=AH), ya[:, :, :]).then_inc(ya_stored, 16)
                elif e[0] == "B" and e[2] == 1:
                    rows = slice(i * P, (i + 1) * P)
                    pool.wait_ge(yb_ready, 8 * (i + 1))
                    pool.dma_start(d["y"][rows, D:2 * D].rearrange("q (h e) -> q h e", h=BH), yb[:, :, :]).then_inc(yb_stored, 16)
            pool.wait_ge(last_out, 3)
            pool.dma_start(d["o_C_prompt"].rearrange("a b h (x q) e -> (a b q) h x e", q=P), cout[:, :, :, :]).then_inc(last_stored, 16)
            pool.dma_start(d["o_n_prompt"][0, 0], h[0:4, 0, 0:P]).then_inc(last_stored, 16)
            pool.wait_ge(last_stored, 32)
            pool.wait_ge(ya_stored, 16 * NB)
            pool.wait_ge(yb_stored, 16 * NB)

        @block.tensor
        def _(pe):
            def take_slot(key):
                n = slot_no[key]
                if n >= 2:
                    pe.wait_ge(slot_free[n % 2], n // 2)
                return n % 2

            def take_bank(key):
                n = bank_no[key]
                if n >= 2:
                    pe.wait_ge(bank_free[n % 2], n // 2)
                return n % 2

            mm, turn = nc.tensor.matmul, nc.tensor.transpose
            pe.wait_ge(state_init, 3)
            for e in events:
                kind, i, p = e[0], e[1], e[1] % 2
                if kind == "S":
                    hd = e[2]
                    if hd == 0:
                        pe.wait_ge(a_loaded[p], 48 * (i // 2 + 1))
                        pe.wait_ge(resident, 32)
                    for q, (lo, width) in enumerate(pieces((i + 1) * P)):
                        s = take_slot((*e, q))
                        for a, m in pieces(width, 512):
                            ins = mm(slot[:, s, a:a + m], bq[p][:, hd, :], kT[:, hd // 4, lo + a:lo + a + m], start=True, stop=True)
                        ins.then_inc(slot_mm, 1)
                elif kind == "T":
                    hd = e[2]
                    pe.wait_ge(p_ready, BH * i + hd + 1)
                    for q in range(key_groups(i)):
                        s = take_bank((*e, q))
                        for t in range(4 * q, min(4 * q + 4, i + 1)):
                            ins = turn(pg[:, s, (t % 4) * P:(t % 4 + 1) * P], prob[(BH * i + hd) % AHEAD][:, t * P:(t + 1) * P], c["ident"][:, :])
                        ins.then_inc(turned, 1)
                elif kind == "O":
                    kv = e[2]
                    last = bank_no[("T", i, 4 * kv + 3, key_groups(i) - 1)]
                    for x in range(2):
                        if (last + 2 - x) // 2:
                            pe.wait_ge(bank_free[x], (last + 2 - x) // 2)
                    if 2 * i + kv:
                        pe.wait_ge(oT_ready, 2 * i + kv)
                    for t in range(i + 1):
                        ins = mm(po[:, :], v[:, t, kv * HD:(kv + 1) * HD], probT[:, t, :, :], start=t == 0, stop=t == i)
                    ins.then_inc(o_mm, 1)
                elif kind == "B":
                    kv = e[2]
                    pe.wait_ge(oT_ready, 2 * i + kv + 1)
                    if 2 * i + kv:
                        pe.wait_ge(yb_ready, 8 * i + 4 * kv)
                    for g in range(4):
                        ins = turn(pb[:, g * P:(g + 1) * P], oT[:, g, :], c["ident"][:, :])
                    ins.then_inc(oback_mm, 1)
                elif kind == "M1":
                    pe.wait_ge(m_loaded[p], 48 * (i // 2 + 1))
                    s = take_slot(e)
                    cols = slice(i * P, (i + 1) * P)
                    for hh in range(AH):
                        mm(slot[:, s, hh * P:(hh + 1) * P], c["sel"][:, hh, :], c["g"][:, cols], start=True, stop=False)
                        mm(slot[:, s, hh * P:(hh + 1) * P], c["ident"][:, :], c["future"][:, :], start=False, stop=True)
                    for hh in range(AH):
                        ins = mm(slot[:, s, 512 + hh * P:512 + (hh + 1) * P], aqk[p][:, 1, hh, :], aqk[p][:, 0, hh, :], start=True, stop=True)
                    ins.then_inc(slot_mm, 1)
                    s = take_bank(e)
                    for hh in range(AH):
                        ins = turn(pg[:, s, hh * P:(hh + 1) * P], aqk[p][:, 1, hh, :], c["ident"][:, :])
                    ins.then_inc(turned, 1)
                elif kind == "M2":
                    if i:
                        after_slot(pe, ("M4", i - 1))
                        after_slot(pe, ("M4", i - 1, "sums"))
                    s = take_slot(e)
                    for hh in range(AH):
                        ins = mm(slot[:, s, hh * DV:(hh + 1) * DV], aqk[p][:, 0, hh, :], cT[:, hh, :], start=True, stop=True)
                    ins.then_inc(slot_mm, 1)
                elif kind == "M3":
                    after_slot(pe, ("M1", i))
                    s = take_slot(e)
                    for hh in range(AH):
                        ins = mm(slot[:, s, hh * DV:(hh + 1) * DV], sd[:, hh, :], av[p][:, hh, :], start=True, stop=True)
                    ins.then_inc(slot_mm, 1)
                    s = take_slot((*e, "sums"))
                    for hh in range(AH):
                        mm(slot[:, s, hh:hh + 1], aqk[p][:, 0, hh, :], nT[:, hh:hh + 1], start=True, stop=True)
                        ins = mm(slot[:, s, 8 + hh:9 + hh], sd[:, hh, :], ones[:, :], start=True, stop=True)
                    ins.then_inc(slot_mm, 1)
                elif kind == "M4":
                    after_bank(pe, ("M1", i))
                    s = take_slot(e)
                    for hh in range(AH):
                        ins = mm(slot[:, s, hh * DV:(hh + 1) * DV], kw[:, hh, :], av[p][:, hh, :], start=True, stop=True)
                    ins.then_inc(slot_mm, 1)
                    s = take_slot((*e, "sums"))
                    for hh in range(AH):
                        ins = mm(slot[:, s, hh:hh + 1], kw[:, hh, :], ones[:, :], start=True, stop=True)
                    ins.then_inc(slot_mm, 1)
            for x in range(2):
                pe.wait_ge(slot_free[x], (len(slot_no) + 1 - x) // 2)
            pe.wait_ge(yb_ready, 8 * NB)
            for hh in range(AH):
                for x in range(2):
                    turn(slot[:, hh // 2, (hh % 2 * 2 + x) * P:(hh % 2 * 2 + x + 1) * P], cT[:, hh, x * P:(x + 1) * P], c["ident"][:, :])
            turn(pb[0:4, 0:P], nT[:, :], c["ident"][:, :]).then_inc(last_t, 1)

        def copy_groups(act, i, hd):
            for q in range(key_groups(i)):
                n = bank_no[("T", i, hd, q)]
                act.wait_ge(turned, n + 1)
                if hd % 4 == 0 and 2 * i + hd // 4:
                    act.wait_ge(o_mm, 2 * i + hd // 4)
                t0, t1 = 4 * q, min(4 * q + 4, i + 1)
                nc.scalar.copy(probT[:, t0:t1, hd % 4, :],
                     pg[:, n % 2, 0:(t1 - t0) * P].rearrange("p (t q) -> p t q", q=P)).then_inc(bank_free[n % 2], 1)

        def copy_k(act, i):
            n = bank_no[("M1", i)]
            act.wait_ge(turned, n + 1)
            if i:
                after_slot(act, ("M4", i - 1, "sums"))
            for hh in range(AH):
                ins = nc.scalar.activation(kw[:, hh, :], pg[:, n % 2, hh * P:(hh + 1) * P], ACT.Copy, scale=c["ws"][:, i, hh:hh + 1])
            ins.then_inc(bank_free[n % 2], 1)

        @block.scalar
        def _(act):
            for e in events:
                kind, i, p = e[0], e[1], e[1] % 2
                if kind == "E":
                    hd = e[2]
                    act.wait_ge(nbias_ready, BH * i + hd + 1)
                    if i:
                        act.wait_ge(yb_ready, 8 * (i - 1) + 4 if hd < 4 else 8 * i)
                    nc.scalar.activation(prob[(BH * i + hd) % AHEAD][:, 0:(i + 1) * P], prob[(BH * i + hd) % AHEAD][:, 0:(i + 1) * P], ACT.Exp,
                                         scale=SCALE, bias=mx[:, (BH * i + hd) % AHEAD, 1:2], accum_out=sums[:, 0, hd:hd + 1]).then_inc(p_ready, 1)
                elif kind == "T":
                    copy_groups(act, i, e[2])
                elif kind == "O":
                    kv = e[2]
                    act.wait_ge(o_mm, 2 * i + kv + 1)
                    if 2 * i + kv:
                        act.wait_ge(oback_mm, 2 * i + kv)
                    nc.scalar.copy(oT[:, :, :], po[:, :].rearrange("p (g q) -> p g q", g=4)).then_inc(oT_ready, 1)
                elif kind == "M1":
                    s = slot_filled(act, e)
                    if i:
                        after_slot(act, ("M1", i - 1))
                    for hh in range(AH):
                        ins = nc.scalar.activation(dmat[:, hh, :], slot[:, s, hh * P:(hh + 1) * P], ACT.Exp, bias=c["a"][:, i, hh:hh + 1])
                    ins.then_inc(dmat_ready, 1)
                    copy_k(act, i)
                elif kind == "M2":
                    s = slot_filled(act, e)
                    if i:
                        after_slot(act, ("M3", i - 1))
                        act.wait_ge(rms_ready, i)
                    for hh in range(AH):
                        ins = nc.scalar.activation(inter[:, hh, :], slot[:, s, hh * DV:(hh + 1) * DV], ACT.Copy,
                                                   scale=c["wi"][:, i, hh:hh + 1])
                    ins.then_inc(slot_free[s], 1)
                elif kind == "Q":
                    if i < NB:
                        act.wait_ge(rden_ready, i + 1)
                        after_slot(act, ("M3", i))
                        for hh in range(AH):
                            ins = nc.scalar.activation(inter[:, hh, :], h[:, hh, :], ACT.Square, scale=den[:, 2, hh:hh + 1],
                                                       accum_out=den[:, 3, hh:hh + 1])
                        ins.then_inc(sq_ready, 1)
                        act.wait_ge(sq_ready, i + 1)
                        nc.scalar.activation(den[:, 1, :], den[:, 3, :], ACT.Sqrt, scale=1.0 / DV, bias=c["eps"][:, 0:1]).then_inc(rms_ready, 1)
                        act.wait_ge(m_loaded[p], 48 * (i // 2 + 1))
                        if i:
                            act.wait_ge(ya_ready, 4 * i)
                        nc.scalar.activation(sga[:, :, :], ozb[p][:, 0:2, :], ACT.Sigmoid).then_inc(sig_a, 1)
                    if i:
                        act.wait_ge(a_loaded[1 - p], 48 * ((i - 1) // 2 + 1))
                        if i >= 2:
                            act.wait_ge(yb_ready, 8 * (i - 1))
                        nc.scalar.activation(sgb[:, :], ozb[1 - p][:, 2, :], ACT.Sigmoid).then_inc(sig_b, 1)
            act.wait_ge(last_t, 1)
            for x in range(2):
                nc.scalar.copy(cout[:, 2 * x:2 * x + 2, :, :],
                               slot[:, x, 0:512].rearrange("p (h x e) -> p h x e", h=2, x=2)).then_inc(last_out, 1)
            nc.scalar.copy(h[0:4, 0, 0:P], pb[0:4, 0:P]).then_inc(last_out, 1)

        @block.vector
        def _(dve):
            links = [0]

            def link(ins):
                links[0] += 1
                ins.then_inc(chain, 1)
                dve.wait_ge(chain, links[0])

            for e in events:
                kind, i, p = e[0], e[1], e[1] % 2
                if kind == "S":
                    hd = e[2]
                    b = (BH * i + hd) % AHEAD
                    for q, (lo, width) in enumerate(pieces((i + 1) * P)):
                        s = slot_filled(dve, (*e, q))
                        if q == 0:
                            dve.wait_ge(a_loaded[p], 48 * (i // 2 + 1))
                            if BH * i + hd >= AHEAD:
                                j, hp = divmod(BH * i + hd - AHEAD, BH)
                                dve.wait_ge(turned, bank_no[("T", j, hp, key_groups(j) - 1)] + 1)
                        else:
                            after_slot(dve, (*e, q - 1))
                        nc.vector.tensor_tensor_reduce(out=prob[b][:, lo:lo + width], in0=slot[:, s, 0:width],
                                                       in1=mk[p][:, lo:lo + width], scale=1.0,
                                                       scalar=mx[:, b, 0:1] if q else TAKEN, op0=ALU.add, op1=ALU.max,
                                                       accum_out=mx[:, b, 0:1]).then_inc(slot_free[s], 1)
                    after_slot(dve, (*e, q))
                    if BH * i + hd >= AHEAD:
                        dve.wait_ge(p_ready, BH * i + hd - AHEAD + 1)
                    nc.vector.tensor_scalar(mx[:, b, 1:2], mx[:, b, 0:1], -SCALE, None, ALU.mult).then_inc(nbias_ready, 1)
                elif kind == "B":
                    kv = e[2]
                    dve.wait_ge(oback_mm, 2 * i + kv + 1)
                    dve.wait_ge(gates_b, i + 1)
                    link(nc.vector.reciprocal(rsum[:, 4 * kv:4 * kv + 4], sums[:, 0, 4 * kv:4 * kv + 4]))
                    if i and kv == 0:
                        dve.wait_ge(yb_stored, 16 * i)
                    for g in range(4):
                        hq = 4 * kv + g
                        nc.vector.scalar_tensor_tensor(yb[:, hq, :], pb[:, g * P:(g + 1) * P], rsum[:, hq:hq + 1],
                                                       sgb[:, hq * P:(hq + 1) * P], ALU.mult, ALU.mult).then_inc(yb_ready, 1)
                elif kind == "M1":
                    s = slot_filled(dve, e)
                    dve.wait_ge(dmat_ready, i + 1)
                    if i:
                        dve.wait_ge(slot_mm, slot_no[("M3", i - 1, "sums")] + 1)
                    nc.vector.tensor_tensor(sd[:, :, :], slot[:, s, 512:1024].rearrange("p (h q) -> p h q", h=AH),
                                            dmat[:, :, :], ALU.mult).then_inc(slot_free[s], 1)
                elif kind == "M3":
                    s = slot_filled(dve, e)
                    after_slot(dve, ("M2", i))
                    if i:
                        dve.wait_ge(rms_ready, i)
                        dve.wait_ge(ya_ready, 4 * i)
                    nc.vector.tensor_tensor(h[:, :, :], inter[:, :, :], slot[:, s, :].rearrange("p (h e) -> p h e", h=AH),
                                            ALU.add).then_inc(slot_free[s], 1)
                    s = slot_filled(dve, (*e, "sums"))
                    link(nc.vector.tensor_tensor(den[:, 0, :], slot[:, s, 0:4], c["wi"][:, i, :], ALU.mult))
                    nc.vector.tensor_tensor(den[:, 0, :], slot[:, s, 8:12], den[:, 0, :], ALU.add).then_inc(slot_free[s], 1)
                    after_slot(dve, (*e, "sums"))
                    link(nc.vector.scalar_tensor_tensor(den[:, 1, :], den[:, 0, :], -1.0, den[:, 0, :], ALU.mult, ALU.max))
                    link(nc.vector.tensor_tensor(den[:, 1, :], den[:, 1, :], c["em"][:, i, :], ALU.max))
                    nc.vector.reciprocal(den[:, 2, :], den[:, 1, :]).then_inc(rden_ready, 1)
                elif kind == "M4":
                    s = slot_filled(dve, e)
                    for hh in range(AH):
                        ins = nc.vector.scalar_tensor_tensor(cT[:, hh, :], cT[:, hh, :], c["wp"][:, i, hh:hh + 1],
                                                             slot[:, s, hh * DV:(hh + 1) * DV], ALU.mult, ALU.add)
                    ins.then_inc(slot_free[s], 1)
                    s = slot_filled(dve, (*e, "sums"))
                    link(nc.vector.tensor_tensor(nw[:, :], nT[:, :], c["wp"][:, i, :], ALU.mult))
                    nc.vector.tensor_tensor(nT[:, :], nw[:, :], slot[:, s, 0:4], ALU.add).then_inc(slot_free[s], 1)
                    after_slot(dve, e)
                    after_slot(dve, (*e, "sums"))
                elif kind == "Y":
                    dve.wait_ge(rms_ready, i + 1)
                    link(nc.vector.reciprocal(den[:, 0, :], den[:, 1, :]))
                    link(nc.vector.tensor_tensor(den[:, 0, :], den[:, 0, :], den[:, 2, :], ALU.mult))
                    dve.wait_ge(gates_a, i + 1)
                    if i:
                        dve.wait_ge(ya_stored, 16 * i)
                    for hh in range(AH):
                        nc.vector.scalar_tensor_tensor(ya[:, hh, :], h[:, hh, :], den[:, 0, hh:hh + 1],
                                                       sga[:, 1, hh * DV:(hh + 1) * DV], ALU.mult, ALU.mult).then_inc(ya_ready, 1)


class Steps:

    def __init__(self, sem, *names):
        self.sem, self.names, self.done = sem, list(names), 0
        assert len(set(names)) == len(names), "a step's name is used twice"

    def __getitem__(self, name):
        return self.names.index(name) + 1

    def step(self, name):
        assert self.names[self.done] == name, (self.names[self.done], name)
        self.done += 1
        return 1


def sample_index_projection_phase(nc, c, d):
    with ExitStack() as ctx:
        sb = lambda name, shape, dt=F32: ctx.enter_context(nc.sbuf_tensor("sp_" + name, shape, dt))
        sem = phase_semaphores(nc, ctx, "sample_index_projection")
        NC = C_IK + 72 - C_IQ
        x, xs, junk = (sb(n, [SR, D]) for n in ("x", "xs", "junk"))
        stat = sb("stat", [SR, 3])
        gcol = sb("gcol", [P, KT])
        xT = sb("xT", [P, KT, SR])
        w = sb("w", [P, KT, NC])
        out = sb("out", [P, 5, SR])
        iw = sb("iw", [SR, IH])
        px = ctx.enter_context(nc.psum_tensor("sp_px", [P, KT, SR], F32))
        pq = ctx.enter_context(nc.psum_tensor("sp_pq", [P, 5, SR], F32))
        pw = ctx.enter_context(nc.psum_tensor("sp_pw", [SR, IH], F32))
        loaded, w_loaded, ident_step, eps_set = sem("loaded"), sem("w_loaded"), sem("ident_step"), sem("eps_set")
        squared, rooted, rstd_ready, scaled = sem("squared"), sem("rooted"), sem("rstd_ready"), sem("scaled")
        turned, xT_ready, multiplied, out_ready, stored = sem("turned"), sem("xT_ready"), sem("multiplied"), sem("out_ready"), sem("stored")
        block = ctx.enter_context(nc.Block())

        @block.sync
        def _(sp):
            sp.dma_start(x[:, :], d["x_sample"].rearrange("b t c -> (b t) c")).then_inc(loaded, 16)
            sp.dma_start(gcol[:, :], d["norm_pre"].rearrange("a (t p) -> (a p) t", p=P)).then_inc(loaded, 16)
            w_in = d["w_in"].rearrange("a (k p) n -> (a p) k n", p=P)
            for half in range(2):
                ks = slice(half * KT // 2, (half + 1) * KT // 2)
                sp.dma_start(w[:, ks, :], w_in[:, ks, C_IQ:C_IQ + NC]).then_inc(w_loaded, 16)
            sp.wait_ge(out_ready, 3)
            sp.dma_start(d["iq_scr"].rearrange("t p s -> p t s"), out[:, 0:4, :]).then_inc(stored, 16)
            sp.dma_start(d["ik_scr"], out[0:ID, 4, :]).then_inc(stored, 16)
            sp.dma_start(d["iw_scr"], iw[:, :]).then_inc(stored, 16)
            sp.wait_ge(stored, 48)

        @block.gpsimd
        def _(pool):
            nc.gpsimd.memset(c["ident"][:, :], 0.0).then_inc(ident_step, 1)
            pool.wait_ge(ident_step, 1)
            nc.gpsimd.affine_select(out=c["ident"][:, :], in_=c["ident"][:, :], compare_op=ALU.not_equal,
                                    fill=1.0, base=0, pattern=[[-1, P]], channel_multiplier=1).then_inc(ident_step, 1)

        @block.scalar
        def _(act):
            act.wait_ge(loaded, 32)
            nc.scalar.activation(junk[:, :], x[:, :], ACT.Square, accum_out=stat[:, 0:1]).then_inc(squared, 1)
            act.wait_ge(squared, 1)
            act.wait_ge(eps_set, 1)
            nc.scalar.activation(stat[:, 1:2], stat[:, 0:1], ACT.Sqrt, scale=1.0 / D, bias=c["eps"][0:SR, 0:1]).then_inc(rooted, 1)
            act.wait_ge(multiplied, 2)
            nc.scalar.copy(iw[:, :], pw[:, :]).then_inc(out_ready, 1)

        @block.vector
        def _(dve):
            nc.vector.memset(c["eps"][:, :], EPS).then_inc(eps_set, 1)
            dve.wait_ge(rooted, 1)
            nc.vector.reciprocal(stat[:, 2:3], stat[:, 1:2]).then_inc(rstd_ready, 1)
            dve.wait_ge(rstd_ready, 1)
            nc.vector.tensor_scalar(xs[:, :], x[:, :], stat[:, 2:3], None, ALU.mult).then_inc(scaled, 1)
            dve.wait_ge(turned, 1)
            dve.wait_ge(loaded, 32)
            nc.vector.tensor_tensor(xT[:, :, :], px[:, :, :], gcol[:, :].unsqueeze(2).to_broadcast([P, KT, SR]), ALU.mult
                                    ).then_inc(xT_ready, 1)
            dve.wait_ge(multiplied, 1)
            nc.vector.tensor_copy(out[:, 0:4, :], pq[:, 0:4, :]).then_inc(out_ready, 1)
            nc.vector.tensor_copy(out[0:ID, 4, :], pq[0:ID, 4, :]).then_inc(out_ready, 1)

        @block.tensor
        def _(pe):
            pe.wait_ge(ident_step, 2)
            pe.wait_ge(scaled, 1)
            for k in range(KT):
                ins = nc.tensor.transpose(px[:, k, :], xs[:, k * P:(k + 1) * P], c["ident"][0:SR, 0:SR])
            ins.then_inc(turned, 1)
            pe.wait_ge(xT_ready, 1)
            pe.wait_ge(w_loaded, 32)
            for t, cols in enumerate((P, P, P, P, ID)):
                for k in range(KT):
                    ins = nc.tensor.matmul(pq[0:cols, t, :], w[:, k, t * P:t * P + cols], xT[:, k, :],
                                           start=k == 0, stop=k == KT - 1)
            ins.then_inc(multiplied, 1)
            for k in range(KT):
                ins = nc.tensor.matmul(pw[:, :], xT[:, k, :], w[:, k, NC - IH:NC], start=k == 0, stop=k == KT - 1)
            ins.then_inc(multiplied, 1)


GATHERS = DB // 2
SB_COLS = PAST + DT
SEG = SB_COLS // 4


def sample_index_phase(nc, c, d):
    with ExitStack() as ctx:
        sb = lambda name, shape, dt=F32: ctx.enter_context(nc.sbuf_tensor("si_" + name, shape, dt))
        sem = phase_semaphores(nc, ctx, "sample_index")
        ps = lambda name, shape: ctx.enter_context(nc.psum_tensor("si_" + name, shape, F32))
        pages = [sb(f"pages{p}", [P, PAGE * ID]) for p in range(2)]
        ptab = sb("ptab", [P, GATHERS], I32)
        iq = sb("iq", [P, IH, SR])
        iqd = sb("iqd", [P, DB, 2, IH, DT])
        iwc = sb("iwc", [P, GATHERS])
        msel = sb("msel", [P, 2, 36])
        w2 = sb("w2", [P, GATHERS, 2, 36])
        ik = sb("ik", [ID, SR])
        keys = [sb(f"keys{p}", [P, 8, P]) for p in range(2)]
        relu = [sb(f"relu{p}", [P, 512]) for p in range(2)]
        rnew = [sb(f"rnew{p}", [P, DT]) for p in range(2)]
        score = [sb(f"score{p}", [36, SB_COLS]) for p in range(2)]
        later = sb("later", [36, DT])
        pt = ps("pt", [P, 2, 512])
        p1 = ps("p1", [P, 2, 512])
        p2 = ps("p2", [P, 2, 512])
        pn = ps("pn", [P, 512])
        pn2 = ps("pn2", [P, 512])
        loaded, paged, stored = sem("loaded"), [sem(f"paged{p}") for p in range(2)], [sem(f"score_stored{p}") for p in range(2)]
        setup = Steps(sem("setup"), "msel0", "sel0", "sel1", "sel2", "sel3", "iqd0", "iqd1", "w2")
        iwr, zeroed = sem("iw_reordered"), sem("zeroed")
        pages_t, keys_out = sem("pages_t"), [sem("keys_out_scalar"), sem("keys_out_vector")]
        heads_mm, relu_ready = sem("heads_mm"), [sem("relu_ready_scalar"), sem("relu_ready_vector")]
        sum_mm, score_out = sem("sum_mm"), [sem("score_out_even"), sem("score_out_odd")]
        new_mm, new_relu, new_sum, new_out = sem("new_mm"), sem("new_relu"), sem("new_sum"), sem("new_out")
        NG = PAGE // 2 // 8
        def copy_keys(eng, copy, half, n):
            eng.wait_ge(pages_t, n + 1)
            if n >= 2:
                eng.wait_ge(heads_mm, 2 * (n - 1))
            copy(keys[n % 2][:, 4 * half:4 * half + 4, :],
                 pt[:, half, :].rearrange("p (k s) -> p k s", k=4)).then_inc(keys_out[half], 1)

        def copy_scores(eng, copy, e, n):
            q, g = n // NG, n % NG
            eng.wait_ge(sum_mm, 2 * n + 1 + e)
            if g == 0 and q >= 2:
                eng.wait_ge(stored[q % 2], 16 * 8 * (q // 2))
            dst = score[q % 2][:, 0:PAST].rearrange("r (p k) -> r k p", k=PAGE)[:, 16 * g + e:16 * g + 16:2, :]
            copy(dst, p2[0:36, e, :].rearrange("r (k p) -> r k p", k=8)).then_inc(score_out[e], 1)

        block = ctx.enter_context(nc.Block())

        @block.sync
        def _(sp):
            for q in range(GATHERS):
                sp.dma_start(ptab[:, q:q + 1], d["page_table"][2 * q:2 * q + 2, :].rearrange("b (p a) -> (b p) a", a=1)
                             ).then_inc(loaded, 16)
            qsrc = d["iq_scr"].rearrange("t (e d) s -> d (t e) s", e=2)
            for e in range(2):
                sp.dma_start(iq[64 * e:64 * e + 64, :, :], qsrc).then_inc(loaded, 16)
            sp.dma_start(ik[:, :], d["ik_scr"]).then_inc(loaded, 16)
            for b in range(2):
                for h in range(IH):
                    sp.dma_start(d["iwc_scr"][b, h], d["iw_scr"].rearrange("(q b t) h -> b h t q", b=2, t=DT)[b, h]).then_inc(iwr, 16)
            sp.wait_ge(iwr, 16 * 2 * IH)
            for b in range(2):
                for e in range(2):
                    sp.dma_start(iwc[64 * b + 32 * e:64 * b + 32 * e + 32, :],
                                 d["iwc_scr"][b].rearrange("h t q -> (h t) q")).then_inc(loaded, 16)
            for q in range(GATHERS):
                for e in range(2):
                    sp.wait_ge(score_out[e], NG * (q + 1))
                sp.wait_ge(new_out, q + 1)
                for b in range(2):
                    row = (2 * q + b) * DT
                    for s in range(4):
                        sp.dma_start(d["ss_scr"][s, row:row + DT, :],
                                     score[q % 2][32 * b:32 * b + DT, s * SEG:(s + 1) * SEG]).then_inc(stored[q % 2], 16)
            for p in range(2):
                sp.wait_ge(stored[p], 16 * 8 * GATHERS // 2)

        @block.gpsimd
        def _(pool):
            nc.gpsimd.memset(iqd[:, :, :, :, :], 0.0).then_inc(zeroed, 1)
            nc.gpsimd.memset(msel[:, :, :], 0.0).then_inc(zeroed, 1)
            for p in range(2):
                nc.gpsimd.memset(rnew[p][:, :], 0.0).then_inc(zeroed, 1)
            nc.gpsimd.memset(later[:, :], 0.0).then_inc(zeroed, 1)
            pool.wait_ge(zeroed, 5)
            for b in range(2):
                nc.gpsimd.affine_select(out=later[32 * b:32 * b + DT, :], in_=later[32 * b:32 * b + DT, :],
                                        compare_op=ALU.is_ge, fill=HIDDEN, base=0, pattern=[[-1, DT]],
                                        channel_multiplier=1).then_inc(zeroed, 1)
            pool.wait_ge(zeroed, 7)
            pool.wait_ge(loaded, 16 * (GATHERS + 7))
            for q in range(GATHERS):
                if q >= 2:
                    pool.wait_ge(pages_t, NG * (q - 1))
                pool.indirect_dma_start(out=pages[q % 2][:, :], out_offset=None,
                                        in_=d["cache_idx_k"].rearrange("a n s e -> (a n) (s e)"),
                                        in_offset=bass.IndirectOffsetOnAxis(ap=ptab[:, q:q + 1].bitcast(U32), axis=0)
                                        ).then_inc(paged[q % 2], 16)

        @block.tensor
        def _(pe):
            pe.wait_ge(setup.sem, setup["w2"])
            for q in range(GATHERS):
                pe.wait_ge(paged[q % 2], 16 * (q // 2 + 1))
                for b in range(2):
                    n = 2 * q + b
                    if n:
                        pe.wait_ge(new_relu, n)
                    nc.tensor.matmul(pn[0:32, 0:DT], iqd[0:64, n, 0, :, :].rearrange("p h t -> p (h t)"),
                                     ik[:, n * DT:(n + 1) * DT], start=True, stop=True).then_inc(new_mm, 1)
                pe.wait_ge(new_relu, 2 * q + 2)
                if q:
                    pe.wait_ge(new_out, q)
                nc.tensor.matmul(pn2[0:36, 0:DT], w2[:, q, 0, :], rnew[q % 2][:, :], start=True, stop=True).then_inc(new_sum, 1)

                def turn(g):
                    n = NG * q + g
                    for half in range(2):
                        if n:
                            pe.wait_ge(keys_out[half], n)
                        for k in range(4):
                            kp = 8 * g + 4 * half + k
                            ins = nc.tensor.transpose(pt[:, half, k * P:(k + 1) * P], pages[q % 2][:, kp * P:(kp + 1) * P],
                                                      c["ident"][:, :])
                    ins.then_inc(pages_t, 1)

                def total(g):
                    n = NG * q + g
                    for e in range(2):
                        pe.wait_ge(relu_ready[e], n + 1)
                    for e in range(2):
                        if n:
                            pe.wait_ge(score_out[e], n)
                        nc.tensor.matmul(p2[0:36, e, :], w2[:, q, e, :], relu[n % 2][:, :], start=True, stop=True).then_inc(sum_mm, 1)

                turn(0)
                for g in range(NG):
                    n = NG * q + g
                    for e in range(2):
                        pe.wait_ge(keys_out[e], n + 1)
                    for b in range(2):
                        if n:
                            pe.wait_ge(relu_ready[b], n)
                        nc.tensor.matmul(p1[0:64, b, :], iqd[:, 2 * q + b, :, :, :].rearrange("p e h t -> p (e h t)"),
                                         keys[n % 2][:, :, 64 * b:64 * b + 64], start=True, stop=True).then_inc(heads_mm, 1)
                    if g + 1 < NG:
                        turn(g + 1)
                    total(g)

        @block.scalar
        def _(act):
            act.wait_ge(zeroed, 7)
            for q in range(GATHERS):
                for b in range(2):
                    act.wait_ge(new_mm, 2 * q + b + 1)
                    if q >= 2:
                        act.wait_ge(new_sum, q - 1)
                    nc.scalar.activation(rnew[q % 2][64 * b:64 * b + 32, :], pn[0:32, 0:DT], ACT.Relu,
                                         scale=float(ID) ** -0.5).then_inc(new_relu, 1)
                copy_keys(act, nc.scalar.copy, 0, NG * q)
                for g in range(NG):
                    n = NG * q + g
                    act.wait_ge(heads_mm, 2 * n + 1)
                    if n >= 2:
                        act.wait_ge(sum_mm, 2 * (n - 1))
                    nc.scalar.activation(relu[n % 2][0:64, :], p1[0:64, 0, :], ACT.Relu, scale=float(ID) ** -0.5
                                         ).then_inc(relu_ready[0], 1)
                    if g + 1 < NG:
                        copy_keys(act, nc.scalar.copy, 0, n + 1)
                    copy_scores(act, nc.scalar.copy, 0, n)

        @block.vector
        def _(dve):
            dve.wait_ge(zeroed, 7)
            dve.wait_ge(loaded, 16 * (GATHERS + 7))
            nc.vector.tensor_copy(msel[0:1, 0, 0:1], msel[0:1, 0, 0:1]).then_inc(setup.sem, setup.step("msel0"))
            dve.wait_ge(setup.sem, setup["msel0"])
            for b in range(2):
                for e in range(2):
                    lo = 64 * b + 32 * e
                    nc.vector.reduce_sum(msel[lo:lo + 32, e, 32 * b:32 * b + DT],
                                         c["ident"][lo:lo + 32, lo:lo + 32].rearrange("p (h t) -> p t h", t=DT),
                                         AX_X).then_inc(setup.sem, setup.step(f"sel{2 * b + e}"))
            for e in range(2):
                nc.vector.tensor_copy(iqd[64 * e:64 * e + 64, :, e, :, :],
                                      iq[64 * e:64 * e + 64, :, :].rearrange("p h (b t) -> p b h t", t=DT)
                                      ).then_inc(setup.sem, setup.step(f"iqd{e}"))
            dve.wait_ge(setup.sem, setup["sel3"])
            for q in range(GATHERS):
                ins = nc.vector.tensor_scalar(w2[:, q, :, :], msel[:, :, :], iwc[:, q:q + 1], float(IH) ** -0.5,
                                              ALU.mult, ALU.mult)
            ins.then_inc(setup.sem, setup.step("w2"))
            for q in range(GATHERS):
                dve.wait_ge(new_sum, q + 1)
                if q >= 2:
                    dve.wait_ge(stored[q % 2], 16 * 8 * (q // 2))
                nc.vector.tensor_tensor(score[q % 2][:, PAST:SB_COLS], pn2[0:36, 0:DT], later[:, :], ALU.add).then_inc(new_out, 1)
                copy_keys(dve, nc.vector.tensor_copy, 1, NG * q)
                for g in range(NG):
                    n = NG * q + g
                    dve.wait_ge(heads_mm, 2 * n + 2)
                    if n >= 2:
                        dve.wait_ge(sum_mm, 2 * (n - 1))
                    nc.vector.tensor_scalar(relu[n % 2][64:128, :], p1[0:64, 1, :], float(ID) ** -0.5, 0.0,
                                            ALU.mult, ALU.max).then_inc(relu_ready[1], 1)
                    if g + 1 < NG:
                        copy_keys(dve, nc.vector.tensor_copy, 1, n + 1)
                    copy_scores(dve, nc.vector.tensor_copy, 1, n)


ONE = 32


def sample_selection(nc, c, d, sb, sem, bank):
    score = sb("score", [P, SEG])
    val = sb("val", [P, TOPK])
    idx = sb("idx", [P, TOPK], U32)
    idf = sb("idf", [P, TOPK])
    segb = sb("segb", [P, 1])
    val4 = sb("val4", [SR, 4, TOPK])
    idf4 = sb("idf4", [SR, 4, TOPK])
    pos = sb("pos", [SR, TOPK])
    best = sb("best", [SR, 8])
    pint = sb("pint", [SR, 2, TOPK], I32)
    pfl = sb("pfl", [SR, 2, TOPK])
    ptab = sb("ptab", [SR, PAGES], I32)
    ptf = sb("ptf", [SR, PAGES])
    iota = sb("iota", [SR, PAGES])
    one = sb("one", [SR, ONE, PAGES])
    phys = sb("phys", [SR, TOPK])
    seln = sb("seln", [SR, DT])
    junk = sb("junk", [SR, TOPK])
    bm = sb("bm", [SR, DB])
    bias = sb("bias", [SR, TOPK + SR])
    expand = sb("expand", [SR, SR, 4])
    loaded, moved, chain = sem("loaded"), sem("moved"), sem("chain")
    merged_ready, turned, copied, iota_ready, select_done = sem("merged_ready"), sem("turned"), sem("copied"), sem("iota_ready"), sem("select_done")
    links = [0]

    def link(ins):
        links[0] += 1
        ins.then_inc(chain, 1)
        nc.vector.wait_ge(chain, links[0])

    def load(sp):
        sp.dma_start(score[:, :], d["ss_scr"].rearrange("s r k -> (s r) k")).then_inc(loaded, 16)
        for b in range(DB):
            sp.dma_start(ptab[DT * b:DT * b + DT, :], d["page_table"][b:b + 1, :].to_broadcast([DT, PAGES])).then_inc(loaded, 16)

    def move(sp):
        sp.wait_ge(merged_ready, 1)
        for s in range(4):
            sp.dma_start(val4[:, s, :], val[32 * s:32 * s + 32, :]).then_inc(moved, 16)
            sp.dma_start(idf4[:, s, :], idf[32 * s:32 * s + 32, :]).then_inc(moved, 16)

    def count(pool):
        nc.gpsimd.iota(pint[:, 0, 0:PAGES], pattern=[[1, PAGES]], base=0, channel_multiplier=0).then_inc(iota_ready, 1)

    def begin(dve):
        for s in range(4):
            nc.vector.memset(segb[32 * s:32 * s + 32, :], float(s * SEG + 1))
        dve.wait_ge(iota_ready, 1)
        link(nc.vector.tensor_copy(iota[:, :], pint[:, 0, 0:PAGES]))
        dve.wait_ge(loaded, 16 * (1 + DB))
        link(nc.vector.tensor_copy(ptf[:, :], ptab[:, :]))

    def take(dve, steps):
        for j in steps:
            v8 = val[:, 8 * j:8 * j + 8]
            link(nc.vector.max(v8, score[:, :]))
            nc.vector.max_index(idx[:, 8 * j:8 * j + 8], v8, score[:, :])
            link(nc.vector.match_replace(score[:, :], v8, score[:, :], TAKEN))

    def finish(dve):
        link(nc.vector.tensor_copy(idf[:, :], idx[:, :]))
        nc.vector.tensor_scalar(idf[:, :], idf[:, :], segb[:, 0:1], None, ALU.add).then_inc(merged_ready, 1)
        dve.wait_ge(moved, 16 * 8)
        flat = val4[:, :, :].rearrange("p s k -> p (s k)")
        for j in range(TOPK // 8):
            link(nc.vector.max(best[:, :], flat))
            link(nc.vector.match_replace(flat, best[:, :], flat, TAKEN))
        link(nc.vector.scalar_tensor_tensor(flat, flat, TAKEN, idf4[:, :, :].rearrange("p s k -> p (s k)"),
                                            ALU.is_equal, ALU.mult))
        for j in range(TOPK // 8):
            link(nc.vector.max(pos[:, 8 * j:8 * j + 8], flat))
            link(nc.vector.match_replace(flat, pos[:, 8 * j:8 * j + 8], flat, -1.0))
        link(nc.vector.tensor_scalar(pos[:, :], pos[:, :], -1.0, None, ALU.add))
        link(nc.vector.tensor_copy(pint[:, 1, :], pos[:, :]))
        nc.vector.tensor_scalar(pint[:, 0, :], pint[:, 1, :], 7, None, ALU.arith_shift_right)
        link(nc.vector.tensor_scalar(pint[:, 1, :], pint[:, 1, :], PAGE - 1, None, ALU.bitwise_and))
        link(nc.vector.tensor_copy(pfl[:, :, :], pint[:, :, :]))
        for q in range(TOPK // ONE):
            cols = slice(ONE * q, ONE * q + ONE)
            link(nc.vector.tensor_tensor(one[:, :, :], pfl[:, 0, cols].unsqueeze(2).to_broadcast([SR, ONE, PAGES]),
                                         iota[:, :].unsqueeze(1).to_broadcast([SR, ONE, PAGES]), ALU.is_equal))
            link(nc.vector.tensor_tensor(one[:, :, :], one[:, :, :],
                                         ptf[:, :].unsqueeze(1).to_broadcast([SR, ONE, PAGES]), ALU.mult))
            link(nc.vector.reduce_sum(phys[:, cols], one[:, :, :], AX_X))
        link(nc.vector.scalar_tensor_tensor(phys[:, :], phys[:, :], float(PAGE), pfl[:, 1, :], ALU.mult, ALU.add))
        nc.vector.tensor_scalar(bias[:, 0:TOPK], pos[:, :], float(PAST), NEG, ALU.is_ge, ALU.mult)
        for t in range(DT):
            link(nc.vector.tensor_scalar(junk[:, :], pos[:, :], float(PAST + t), None, ALU.is_equal, ALU.max,
                                         accum_out=seln[:, t:t + 1]))
        link(nc.vector.reduce_sum(bm[:, :], c["ident"][0:SR, 0:SR].rearrange("p (b t) -> p b t", t=DT), AX_X))
        bnew = bias[:, TOPK:TOPK + SR].rearrange("p (b t) -> p b t", t=DT)
        link(nc.vector.tensor_tensor(bnew, bm[:, :].unsqueeze(2).to_broadcast([SR, DB, DT]),
                                     seln[:, :].unsqueeze(1).to_broadcast([SR, DB, DT]), ALU.mult))
        link(nc.vector.tensor_scalar(bnew, bnew, -1.0, -NEG, ALU.add, ALU.mult))
        nc.vector.tensor_copy(expand[:, :, :], c["ident"][0:SR, 0:SR].unsqueeze(2).to_broadcast([SR, SR, 4])
                              ).then_inc(select_done, 1)

    def keep(dve):
        dve.wait_ge(turned, 2)
        nc.vector.tensor_copy(c["rowid"][:, :, :], bank[:, 0:2 * SR].rearrange("p (a r) -> p a r", a=2)).then_inc(copied, 1)
        nc.vector.tensor_copy(c["sbias"][:, :], bank[:, 2 * SR:3 * SR + TOPK]).then_inc(copied, 1)

    def turn(pe):
        pe.wait_ge(select_done, 1)
        for a in range(2):
            ins = nc.tensor.transpose(bank[:, a * SR:(a + 1) * SR], phys[:, a * P:(a + 1) * P], c["ident"][0:SR, 0:SR])
        ins.then_inc(turned, 1)
        nc.tensor.matmul(bank[:, 2 * SR:3 * SR + TOPK], expand[:, :, :].rearrange("p r g -> p (r g)"), bias[:, :],
                         start=True, stop=True).then_inc(turned, 1)
    return load, move, count, begin, take, finish, keep, turn


def sample_attention_phase(nc, c, d):
    with ExitStack() as ctx:
        sb = lambda name, shape, dt=F32: ctx.enter_context(nc.sbuf_tensor("sa_" + name, shape, dt))
        sem = phase_semaphores(nc, ctx, "sample_attention")
        ps = lambda name, shape: ctx.enter_context(nc.psum_tensor("sa_" + name, shape, F32))
        KS = 6
        WIN = 2 * P - 4
        kg = [sb(f"kg{s}", [P, 2, KV * HD]) for s in range(KS)]
        vg = sb("vg", [P, SR, 2, KV * HD])
        q = sb("q", [P, BH, SR])
        qw = [sb(f"qw{p}", [P, KV, WIN]) for p in range(2)]
        qa = sb("qa", [P, KV, SR, 4])
        kTn = sb("kTn", [P, KV, SR])
        vn = sb("vn", [SR, KV * HD])
        kT = [sb(f"kT{p}", [P, KV, 2, P]) for p in range(2)]
        x = sb("x", [P, KV, TOPK + SR])
        xT = sb("xT", [P, KV, 3, P])
        stat = sb("stat", [P, 3, KV])
        oT = sb("oT", [P, KV, SR, 4])
        bz = sb("bz", [SR, D])
        sz = sb("sz", [SR, D])
        yb = sb("yb", [SR, D])
        pk = [ps(f"pk{p}", [P, 512]) for p in range(2)]
        psc = ps("psc", [P, KV, 512])
        pn = ps("pn", [P, 512])
        po = ps("po", [P, 512])
        py = ps("py", [P, 2, 512])
        loaded = sem("loaded")
        k_in = [sem(f"k_in{s}") for s in range(KS)]
        v_in, zero = sem("v_in"), sem("zero")
        window, turned, k_out, score_mm = sem("window"), sem("turned"), sem("k_out"), sem("score_mm")
        v = Steps(sem("vector_steps"), "x", "new", "max", "nmax", "rsum", "norm0", "norm1", "xT0", "yb")
        a = Steps(sem("scalar_steps"), "exp0", "exp1", "xT1", "xTn", "oT", "sig")
        t = Steps(sem("tensor_steps"), "new", "xT", "o", "y")
        sz_ready, y_stored = sem("sz_ready"), sem("y_stored")
        SCALE = float(HD) ** -0.5
        block = ctx.enter_context(nc.Block())

        @block.sync
        def _(sp):
            sp.dma_start(q[:, :, :], d["qt"][T_BQ:T_BK, :, SEQ:ROWS].rearrange("t p s -> p t s")).then_inc(loaded, 16)
            sp.dma_start(kTn[:, :, :], d["qt"][T_BK:T_IQ, :, SEQ:ROWS].rearrange("t p s -> p t s")).then_inc(loaded, 16)
            sp.dma_start(vn[:, :], d["r"][SEQ:ROWS, R_BKV + 256:R_BKV + 512]).then_inc(loaded, 16)
            sp.dma_start(bz[:, :], d["r"][SEQ:ROWS, R_BZ:R_BZ + D]).then_inc(loaded, 16)
            sp.wait_ge(v.sem, v["yb"])
            sp.dma_start(d["y"][SEQ:ROWS, D:2 * D], yb[:, :]).then_inc(y_stored, 16)
            sp.wait_ge(y_stored, 16)

        @block.gpsimd
        def _(pool):
            for p in range(2):
                nc.gpsimd.memset(qw[p][:, :, :], 0.0).then_inc(zero, 1)

            def gather(dst, cache, r, half):
                return pool.indirect_dma_start(out=dst, out_offset=None,
                                               in_=d[cache].rearrange("a n s k e -> (a n s) (k e)"),
                                               in_offset=bass.IndirectOffsetOnAxis(ap=c["rowid"][:, half, r:r + 1], axis=0))
            for r in range(SR):
                if r >= KS:
                    pool.wait_ge(turned, r - KS + 1)
                for half in range(2):
                    gather(kg[r % KS][:, half, :], "cache_k", r, half).then_inc(k_in[r % KS], 16)
                for half in range(2):
                    gather(vg[:, r, half, :], "cache_v", r, half).then_inc(v_in, 16)
            pool.wait_ge(a.sem, a["sig"])
            nc.gpsimd.tensor_tensor(sz[:, :], sz[:, :], bz[:, :], ALU.mult).then_inc(sz_ready, 1)

        @block.tensor
        def _(pe):
            def turn(r):
                pe.wait_ge(k_in[r % KS], 32 * (r // KS + 1))
                if r >= 2:
                    pe.wait_ge(k_out, r - 1)
                for kv in range(KV):
                    for half in range(2):
                        ins = nc.tensor.transpose(pk[r % 2][:, (2 * kv + half) * P:(2 * kv + half + 1) * P],
                                                  kg[r % KS][:, half, kv * HD:(kv + 1) * HD], c["ident"][:, :])
                ins.then_inc(turned, 1)

            turn(0)
            for r in range(SR):
                if r + 1 < SR:
                    turn(r + 1)
                pe.wait_ge(k_out, r + 1)
                pe.wait_ge(window, r + 1)
                lo = P - 4 - 4 * r
                for kv in range(KV):
                    ins = nc.tensor.matmul(psc[:, kv, 0:TOPK], qw[r % 2][:, kv, lo:lo + P],
                                           kT[r % 2][:, kv, :, :].rearrange("p a k -> p (a k)"),
                                           start=r == 0, stop=r == SR - 1)
                ins.then_inc(score_mm, 1)
            for kv in range(KV):
                ins = nc.tensor.matmul(pn[:, kv * SR:(kv + 1) * SR], qa[:, kv, :, :].rearrange("p r g -> p (r g)"),
                                       kTn[:, kv, :], start=True, stop=True)
            ins.then_inc(t.sem, t.step("new"))
            pe.wait_ge(v.sem, v["norm1"])
            for kv in range(KV):
                for half in range(2):
                    nc.tensor.transpose(pk[0][:, (2 * kv + half) * P:(2 * kv + half + 1) * P],
                                        x[:, kv, half * P:(half + 1) * P], c["ident"][:, :])
                ins = nc.tensor.transpose(pk[1][0:SR, kv * P:(kv + 1) * P], x[:, kv, TOPK:TOPK + SR], c["ident"][:, :])
            ins.then_inc(t.sem, t.step("xT"))
            pe.wait_ge(a.sem, a["xTn"])
            pe.wait_ge(v_in, 32 * SR)
            for kv in range(KV):
                for r in range(SR):
                    o = po[:, kv * P + 4 * r:kv * P + 4 * r + 4]
                    for half in range(2):
                        nc.tensor.matmul(o, vg[:, r, half, kv * HD:(kv + 1) * HD], xT[:, kv, half, 4 * r:4 * r + 4],
                                         start=half == 0, stop=False)
                    ins = nc.tensor.matmul(o, vn[:, kv * HD:(kv + 1) * HD], xT[0:SR, kv, 2, 4 * r:4 * r + 4],
                                           start=False, stop=True)
            ins.then_inc(t.sem, t.step("o"))
            pe.wait_ge(a.sem, a["oT"])
            for kv in range(KV):
                for g in range(4):
                    ins = nc.tensor.transpose(py[0:SR, kv, g * P:(g + 1) * P], oT[:, kv, :, g], c["ident"][:, :])
            ins.then_inc(t.sem, t.step("y"))

        @block.vector
        def _(dve):
            dve.wait_ge(zero, 2)
            dve.wait_ge(loaded, 16 * 4)
            nc.vector.tensor_copy(qa[:, :, :, :], q[:, :, :].rearrange("p (k g) r -> p k r g", k=KV))
            for r in range(SR):
                if r >= 2:
                    dve.wait_ge(score_mm, r - 1)
                nc.vector.tensor_copy(qw[r % 2][:, :, P - 4:P],
                                      q[:, :, r].rearrange("p (k g) -> p k g", k=KV)).then_inc(window, 1)
            dve.wait_ge(score_mm, SR)
            nc.vector.tensor_tensor(x[:, :, 0:TOPK], psc[:, :, 0:TOPK],
                                    c["sbias"][:, 0:TOPK].unsqueeze(1).to_broadcast([P, KV, TOPK]), ALU.add
                                    ).then_inc(v.sem, v.step("x"))
            dve.wait_ge(t.sem, t["new"])
            nc.vector.tensor_tensor(x[:, :, TOPK:TOPK + SR], pn[:, 0:KV * SR].rearrange("p (k s) -> p k s", k=KV),
                                    c["sbias"][:, TOPK:TOPK + SR].unsqueeze(1).to_broadcast([P, KV, SR]), ALU.add
                                    ).then_inc(v.sem, v.step("new"))
            dve.wait_ge(v.sem, v["new"])
            nc.vector.reduce_max(stat[:, 0, :], x[:, :, :], AX_X).then_inc(v.sem, v.step("max"))
            dve.wait_ge(v.sem, v["max"])
            nc.vector.tensor_scalar(stat[:, 0, :], stat[:, 0, :], -SCALE, None, ALU.mult).then_inc(v.sem, v.step("nmax"))
            dve.wait_ge(a.sem, a["exp1"])
            nc.vector.reciprocal(stat[:, 2, :], stat[:, 1, :]).then_inc(v.sem, v.step("rsum"))
            dve.wait_ge(v.sem, v["rsum"])
            for kv in range(KV):
                nc.vector.tensor_scalar(x[:, kv, :], x[:, kv, :], stat[:, 2, kv:kv + 1], None, ALU.mult
                                        ).then_inc(v.sem, v.step(f"norm{kv}"))
            dve.wait_ge(t.sem, t["xT"])
            nc.vector.tensor_copy(xT[:, :, 0:2, :], pk[0][:, :].rearrange("p (k h s) -> p k h s", k=KV, h=2)
                                  ).then_inc(v.sem, v.step("xT0"))
            dve.wait_ge(t.sem, t["y"])
            dve.wait_ge(sz_ready, 1)
            nc.vector.tensor_tensor(yb[:, :], py[0:SR, :, :].rearrange("p a b -> p (a b)"), sz[:, :], ALU.mult
                                    ).then_inc(v.sem, v.step("yb"))

        @block.scalar
        def _(act):
            for r in range(SR):
                act.wait_ge(turned, r + 1)
                if r >= 2:
                    act.wait_ge(score_mm, r - 1)
                nc.scalar.copy(kT[r % 2][:, :, :, :], pk[r % 2][:, :].rearrange("p (k h s) -> p k h s", k=KV, h=2)
                               ).then_inc(k_out, 1)
            act.wait_ge(v.sem, v["nmax"])
            for kv in range(KV):
                nc.scalar.activation(x[:, kv, :], x[:, kv, :], ACT.Exp, scale=SCALE, bias=stat[:, 0, kv:kv + 1],
                                     accum_out=stat[:, 1, kv:kv + 1]).then_inc(a.sem, a.step(f"exp{kv}"))
            act.wait_ge(t.sem, t["xT"])
            nc.scalar.copy(xT[0:SR, :, 2, :], pk[1][0:SR, 0:2 * P].rearrange("p (k s) -> p k s", k=KV)
                           ).then_inc(a.sem, a.step("xT1"))
            act.wait_ge(v.sem, v["xT0"])
            act.wait_ge(a.sem, a["xT1"])
            nc.scalar.copy(stat[:, 0, :], stat[:, 2, :]).then_inc(a.sem, a.step("xTn"))
            act.wait_ge(t.sem, t["o"])
            nc.scalar.copy(oT[:, :, :, :], po[:, 0:2 * P].rearrange("p (k r g) -> p k r g", k=KV, g=4)
                           ).then_inc(a.sem, a.step("oT"))
            act.wait_ge(loaded, 64)
            nc.scalar.activation(sz[:, :], bz[:, :], ACT.Sigmoid).then_inc(a.sem, a.step("sig"))


def sample_memory_phase(nc, c, d):
    with ExitStack() as ctx:
        sb = lambda name, shape, dt=F32: ctx.enter_context(nc.sbuf_tensor("sm_" + name, shape, dt))
        sem = phase_semaphores(nc, ctx, "sample_memory")
        ps = lambda name, shape: ctx.enter_context(nc.psum_tensor("sm_" + name, shape, F32))
        C = sb("C", [P, DB, AH, 2, P])
        qk = sb("qk", [P, 2, AH, SR])
        vr = sb("vr", [SR, AH, DV])
        oz = sb("oz", [SR, 2, D])
        sg = sb("sg", [SR, 2, D])
        na = sb("na", [SR, D])
        m0 = sb("m0", [AH, DB])
        m0r = sb("m0r", [SR, AH])
        nr = sb("nr", [SR, AH, P])
        n8 = sb("n8", [DB, AH, P])
        mt, bt, gt = (sb(n, [AH, SR]) for n in ("mt", "bt", "gt"))
        row = sb("row", [SR, 4, AH])
        am = sb("am", [SR, AH])
        ws, wi, em, wpr = (sb(n, [SR, AH]) for n in ("ws", "wi", "em", "wpr"))
        fut = sb("fut", [SR, DB, DT])
        last = sb("last", [SR, DB, DT])
        bm = sb("bm", [SR, DB])
        ones = sb("ones", [SR, P])
        one4 = sb("one4", [AH, DT])
        wpx = sb("wpx", [SR, DB, AH])
        wpb = sb("wpb", [P, DB, AH])
        wp8 = sb("wp8", [DB, AH])
        dm = sb("dm", [SR, AH, SR])
        sd = sb("sd", [SR, AH, SR])
        kq = sb("kq", [SR, 2, AH, P])
        kwz = sb("kwz", [SR, DB, AH, P])
        qz = sb("qz", [P, AH, DB, SR])
        cT = [sb(f"cT{p}", [P, 2, P]) for p in range(2)]
        inter = sb("inter", [SR, AH, DV])
        h = sb("h", [SR, AH, DV])
        ya = sb("ya", [SR, AH, DV])
        den = sb("den", [SR, 5, AH])
        prod = sb("prod", [SR, AH, P])
        pa = ps("pa", [P, 512])
        pc = [ps(f"pc{p}", [P, 512]) for p in range(2)]
        pi = ps("pi", [P, 2, 512])
        pn = ps("pn", [P, 2, 512])
        pr = ps("pr", [P, 512])
        loaded, c_loaded, stored = sem("loaded"), sem("c_loaded"), sem("stored")
        g = Steps(sem("pool_steps"), "qz0", "fut0", "fut1", "fut2", "ones", "so", "zn", "gz")
        v = Steps(sem("vector_steps"), "last", "bm", "m", "b", "g", "row", "gl", "wi0", "em0", "ws0", "wpr0",
                  "wpx", "wpb", "kwz", "qz", "sd", "qn", "qnr", "hh", "den0", "den1", "den2", "den3", "den4", "rden",
                  "decay", "n0", "n1", "rms", "rr", "ya")
        a = Steps(sem("scalar_steps"), "wi", "em", "ws", "wpr", "dm", "kw", "q", "inter", "sq", "rt", "sig")
        t = Steps(sem("tensor_steps"), "rows", "last", "dm", "kq", "wpb", "intra", "inter", "n8")
        c_turned, c_out, c_used = sem("memory_turned"), sem("memory_out"), sem("memory_used")
        upd_mm, upd_done = sem("update_mm"), sem("update_done")
        block = ctx.enter_context(nc.Block())

        @block.sync
        def _(sp):
            sp.dma_start(qk[:, :, :, :], d["qt"][0:8, :, SEQ:ROWS].rearrange("(a t) p s -> p a t s", a=2)).then_inc(loaded, 16)
            sp.dma_start(vr[:, :, :].rearrange("p h e -> p (h e)"), d["r"][SEQ:ROWS, 0:D]).then_inc(loaded, 16)
            sp.dma_start(oz[:, :, :].rearrange("p a e -> p (a e)"), d["r"][SEQ:ROWS, R_AO:R_AO + 2 * D]).then_inc(loaded, 16)
            sp.dma_start(na[:, :], d["norm_a"][0:1, :].to_broadcast([SR, D])).then_inc(loaded, 16)
            sp.dma_start(m0[:, :], d["state_m"][0].rearrange("b h -> h b")).then_inc(loaded, 16)
            sp.dma_start(n8[:, :, :].rearrange("p h e -> p (h e)"), d["state_n"][0].rearrange("b h e -> b (h e)")).then_inc(loaded, 16)
            for b in range(DB):
                rows = slice(DT * b, DT * b + DT)
                sp.dma_start(m0r[rows, :], d["state_m"][0, b:b + 1, :].to_broadcast([DT, AH])).then_inc(loaded, 16)
                sp.dma_start(nr[rows, :, :].rearrange("p h e -> p (h e)"),
                             d["state_n"][0, b:b + 1].rearrange("b h e -> b (h e)").to_broadcast([DT, AH * P])).then_inc(loaded, 16)
            for b in range(DB):
                sp.dma_start(C[:, b, :, :, :], d["state_C"][0, b].rearrange("h (x p) e -> p h x e", p=P)).then_inc(c_loaded, 16)
            sp.wait_ge(v.sem, v["b"])
            sp.dma_start(d["o_m_sample"][0].rearrange("b h -> h b"), mt[:, DT - 1:SR:DT]).then_inc(stored, 16)
            sp.wait_ge(v.sem, v["n1"])
            sp.dma_start(d["o_n_sample"][0].rearrange("b h e -> b (h e)"), n8[:, :, :].rearrange("p h e -> p (h e)")).then_inc(stored, 16)
            sp.wait_ge(v.sem, v["ya"])
            sp.dma_start(d["y"][SEQ:ROWS, 0:D], ya[:, :, :].rearrange("p h e -> p (h e)")).then_inc(stored, 16)
            sp.wait_ge(upd_done, 16)
            for b in range(DB):
                sp.dma_start(d["o_C_sample"][0, b].rearrange("h (x p) e -> p h x e", p=P), C[:, b, :, :, :]).then_inc(stored, 16)
            sp.wait_ge(stored, 16 * (3 + DB))

        N_LOADED = 16 * (6 + 2 * DB)

        @block.gpsimd
        def _(pool):
            nc.gpsimd.memset(qz[:, :, :, :], 0.0).then_inc(g.sem, g.step("qz0"))
            nc.gpsimd.memset(fut[:, :, :], 0.0).then_inc(g.sem, g.step("fut0"))
            pool.wait_ge(g.sem, g["fut0"])
            nc.gpsimd.affine_select(out=fut[:, :, :], in_=fut[:, :, :], compare_op=ALU.is_ge, fill=NEG, base=0,
                                    pattern=[[-DT, DB], [0, DT]], channel_multiplier=1).then_inc(g.sem, g.step("fut1"))
            pool.wait_ge(g.sem, g["fut1"])
            nc.gpsimd.affine_select(out=fut[:, :, :], in_=fut[:, :, :], compare_op=ALU.is_ge, fill=NEG, base=0,
                                    pattern=[[DT, DB], [1, DT]], channel_multiplier=-1).then_inc(g.sem, g.step("fut2"))
            nc.gpsimd.memset(ones[:, :], 1.0).then_inc(g.sem, g.step("ones"))
            pool.wait_ge(a.sem, a["sig"])
            nc.gpsimd.tensor_tensor(sg[:, 0, :], sg[:, 0, :], sg[:, 1, :], ALU.mult).then_inc(g.sem, g.step("so"))
            nc.gpsimd.tensor_tensor(oz[:, 1, :], oz[:, 1, :], na[:, :], ALU.mult).then_inc(g.sem, g.step("zn"))
            pool.wait_ge(g.sem, g["zn"])
            nc.gpsimd.tensor_tensor(sg[:, 1, :], sg[:, 0, :], oz[:, 1, :], ALU.mult).then_inc(g.sem, g.step("gz"))

        @block.vector
        def _(dve):
            def step(ins, name):
                ins.then_inc(v.sem, v.step(name))
                dve.wait_ge(v.sem, v[name])
            nc.vector.memset(one4[:, :], 1.0)
            id32 = c["ident"][0:SR, 0:SR].rearrange("p (b t) -> p b t", t=DT)
            step(nc.vector.tensor_copy(last[:, :, :], id32[:, :, DT - 1:DT].to_broadcast([SR, DB, DT])), "last")
            step(nc.vector.reduce_sum(bm[:, :], id32, AX_X), "bm")
            dve.wait_ge(loaded, N_LOADED)
            for b in range(DB):
                cols = slice(DT * b, DT * b + DT)
                ins = nc.vector.tensor_tensor_scan(mt[:, cols], c["lfs"][:, cols], c["gis"][:, cols], m0[:, b:b + 1],
                                                   ALU.add, ALU.max)
            step(ins, "m")
            for b in range(DB):
                cols = slice(DT * b, DT * b + DT)
                ins = nc.vector.tensor_tensor_scan(bt[:, cols], one4[:, :], c["lfs"][:, cols], 0.0, ALU.mult, ALU.add)
            step(ins, "b")
            step(nc.vector.tensor_tensor(gt[:, :], bt[:, :], mt[:, :], ALU.subtract), "g")
            dve.wait_ge(t.sem, t["rows"])
            step(nc.vector.tensor_copy(row[:, :, :], pa[0:SR, 0:16].rearrange("p (x h) -> p x h", x=4)), "row")
            i, b_, m, gg = (row[:, x, :] for x in range(4))
            step(nc.vector.tensor_tensor(am[:, :], i, b_, ALU.subtract), "gl")
            step(nc.vector.tensor_tensor(wi[:, :], gg, m0r[:, :], ALU.add), "wi0")
            step(nc.vector.tensor_scalar(em[:, :], m, -1.0, None, ALU.mult), "em0")
            dve.wait_ge(t.sem, t["last"])
            step(nc.vector.tensor_tensor(ws[:, :], am[:, :], pa[0:SR, 16:20], ALU.add), "ws0")
            step(nc.vector.tensor_tensor(wpr[:, :], m0r[:, :], pa[0:SR, 16:20], ALU.add), "wpr0")
            dve.wait_ge(a.sem, a["wpr"])
            step(nc.vector.tensor_tensor(wpx[:, :, :], wpr[:, :].unsqueeze(1).to_broadcast([SR, DB, AH]),
                                         last[:, :, 0:1].to_broadcast([SR, DB, AH]), ALU.mult), "wpx")
            dve.wait_ge(t.sem, t["wpb"])
            nc.vector.tensor_copy(wp8[:, :], pr[0:DB, 0:AH])
            step(nc.vector.tensor_copy(wpb[:, :, :], pr[:, 32:64].rearrange("p (b h) -> p b h", b=DB)), "wpb")
            dve.wait_ge(a.sem, a["kw"])
            for b in range(DB):
                ins = nc.vector.tensor_scalar(kwz[:, b, :, :], kq[:, 0, :, :], bm[:, b:b + 1], None, ALU.mult)
            step(ins, "kwz")
            dve.wait_ge(g.sem, g["qz0"])
            for b in range(DB):
                cols = slice(DT * b, DT * b + DT)
                ins = nc.vector.tensor_copy(qz[:, :, b, cols], qk[:, 0, :, cols])
            step(ins, "qz")
            dve.wait_ge(a.sem, a["dm"])
            step(nc.vector.tensor_tensor(sd[:, :, :], pa[0:SR, 256:384].rearrange("p (h s) -> p h s", h=AH), dm[:, :, :],
                                         ALU.mult), "sd")
            dve.wait_ge(a.sem, a["q"])
            step(nc.vector.tensor_tensor(prod[:, :, :], kq[:, 1, :, :], nr[:, :, :], ALU.mult), "qn")
            step(nc.vector.reduce_sum(den[:, 0, :], prod[:, :, :], AX_X), "qnr")
            dve.wait_ge(t.sem, t["intra"])
            dve.wait_ge(a.sem, a["inter"])
            step(nc.vector.tensor_tensor(h[:, :, :], inter[:, :, :], pn[0:SR, :, :].rearrange("p a (h e) -> p (a h) e", h=2),
                                         ALU.add), "hh")
            step(nc.vector.tensor_tensor(den[:, 0, :], den[:, 0, :], wi[:, :], ALU.mult), "den0")
            step(nc.vector.tensor_tensor(den[:, 0, :], pa[0:SR, 384:388], den[:, 0, :], ALU.add), "den1")
            step(nc.vector.scalar_tensor_tensor(den[:, 1, :], den[:, 0, :], -1.0, den[:, 0, :], ALU.mult, ALU.max), "den2")
            step(nc.vector.tensor_tensor(den[:, 1, :], den[:, 1, :], em[:, :], ALU.max), "den3")
            step(nc.vector.reciprocal(den[:, 2, :], den[:, 1, :]), "den4")
            step(nc.vector.tensor_copy(den[:, 4, :], den[:, 2, :]), "rden")
            dve.wait_ge(c_used, AH * DB)
            step(nc.vector.tensor_tensor(C[:, :, :, :, :].rearrange("p b h x e -> p (b h) (x e)"),
                                         C[:, :, :, :, :].rearrange("p b h x e -> p (b h) (x e)"),
                                         wpb[:, :, :].rearrange("p b h -> p (b h)").unsqueeze(2).to_broadcast([P, DB * AH, 2 * P]),
                                         ALU.mult), "decay")
            step(nc.vector.tensor_tensor(n8[:, :, :], n8[:, :, :], wp8[:, :].unsqueeze(2).to_broadcast([DB, AH, P]), ALU.mult), "n0")
            dve.wait_ge(t.sem, t["n8"])
            step(nc.vector.tensor_tensor(n8[:, :, :], n8[:, :, :], pr[0:DB, :].rearrange("p (h e) -> p h e", h=AH), ALU.add), "n1")
            dve.wait_ge(a.sem, a["rt"])
            step(nc.vector.reciprocal(den[:, 0, :], den[:, 1, :]), "rms")
            step(nc.vector.tensor_tensor(den[:, 0, :], den[:, 0, :], den[:, 2, :], ALU.mult), "rr")
            dve.wait_ge(g.sem, g["gz"])
            for hh in range(AH):
                ins = nc.vector.scalar_tensor_tensor(ya[:, hh, :], h[:, hh, :], den[:, 0, hh:hh + 1],
                                                     sg[:, 1, hh * DV:(hh + 1) * DV], ALU.mult, ALU.mult)
            step(ins, "ya")
            for n in range(16):
                hh, x, half = n // 4, n // 2 % 2, n % 2
                dve.wait_ge(upd_mm, n + 1)
                nc.vector.tensor_tensor(C[:, 4 * half:4 * half + 4, hh, x, :], C[:, 4 * half:4 * half + 4, hh, x, :],
                                        pc[n % 2][:, :].rearrange("p (b e) -> p b e", b=4), ALU.add).then_inc(upd_done, 1)

        @block.scalar
        def _(act):
            def step(ins, name):
                ins.then_inc(a.sem, a.step(name))
            for name, x, after in (("wi", wi, "wi0"), ("em", em, "em0"), ("ws", ws, "ws0"), ("wpr", wpr, "wpr0")):
                act.wait_ge(v.sem, v[after])
                step(nc.scalar.activation(x[:, :], x[:, :], ACT.Exp), name)
            act.wait_ge(t.sem, t["dm"])
            for hh in range(AH):
                ins = nc.scalar.activation(dm[:, hh, :], pa[0:SR, 128 + hh * SR:128 + (hh + 1) * SR], ACT.Exp, bias=am[:, hh:hh + 1])
            step(ins, "dm")
            act.wait_ge(t.sem, t["kq"])
            act.wait_ge(a.sem, a["ws"])
            for hh in range(AH):
                ins = nc.scalar.activation(kq[:, 0, hh, :], pn[0:SR, 0, hh * P:(hh + 1) * P], ACT.Copy, scale=ws[:, hh:hh + 1])
            step(ins, "kw")
            step(nc.scalar.copy(kq[:, 1, :, :], pn[0:SR, 1, :].rearrange("p (h e) -> p h e", h=AH)), "q")
            for n in range(AH * DB):
                act.wait_ge(c_turned, n + 1)
                if n >= 2:
                    act.wait_ge(c_used, n - 1)
                nc.scalar.copy(cT[n % 2][:, :, :], pc[n % 2][:, 0:2 * P].rearrange("p (x e) -> p x e", x=2)).then_inc(c_out, 1)
            act.wait_ge(t.sem, t["inter"])
            for hh in range(AH):
                ins = nc.scalar.activation(inter[:, hh, :], pi[0:SR, hh // 2, (hh % 2) * DV:(hh % 2 + 1) * DV], ACT.Copy,
                                           scale=wi[:, hh:hh + 1])
            step(ins, "inter")
            act.wait_ge(v.sem, v["rden"])
            for hh in range(AH):
                ins = nc.scalar.activation(inter[:, hh, :], h[:, hh, :], ACT.Square, scale=den[:, 2, hh:hh + 1],
                                           accum_out=den[:, 3, hh:hh + 1])
            step(ins, "sq")
            act.wait_ge(a.sem, a["sq"])
            step(nc.scalar.activation(den[:, 1, :], den[:, 3, :], ACT.Sqrt, scale=1.0 / DV, bias=c["eps"][0:SR, 0:1]), "rt")
            act.wait_ge(loaded, N_LOADED)
            step(nc.scalar.activation(sg[:, :, :], oz[:, :, :], ACT.Sigmoid), "sig")

        @block.tensor
        def _(pe):
            pe.wait_ge(v.sem, v["g"])
            for x, src in enumerate((c["gis"], bt, mt, gt)):
                ins = nc.tensor.transpose(pa[0:SR, 4 * x:4 * x + 4], src[:, :], c["ident"][0:4, 0:4])
            ins.then_inc(t.sem, t.step("rows"))
            pe.wait_ge(v.sem, v["row"])
            nc.tensor.matmul(pa[0:SR, 16:20], last[:, :, :].rearrange("p b t -> p (b t)"), row[:, 3, :],
                             start=True, stop=True).then_inc(t.sem, t.step("last"))
            pe.wait_ge(g.sem, g["ones"])
            pe.wait_ge(v.sem, v["wpr0"])
            for hh in range(AH):
                o = pa[0:SR, 128 + hh * SR:128 + (hh + 1) * SR]
                nc.tensor.matmul(o, c["sel"][:, hh, 0:SR], gt[:, :], start=True, stop=False)
                nc.tensor.matmul(o, c["ident"][0:SR, 0:SR], fut[:, :, :].rearrange("p b t -> p (b t)"), start=False, stop=True)
            for hh in range(AH):
                ins = nc.tensor.matmul(pa[0:SR, 256 + hh * SR:256 + (hh + 1) * SR], qk[:, 1, hh, :], qk[:, 0, hh, :],
                                       start=True, stop=True)
            ins.then_inc(t.sem, t.step("dm"))
            for x in range(2):
                for hh in range(AH):
                    ins = nc.tensor.transpose(pn[0:SR, x, hh * P:(hh + 1) * P], qk[:, 1 - x, hh, :], c["ident"][:, :])
            ins.then_inc(t.sem, t.step("kq"))
            pe.wait_ge(v.sem, v["wpx"])
            nc.tensor.matmul(pr[:, 32:64], ones[:, :], wpx[:, :, :].rearrange("p b h -> p (b h)"), start=True, stop=True)
            nc.tensor.matmul(pr[0:DB, 0:AH], last[:, :, 0], wpr[:, :], start=True, stop=True).then_inc(t.sem, t.step("wpb"))
            pe.wait_ge(v.sem, v["sd"])
            pe.wait_ge(a.sem, a["q"])
            for hh in range(AH):
                nc.tensor.matmul(pn[0:SR, hh // 2, (hh % 2) * DV:(hh % 2 + 1) * DV], sd[:, hh, :], vr[:, hh, :], start=True, stop=True)
                ins = nc.tensor.matmul(pa[0:SR, 384 + hh:385 + hh], sd[:, hh, :], ones[:, 0:1], start=True, stop=True)
            ins.then_inc(t.sem, t.step("intra"))
            for n in range(AH * DB):
                hh, b = n // DB, n % DB
                if hh == 0:
                    pe.wait_ge(c_loaded, 16 * DB)
                if n >= 2:
                    pe.wait_ge(c_out, n - 1)
                for x in range(2):
                    ins = nc.tensor.transpose(pc[n % 2][:, x * P:(x + 1) * P], C[:, b, hh, x, :], c["ident"][:, :])
                ins.then_inc(c_turned, 1)
                pe.wait_ge(c_out, n + 1)
                pe.wait_ge(v.sem, v["qz"])
                nc.tensor.matmul(pi[0:SR, hh // 2, (hh % 2) * DV:(hh % 2 + 1) * DV], qz[:, hh, b, :],
                                 cT[n % 2][:, :, :].rearrange("p x e -> p (x e)"),
                                 start=b == 0, stop=b == DB - 1).then_inc(c_used, 1)
            nc.tensor.matmul(pr[0:DB, 0:8], bm[:, :], ones[:, 0:8], start=True, stop=True).then_inc(t.sem, t.step("inter"))
            pe.wait_ge(v.sem, v["n0"])
            nc.tensor.matmul(pr[0:DB, :], bm[:, :], kq[:, 0, :, :].rearrange("p h e -> p (h e)"), start=True, stop=True
                             ).then_inc(t.sem, t.step("n8"))
            for n in range(16):
                hh, x, half = n // 4, n // 2 % 2, n % 2
                if n >= 2:
                    pe.wait_ge(upd_done, n - 1)
                nc.tensor.matmul(pc[n % 2][:, :], vr[:, hh, x * P:(x + 1) * P], kwz[:, 4 * half:4 * half + 4, hh, :],
                                 start=True, stop=True).then_inc(upd_mm, 1)


def output_phase(nc, c, d):
    with ExitStack() as ctx:
        sb = lambda name, shape, dt=F32: ctx.enter_context(nc.sbuf_tensor("out_" + name, shape, dt))
        sem = phase_semaphores(nc, ctx, "output")
        wa, wb, wo, wg = (sb(n, [P, KT, D]) for n in ("wa", "wb", "wo", "wg"))
        wp = sb("wp", [P, PLE // P, D])
        npost = sb("npost", [P, D])
        y = sb("y", [P, 2, KT, P])
        g = sb("g", [P, 2, D])
        x = [sb(f"x{p}", [P, D]) for p in range(2)]
        pe_in = [sb(f"pe{p}", [P, PLE]) for p in range(2)]
        yT = sb("yT", [P, 2, KT, P])
        mT = sb("mT", [P, KT, P])
        xT = sb("xT", [P, KT, P])
        peT = sb("peT", [P, 2, P])
        merged = sb("merged", [P, D])
        tmp = sb("tmp", [P, D])
        sg2 = sb("sg2", [P, D])
        st = sb("st", [P, 4])
        U = [ctx.enter_context(nc.psum_tensor(f"out_u{j}", [P, 2, 512], F32)) for j in range(4)]
        y_loaded, g_loaded = sem("y_loaded"), sem("g_loaded")
        x_loaded, x_stored = [sem(f"x_loaded{p}") for p in range(2)], [sem(f"x_stored{p}") for p in range(2)]
        w_loaded = {n: sem(f"{n}_loaded") for n in ("wa", "wb", "wo", "wg", "wp", "npost")}
        filled, out_a, out_v = sem("filled"), sem("out_a"), sem("out_v")
        ab_mm, out_mm, gate_mm, ple_mm = sem("ab_mm"), sem("out_mm"), sem("gate_mm"), sem("ple_mm")
        g_ready, sq_ready, rms_ready, sg2_ready = sem("g_ready"), sem("sq_ready"), sem("rms_ready"), sem("sg2_ready")
        merge_step, merged_ready, norm_step, x1_ready, y_ready = (
            sem(n) for n in ("merge_step", "merged_ready", "norm_step", "x1_ready", "y_ready"))
        FILLS = 5

        def before(n):
            return FILLS * n + 2

        def steps(eng, body):
            for p in range(2):
                body(0, p, P, P, False)
            with eng.Fori(1, NB // 2 - 1) as j:
                for p in range(2):
                    body(j, p, P, P, True)
            body(NB // 2 - 1, 0, P, P, True)
            body(NB // 2 - 1, 1, P, SR, True)
            body(NB // 2, 0, SR, 0, True)

        block = ctx.enter_context(nc.Block())

        @block.sync
        def _(sp):
            def load_y(n, rows):
                src = d["y"][SEQ:ROWS, :] if rows == SR else d["y"][0:SEQ, :].rearrange("(n q) m -> n q m", q=P)[n]
                sp.dma_start(y[0:rows, :, :, :].rearrange("p a k q -> p (a k q)"), src).then_inc(y_loaded, 16)

            def load_g(n, rows):
                src = d["r"][SEQ:ROWS, R_GA:R_GA + 2 * D] if rows == SR else \
                    d["r"][0:SEQ, R_GA:R_GA + 2 * D].rearrange("(n q) m -> n q m", q=P)[n]
                sp.dma_start(g[0:rows, :, :].rearrange("p a k -> p (a k)"), src).then_inc(g_loaded, 16)

            def load_x(n, p, rows):
                xs = d["x_sample"].rearrange("b t c -> (b t) c") if rows == SR else \
                    d["x_prompt"].rearrange("a (n q) c -> (a n) q c", q=P)[n]
                ps = d["p_sample"].rearrange("a b t c -> (a b t) c") if rows == SR else \
                    d["p_prompt"].rearrange("a e (n q) c -> (a e n) q c", q=P)[n]
                sp.dma_start(x[p][0:rows, :], xs).then_inc(x_loaded[p], 16)
                sp.dma_start(pe_in[p][0:rows, :], ps).then_inc(x_loaded[p], 16)

            load_y(0, P)
            for dst, name, key in ((wa, "w_a_proj", "wa"), (wb, "w_b_proj", "wb")):
                sp.dma_start(dst[:, :, :], d[name].rearrange("a (k p) n -> (a p) k n", p=P)).then_inc(w_loaded[key], 16)
            load_g(0, P)
            sp.dma_start(wo[:, :, :], d["w_out"].rearrange("a (k p) n -> (a p) k n", p=P)).then_inc(w_loaded["wo"], 16)
            load_x(0, 0, P)
            sp.dma_start(npost[:, :], d["norm_post"][0:1, :].to_broadcast([P, D])).then_inc(w_loaded["npost"], 16)
            sp.dma_start(wg[:, :, :], d["w_ple_gate"].rearrange("a (k p) n -> (a p) k n", p=P)).then_inc(w_loaded["wg"], 16)
            sp.dma_start(wp[:, :, :], d["w_ple"].rearrange("a (k p) n -> (a p) k n", p=P)).then_inc(w_loaded["wp"], 16)
            load_x(1, 1, P)

            def step(j, p, rows, nxt, warm):
                n = 2 * j + p
                if nxt:
                    sp.wait_ge(filled, before(n))
                    load_y(n + 1, nxt)
                    sp.wait_ge(merged_ready, n + 1)
                    load_g(n + 1, nxt)
                if warm or p:
                    q = 1 - p
                    if nxt:
                        sp.wait_ge(x_stored[q], 16 * (j + p))
                        load_x(n + 1, q, nxt)
            steps(sp, step)
            for p in range(2):
                sp.wait_ge(x_stored[p], 16 * (NB // 2 + 1 - p))

        @block.gpsimd
        def _(pool):
            def store(j, p, rows, nxt, warm):
                n = 2 * j + p
                pool.wait_ge(y_ready, n + 1)
                dst = d["y_sample"].rearrange("b t c -> (b t) c") if rows == SR else \
                    d["y_prompt"].rearrange("a (n q) c -> (a n) q c", q=P)[n]
                pool.dma_start(dst, x[p][0:rows, :]).then_inc(x_stored[p], 16)
            steps(pool, store)

        @block.tensor
        def _(pe):
            def free(a, v):
                pe.wait_ge(out_a, a)
                pe.wait_ge(out_v, v)

            def transposes(src, rows, n=KT):
                for k in range(n):
                    ins = nc.tensor.transpose(U[3][:, k // 4, (k % 4) * P:(k % 4) * P + rows], src(k),
                                              c["ident"][0:rows, 0:rows])
                ins.then_inc(filled, 1)

            def product(dst, lhs, w, rows, halves=(0, 1), kt=KT):
                for h in halves:
                    for k in range(kt):
                        ins = nc.tensor.matmul(dst[0:rows, h, :], lhs(k), w[:, k, h * 512:(h + 1) * 512],
                                               start=k == 0, stop=k == kt - 1)
                return ins

            def branches(n, rows):
                pe.wait_ge(w_loaded["wa"], 16)
                product(U[0], lambda k: yT[:, 0, k, 0:rows], wa, rows)
                pe.wait_ge(w_loaded["wb"], 16)
                product(U[1], lambda k: yT[:, 1, k, 0:rows], wb, rows).then_inc(ab_mm, 1)

            pe.wait_ge(y_loaded, 16)
            transposes(lambda k: y[:, 0, k, :], P)
            free(1, 1)
            transposes(lambda k: y[:, 1, k, :], P)
            free(2, 2)
            branches(0, P)

            def step(j, p, rows, nxt, warm):
                n = 2 * j + p
                cnt = before(n)
                pe.wait_ge(merged_ready, n + 1)
                free(cnt, cnt)
                transposes(lambda k: merged[0:rows, k * P:(k + 1) * P], rows)
                free(cnt + 1, cnt + 1)
                pe.wait_ge(w_loaded["wo"], 16)
                if warm or p:
                    pe.wait_ge(sg2_ready, n)
                if nxt:
                    pe.wait_ge(y_loaded, 16 * (n + 2))
                    transposes(lambda k: y[0:nxt, 0, k, :], nxt)
                product(U[2], lambda k: mT[:, k, 0:rows], wo, rows, (0,))
                if nxt:
                    free(cnt + 2, cnt + 2)
                    transposes(lambda k: y[0:nxt, 1, k, :], nxt)
                product(U[2], lambda k: mT[:, k, 0:rows], wo, rows, (1,)).then_inc(out_mm, 1)
                cnt = cnt + 3 if nxt else cnt + 1
                if nxt:
                    free(cnt, cnt)
                    branches(n + 1, nxt)
                pe.wait_ge(x1_ready, n + 1)
                transposes(lambda k: x[p][0:rows, k * P:(k + 1) * P], rows)
                free(cnt + 1, cnt + 1)
                pe.wait_ge(x_loaded[p], 32 * (j + 1))
                transposes(lambda k: pe_in[p][0:rows, k * P:(k + 1) * P], rows, 2)
                pe.wait_ge(w_loaded["wg"], 16)
                product(U[2], lambda k: xT[:, k, 0:rows], wg, rows).then_inc(gate_mm, 1)
                free(cnt + 2, cnt + 1)
                pe.wait_ge(w_loaded["wp"], 16)
                product(U[3], lambda k: peT[:, k, 0:rows], wp, rows, kt=2).then_inc(ple_mm, 1)
            steps(pe, step)

        def copy_half(eng, copy, dst, half, rows, cnt, done):
            eng.wait_ge(filled, cnt + 1)
            copy(dst[:, 4 * half:4 * half + 4, 0:rows],
                 U[3][:, half, :].rearrange("p (k q) -> p k q", k=4)[:, :, 0:rows]).then_inc(done, 1)

        @block.scalar
        def _(act):
            copy = nc.scalar.copy
            copy_half(act, copy, yT[:, 0], 0, P, 0, out_a)
            copy_half(act, copy, yT[:, 1], 0, P, 1, out_a)

            def gate(n, rows):
                act.wait_ge(g_loaded, 16 * (n + 1))
                nc.scalar.activation(g[0:rows, :, :], g[0:rows, :, :], ACT.Sigmoid).then_inc(g_ready, 1)
            gate(0, P)

            def step(j, p, rows, nxt, warm):
                n = 2 * j + p
                cnt = before(n)
                if warm or p:
                    act.wait_ge(out_mm, n)
                copy_half(act, copy, mT, 0, rows, cnt, out_a)
                cnt = cnt + 1
                if nxt:
                    act.wait_ge(ab_mm, n + 1)
                    copy_half(act, copy, yT[:, 0], 0, nxt, cnt, out_a)
                    copy_half(act, copy, yT[:, 1], 0, nxt, cnt + 1, out_a)
                    cnt = cnt + 2
                act.wait_ge(out_mm, n + 1)
                if warm or p:
                    act.wait_ge(y_ready, n)
                    act.wait_ge(norm_step, 2 * n)
                nc.scalar.activation(sg2[0:rows, :], U[2][0:rows, :, :].rearrange("p a b -> p (a b)"), ACT.Square,
                                     accum_out=st[0:rows, 0:1]).then_inc(sq_ready, 1)
                act.wait_ge(sq_ready, n + 1)
                nc.scalar.activation(st[0:rows, 1:2], st[0:rows, 0:1], ACT.Sqrt, scale=1.0 / D,
                                     bias=c["eps"][0:rows, 0:1]).then_inc(rms_ready, 1)
                if nxt:
                    gate(n + 1, nxt)
                if warm or p:
                    act.wait_ge(gate_mm, n)
                copy_half(act, copy, xT, 0, rows, cnt, out_a)
                if warm or p:
                    act.wait_ge(ple_mm, n)
                act.wait_ge(filled, cnt + 2)
                copy(peT[:, :, 0:rows], U[3][:, 0, 0:2 * P].rearrange("p (k q) -> p k q", k=2)[:, :, 0:rows]).then_inc(out_a, 1)
                act.wait_ge(gate_mm, n + 1)
                nc.scalar.activation(sg2[0:rows, :], U[2][0:rows, :, :].rearrange("p a b -> p (a b)"), ACT.Sigmoid
                                     ).then_inc(sg2_ready, 1)
            steps(act, step)

        @block.vector
        def _(dve):
            copy = nc.vector.tensor_copy
            flat = lambda u, rows: u[0:rows, :, :].rearrange("p a b -> p (a b)")
            copy_half(dve, copy, yT[:, 0], 1, P, 0, out_v)
            copy_half(dve, copy, yT[:, 1], 1, P, 1, out_v)

            def merge(n, rows, first=False):
                dve.wait_ge(ab_mm, n + 1)
                dve.wait_ge(g_ready, n + 1)
                if not first:
                    dve.wait_ge(filled, before(n - 1) + 1)
                nc.vector.tensor_tensor(merged[0:rows, :], flat(U[0], rows), g[0:rows, 0, :], ALU.mult).then_inc(merge_step, 1)
                nc.vector.tensor_tensor(tmp[0:rows, :], flat(U[1], rows), g[0:rows, 1, :], ALU.mult).then_inc(merge_step, 1)
                dve.wait_ge(merge_step, 2 * (n + 1))
                nc.vector.tensor_tensor(merged[0:rows, :], merged[0:rows, :], tmp[0:rows, :], ALU.add).then_inc(merged_ready, 1)
            merge(0, P, True)
            dve.wait_ge(w_loaded["npost"], 16)

            def step(j, p, rows, nxt, warm):
                n = 2 * j + p
                cnt = before(n)
                if warm or p:
                    dve.wait_ge(out_mm, n)
                copy_half(dve, copy, mT, 1, rows, cnt, out_v)
                cnt = cnt + 1
                if nxt:
                    dve.wait_ge(ab_mm, n + 1)
                    copy_half(dve, copy, yT[:, 0], 1, nxt, cnt, out_v)
                    copy_half(dve, copy, yT[:, 1], 1, nxt, cnt + 1, out_v)
                    cnt = cnt + 2
                dve.wait_ge(rms_ready, n + 1)
                dve.wait_ge(merged_ready, n + 1)
                nc.vector.reciprocal(st[0:rows, 2:3], st[0:rows, 1:2]).then_inc(norm_step, 1)
                dve.wait_ge(norm_step, 2 * n + 1)
                nc.vector.scalar_tensor_tensor(tmp[0:rows, :], flat(U[2], rows), st[0:rows, 2:3], npost[0:rows, :],
                                               ALU.mult, ALU.mult).then_inc(norm_step, 1)
                dve.wait_ge(x_loaded[p], 32 * (j + 1))
                dve.wait_ge(norm_step, 2 * n + 2)
                nc.vector.tensor_tensor(x[p][0:rows, :], x[p][0:rows, :], tmp[0:rows, :], ALU.add).then_inc(x1_ready, 1)
                if warm or p:
                    dve.wait_ge(gate_mm, n)
                copy_half(dve, copy, xT, 1, rows, cnt, out_v)
                if nxt:
                    merge(n + 1, nxt)
                dve.wait_ge(sg2_ready, n + 1)
                dve.wait_ge(ple_mm, n + 1)
                nc.vector.tensor_tensor(sg2[0:rows, :], flat(U[3], rows), sg2[0:rows, :], ALU.mult).then_inc(out_v, 1)
                dve.wait_ge(out_v, cnt + 2)
                dve.wait_ge(filled, cnt + 1)
                nc.vector.tensor_tensor(x[p][0:rows, :], x[p][0:rows, :], sg2[0:rows, :], ALU.add).then_inc(y_ready, 1)
            steps(dve, step)


def allocate(nc, d):
    t = lambda name, shape, dt=F32: nc.dram_tensor(name, shape, dt, kind="Internal").ap()
    d["qt"] = t("qt_scr", (T_ALL, P, ROWS))
    d["r"] = t("r_scr", (ROWS, RCOLS))
    d["y"] = t("y_scr", (ROWS, 2 * D))
    d["gates"] = t("gates_scr", (8, ROWS))
    d["mask"] = t("mask_scr", (NB, P, SEQ), BF16)
    d["iq_scr"] = t("iq_scr", (4, P, SR))
    d["ik_scr"] = t("ik_scr", (ID, SR))
    d["iwc_scr"] = t("iwc_scr", (2, IH, DT, GATHERS))
    d["ss_scr"] = t("ss_scr", (4, SR, SEG))
    d["iw_scr"] = t("iw_scr", (SR, IH))


def program(nc, d):
    allocate(nc, d)
    with ExitStack() as top:
        top.enter_context(nc.allow_non_contiguous_dma(reason="a few small vectors are loaded by column"))
        c = {}
        def sb(name, shape, dt=F32):
            c[name] = top.enter_context(nc.sbuf_tensor(name, shape, dt))
        sb("ident", [P, P])
        sb("eps", [P, 1])
        sb("rowid", [P, 2, SR], U32)
        sb("sbias", [P, TOPK + SR])
        sample_index_projection_phase(nc, c, d)
        sample_index_phase(nc, c, d)
        with ExitStack() as proj:
            def sbp(name, shape, dt=F32):
                c[name] = proj.enter_context(nc.sbuf_tensor(name, shape, dt))
            sbp("ikT", [P, ROWS])
            sbp("sm", [P, NT, 72])
            sbp("us", [P, KT, DB, 7])
            sbp("xnT", [P, KT, ROWS])
            norm_phase(nc, c, d, None)
            transposed_projection_phase(nc, c, d, None)
            row_projection_and_topk_phase(nc, c, d)
        mixing = top.enter_context(ExitStack())

        def sbm(name, shape, dt=F32):
            c[name] = mixing.enter_context(nc.sbuf_tensor(name, shape, dt))
        sbm("sel", [4, 4, P])
        sbm("future", [P, P])
        sbm("lfs", [4, SR])
        sbm("gis", [4, SR])
        sbm("g", [4, SEQ])
        for name in ("a", "ws", "wp", "wi", "em"):
            sbm(name, [P, NB, 4])
        gate_phase(nc, c, d)
        prompt_mixing_phase(nc, c, d)
        sample_attention_phase(nc, c, d)
        sample_memory_phase(nc, c, d)
        mixing.close()
        output_phase(nc, c, d)


INS = ["x_prompt", "x_sample", "cache_k", "cache_v", "cache_idx_k", "page_table", "state_C", "state_n", "state_m",
       "state_conv", "p_prompt", "p_sample", "w_in", "conv_w", "conv_b", "if_bias", "norm_a", "w_a_proj",
       "w_b_proj", "w_out", "norm_pre", "norm_post", "w_ple", "w_ple_gate"]
OUTS = [("y_prompt", (1, SEQ, D)), ("y_sample", (DB, DT, D)),
        ("o_k_prompt", (1, 1, SEQ, KV, HD)), ("o_v_prompt", (1, 1, SEQ, KV, HD)), ("o_ik_prompt", (1, 1, SEQ, ID)),
        ("o_C_prompt", (1, 1, AH, DV, DQK)), ("o_n_prompt", (1, 1, AH, DQK)), ("o_m_prompt", (1, 1, AH)),
        ("o_conv_prompt", (1, 1, 3, D)),
        ("o_k_sample", (1, DB, DT, KV, HD)), ("o_v_sample", (1, DB, DT, KV, HD)), ("o_ik_sample", (1, DB, DT, ID)),
        ("o_C_sample", (1, DB, AH, DV, DQK)), ("o_n_sample", (1, DB, AH, DQK)), ("o_m_sample", (1, DB, AH)),
        ("o_conv_sample", (1, DB, 3, D))]


def kernel(**inputs):
    import numpy as _np
    import concourse.bacc as _bacc
    from concourse import mybir as _mybir
    from concourse.bass_utils import run_bass_kernel_spmd as _run

    nc = _bacc.Bacc("TRN2", target_bir_lowering=False, num_devices=1)
    arrays, d = {}, {}
    for name in INS:
        a = _np.ascontiguousarray(inputs[name])
        arrays[f"in_{name}"] = a
        d[name] = nc.dram_tensor(f"in_{name}", a.shape, _mybir.dt.from_np(a.dtype), kind="ExternalInput").ap()
    for name, shape in OUTS:
        d[name] = nc.dram_tensor(f"out_{name}", shape, F32, kind="ExternalOutput").ap()
    program(nc, d)
    r = _run(nc, [arrays], core_ids=[0])
    return tuple(r.results[0][f"out_{name}"] for name, _ in OUTS)
```
